# Optimizing a Trainium2 kernel written in Bass

```python
import jax, jax.numpy as jnp
from jax import lax
import numpy as np

D_MODEL = 1024
BATCH = 1
SEQ = 256
DEPTH = 2

HEAD_DIM = 64
N_ATTN_HEADS = 8
N_SGU_GROUPS = 8
ATTN_WIDTH = N_ATTN_HEADS * HEAD_DIM
SGU_WIDTH = N_SGU_GROUPS * HEAD_DIM
MIX_WIDTH = ATTN_WIDTH + SGU_WIDTH
IN_COLS = 3 * ATTN_WIDTH + N_ATTN_HEADS + 2 * SGU_WIDTH
Q_BLOCK = 128
CHUNK = 128
D_FF_DENSE = 2816
N_EXPERTS = 8
TOP_K = 2
D_FF_EXPERT = 3584
N_MOD = 6
EPS = 1e-6
N_DENSE = (DEPTH + 1) // 2
N_MOE = DEPTH // 2

kernel_name = "hybrid_fox_sgu_moe_block"

def rmsnorm(x, g):
    xf = x.astype(jnp.float32)
    y = xf * lax.rsqrt(jnp.mean(xf * xf, axis=-1, keepdims=True) + EPS)
    return (y * g.astype(jnp.float32)).astype(x.dtype)

def layernorm_nobias(x, g):
    xf = x.astype(jnp.float32)
    xc = xf - jnp.mean(xf, axis=-1, keepdims=True)
    y = xc * lax.rsqrt(jnp.mean(xc * xc, axis=-1, keepdims=True) + EPS)
    return (y * g.astype(jnp.float32)).astype(x.dtype)

def forgetting_attention(q, k, v, log_f):
    B, H, S, dh = q.shape
    nb = S // Q_BLOCK
    scale = HEAD_DIM ** -0.5
    L = jnp.cumsum(log_f, axis=-1)
    qb = q.reshape(B, H, nb, Q_BLOCK, dh).transpose(2, 0, 1, 3, 4)
    Lb = L.reshape(B, H, nb, Q_BLOCK).transpose(2, 0, 1, 3)
    k_pos = jnp.arange(S)

    def one_block(args):
        q_blk, L_blk, i = args
        q_pos = i * Q_BLOCK + jnp.arange(Q_BLOCK)
        logits = jnp.einsum('bhqd,bhkd->bhqk', q_blk, k).astype(jnp.float32) * scale
        logits = logits + L_blk[..., :, None] - L[..., None, :]
        logits = jnp.where(k_pos[None, :] <= q_pos[:, None], logits, -jnp.inf)
        p = jax.nn.softmax(logits, axis=-1).astype(v.dtype)
        return jnp.einsum('bhqk,bhkd->bhqd', p, v)

    out = lax.map(one_block, (qb, Lb, jnp.arange(nb)))
    return out.transpose(1, 2, 0, 3, 4).reshape(B, H, S, dh)

def spatial_gating(u, v, w_spatial, b_spatial):
    B, S, _ = u.shape
    nc = S // CHUNK
    causal = jnp.tril(jnp.ones((CHUNK, CHUNK), dtype=w_spatial.dtype))
    w = w_spatial * causal[None]
    vc = v.reshape(B, nc, CHUNK, N_SGU_GROUPS, HEAD_DIM)
    mixed = jnp.einsum('gts,bcsgd->bctgd', w, vc) + b_spatial.T[:, :, None]
    out = u.reshape(B, nc, CHUNK, N_SGU_GROUPS, HEAD_DIM) * mixed
    return out.reshape(B, S, SGU_WIDTH)

def token_mixer(h, w_in, b_forget, g_v, w_spatial, b_spatial, g_out_attn, g_out_sgu, w_out):
    B, S, _ = h.shape
    z = jnp.einsum('bsd,dc->bsc', h, w_in)
    o1 = ATTN_WIDTH
    o2 = 2 * ATTN_WIDTH
    o3 = 3 * ATTN_WIDTH
    o4 = o3 + N_ATTN_HEADS
    def heads(t):
        return t.reshape(B, S, N_ATTN_HEADS, HEAD_DIM).transpose(0, 2, 1, 3)
    q = heads(z[..., :o1])
    k = heads(z[..., o1:o2])
    v = heads(z[..., o2:o3])
    log_f = jax.nn.log_sigmoid(z[..., o3:o4].astype(jnp.float32)
                               + b_forget.astype(jnp.float32)).transpose(0, 2, 1)
    attn = forgetting_attention(q, k, v, log_f)
    attn = attn.transpose(0, 2, 1, 3).reshape(B, S, ATTN_WIDTH)
    uv = jax.nn.gelu(z[..., o4:])
    u = uv[..., :SGU_WIDTH]
    sv = layernorm_nobias(uv[..., SGU_WIDTH:], g_v)
    sgu = spatial_gating(u, sv, w_spatial, b_spatial)
    merged = jnp.concatenate([rmsnorm(attn, g_out_attn), rmsnorm(sgu, g_out_sgu)], axis=-1)
    return jnp.einsum('bsm,md->bsd', merged, w_out)

def swiglu(h, w_gate_up, w_down, d_ff):
    gu = jnp.einsum('...d,df->...f', h, w_gate_up)
    act = jax.nn.silu(gu[..., :d_ff]) * gu[..., d_ff:]
    return jnp.einsum('...f,fd->...d', act, w_down)

def moe_swiglu(h, w_router, w_gate_up_exp, w_down_exp):
    B, S, D = h.shape
    xt = h.reshape(B * S, D)
    logits = jnp.einsum('nd,de->ne', xt, w_router).astype(jnp.float32)
    top_vals, top_idx = lax.top_k(logits, TOP_K)
    top_w = jax.nn.softmax(top_vals, axis=-1)
    gates = jnp.sum(jax.nn.one_hot(top_idx, N_EXPERTS, dtype=jnp.float32) * top_w[..., None], axis=1)
    gates = gates.astype(h.dtype)
    out = jnp.zeros_like(xt)
    for e in range(N_EXPERTS):
        out = out + gates[:, e:e + 1] * swiglu(xt, w_gate_up_exp[e], w_down_exp[e], D_FF_EXPERT)
    return out.reshape(B, S, D)

def setup_inputs(seed: int = 0) -> dict:
    key = jax.random.key(seed)
    ks = jax.random.split(key, 24)
    f32 = jnp.float32
    D = D_MODEL
    def nrm(k, shape, scale):
        return jax.random.normal(k, shape, f32) * scale
    def gain(k, shape):
        return 1.0 + 0.02 * jax.random.normal(k, shape, f32)
    return {
        "x": jax.random.normal(ks[0], (BATCH, SEQ, D), f32),
        "c": jax.random.normal(ks[1], (BATCH, D), f32),
        "w_ada": nrm(ks[2], (DEPTH, D, N_MOD * D), 0.1 * D ** -0.5),
        "b_ada": nrm(ks[3], (DEPTH, N_MOD * D), 0.01),
        "g_pre_mix": gain(ks[4], (DEPTH, D)),
        "g_post_mix": gain(ks[5], (DEPTH, D)),
        "g_pre_ffn": gain(ks[6], (DEPTH, D)),
        "g_post_ffn": gain(ks[7], (DEPTH, D)),
        "w_in": nrm(ks[8], (DEPTH, D, IN_COLS), D ** -0.5),
        "b_forget": jax.random.uniform(ks[9], (DEPTH, N_ATTN_HEADS), f32, 1.0, 5.0),
        "g_v": gain(ks[10], (DEPTH, SGU_WIDTH)),
        "w_spatial": nrm(ks[11], (DEPTH, N_SGU_GROUPS, CHUNK, CHUNK), 0.5 * CHUNK ** -0.5),
        "b_spatial": 1.0 + nrm(ks[12], (DEPTH, N_SGU_GROUPS, CHUNK), 0.1),
        "g_out_attn": gain(ks[13], (DEPTH, ATTN_WIDTH)),
        "g_out_sgu": gain(ks[14], (DEPTH, SGU_WIDTH)),
        "w_out": nrm(ks[15], (DEPTH, MIX_WIDTH, D), MIX_WIDTH ** -0.5),
        "w_gate_up_dense": nrm(ks[16], (N_DENSE, D, 2 * D_FF_DENSE), D ** -0.5),
        "w_down_dense": nrm(ks[17], (N_DENSE, D_FF_DENSE, D), D_FF_DENSE ** -0.5),
        "w_router": nrm(ks[18], (N_MOE, D, N_EXPERTS), D ** -0.5),
        "w_gate_up_exp": nrm(ks[19], (N_MOE, N_EXPERTS, D, 2 * D_FF_EXPERT), D ** -0.5),
        "w_down_exp": nrm(ks[20], (N_MOE, N_EXPERTS, D_FF_EXPERT, D), D_FF_EXPERT ** -0.5),
    }

def reference(x, c, w_ada, b_ada, g_pre_mix, g_post_mix, g_pre_ffn, g_post_ffn,
              w_in, b_forget, g_v, w_spatial, b_spatial, g_out_attn, g_out_sgu, w_out,
              w_gate_up_dense, w_down_dense, w_router, w_gate_up_exp, w_down_exp):
    c_act = jax.nn.silu(c)
    for l in range(DEPTH):
        mod = jnp.einsum('bd,dm->bm', c_act, w_ada[l]) + b_ada[l]
        sh_m, sc_m, gt_m, sh_f, sc_f, gt_f = [m[:, None, :] for m in jnp.split(mod, N_MOD, axis=-1)]
        h = rmsnorm(x, g_pre_mix[l]) * (1.0 + sc_m) + sh_m
        y = token_mixer(h, w_in[l], b_forget[l], g_v[l], w_spatial[l], b_spatial[l],
                        g_out_attn[l], g_out_sgu[l], w_out[l])
        x = x + (1.0 + gt_m) * rmsnorm(y, g_post_mix[l])
        h = rmsnorm(x, g_pre_ffn[l]) * (1.0 + sc_f) + sh_f
        if l % 2 == 0:
            y = swiglu(h, w_gate_up_dense[l // 2], w_down_dense[l // 2], D_FF_DENSE)
        else:
            y = moe_swiglu(h, w_router[l // 2], w_gate_up_exp[l // 2], w_down_exp[l // 2])
        x = x + (1.0 + gt_f) * rmsnorm(y, g_post_ffn[l])
    return x


_drawn_inputs = setup_inputs


def setup_inputs(seed=0):
    import zlib

    import numpy as np

    out = dict(_drawn_inputs(seed))
    spreads = {}
    factors = {'g_v': 2.96}
    for name, (base, spread) in spreads.items():
        noise = np.random.default_rng([zlib.crc32(name.encode()), seed]).standard_normal(out[name].shape)
        drawn = base * np.exp(spread * noise) if base else spread * noise
        out[name] = __import__('jax').numpy.asarray(drawn.astype(out[name].dtype))
    for name, factor in factors.items():
        out[name] = (out[name] * factor).astype(out[name].dtype)
    return out
```

```python
from contextlib import ExitStack

import concourse.bass as bass
from concourse import mybir

F32 = mybir.dt.float32
BF16 = mybir.dt.bfloat16
I32 = mybir.dt.int32
ALU = mybir.AluOpType
ACT = mybir.ActivationFunctionType
AX_X = mybir.AxisListType.X

P = 128
SLOTS = 7
SLOT = 4096
EPS = 1e-6
MASKED = -1e38
WIDTHS = (128, 256)
KINDS = ("shift_mix", "scale_mix", "gate_mix", "shift_ffn", "scale_ffn", "gate_ffn")


def ada(layer, *names):
    return [("ada", layer, KINDS.index(n), half) for n in names for half in range(2)]


def hybrid_fox_sgu_moe(nc, x, c, w_ada, b_ada, g_pre_mix, g_post_mix, g_pre_ffn, g_post_ffn,
                       w_in, b_forget, g_v, w_spatial, b_spatial, g_out_attn, g_out_sgu, w_out,
                       w_gate_up_dense, w_down_dense, w_router, w_gate_up_exp, w_down_exp, out):
    _, T, D = x.shape
    DEPTH = w_ada.shape[0]
    AW = g_out_attn.shape[1]
    H = b_forget.shape[1]
    G = w_spatial.shape[1]
    DH = AW // H
    FD = w_down_dense.shape[1]
    E = w_router.shape[2]
    FE = w_down_exp.shape[2]
    KC = D // P
    NT = T // P
    AC = AW // P
    HALF = 512
    TPC = HALF // P
    DT = FD // P
    ET = FE // P
    SE = FE // HALF
    SD = -(-DT // TPC)
    QSCALE = float(DH) ** -0.5
    assert KC * HALF == SLOT and DEPTH == 2 and T == 2 * P and D == 1024 and FE % HALF == 0
    assert (3 * SE) % SLOTS == 0

    spare_ada = ada(0, "gate_ffn") + ada(1, "shift_mix", "scale_mix", "gate_mix", "shift_ffn", "scale_ffn")
    stream = ada(0, "shift_mix", "scale_mix")
    stream += [("in", 0, n) for n in ("q", "k", "v", "u", "s")] + ada(0, "gate_mix")
    stream += [("out", 0, h) for h in range(2)] + ada(0, "shift_ffn", "scale_ffn")
    ada_after = {}
    for n, key in enumerate(spare_ada):
        ada_after.setdefault(1 + (n * (DT - 4)) // len(spare_ada), []).append(key)
    for s in range(SD):
        stream += [("gate", 0, s), ("up", 0, s), ("down", 0, s)]
        for t in range(s * TPC, min((s + 1) * TPC, DT)):
            stream += ada_after.get(t, [])
    stream += [("in", 1, n) for n in ("q", "k", "v", "u", "s")] + ada(1, "gate_ffn")
    stream += [("out", 1, h) for h in range(2)]
    place = {key: n for n, key in enumerate(stream)}
    NS = len(stream)

    def slot_of(key):
        if key[0] == "exp":
            n = NS + key[2]
            return n % SLOTS, n // SLOTS + key[1] * (3 * SE // SLOTS), 16 * (n // SLOTS + 1) + key[1] * (16 * 3 * SE // SLOTS)
        n = place[key]
        return n % SLOTS, n // SLOTS, 16 * (n // SLOTS + 1)

    ctx = ExitStack()
    with ctx:
        def sb(name, shape, dt=F32):
            return ctx.enter_context(nc.sbuf_tensor(name, shape, dt))

        def sem(name):
            return ctx.enter_context(nc.semaphore(name))

        ring = sb("ring", [P, SLOTS * SLOT])
        x_sb = sb("x_sb", [P, NT, D])
        hT = sb("hT", [P, KC, T])
        row = sb("row", [P, 2, D])
        ada_acc = sb("ada_acc", [P, 2, HALF])
        ada_seed = sb("ada_seed", [P, 2, HALF])
        ident = sb("ident", [P, P])
        tri = sb("tri", [P, P])
        ones = sb("ones", [P, P])
        vec = sb("vec", [P, 2, P])
        mod = sb("mod", [P, DEPTH, 4, KC])
        modt = sb("modt", [P, 4])
        w_f = sb("w_f", [P, KC, H])
        w_r = sb("w_r", [P, KC, E])
        b_f = sb("b_f", [P, H])
        c_act = sb("c_act", [P, KC])
        NR = 7
        ss = sb("ss", [P, DEPTH * NR, NT])
        ms = sb("ms", [P, DEPTH * NR, NT])
        rstd = sb("rstd", [P, DEPTH * NR, NT])
        neg_half = sb("neg_half", [P, NT])
        ssum = sb("ssum", [P, NT])
        nmean = sb("nmean", [P, NT])
        fz = sb("fz", [P, 4, NT * H])
        logf = sb("logf", [P, NT, H])
        Lq = sb("Lq", [P, NT, H])
        nmax = sb("nmax", [P, NT, H])
        psums = sb("psums", [P, NT, H])
        rsums = sb("rsums", [P, NT, H])
        lg = sb("lg", [P, NT, E])
        lmax = sb("lmax", [P, NT])
        rank = sb("rank", [P, NT, E])
        sel = sb("sel", [P, NT, E])
        gate = sb("gate", [P, NT, E])
        gden = sb("gden", [P, NT])
        posm = sb("posm", [P, NT, E])
        clsf = sb("clsf", [1, 3, E])
        cls = sb("cls", [1, E], I32)
        KIB = 256
        scratch = sb("scratch", [P, 58 * KIB])

        def at(kib, size_kib):
            return scratch[:, int(kib * KIB):int((kib + size_kib) * KIB)]

        qz = at(0, 8).rearrange("p (h t) -> p h t", h=H)
        kT = at(8, 4).rearrange("p (m t) -> p m t", m=AC)
        PT = at(0, 12).rearrange("p (b t) -> p b t", t=P)
        v_sb = at(12, 4).rearrange("p (i n) -> p i n", i=NT)
        u_sb = at(16, 4).rearrange("p (i n) -> p i n", i=NT)
        s_sb = at(20, 4).rearrange("p (i n) -> p i n", i=NT)
        S0 = at(24, 4).rearrange("p (h k) -> p h k", h=H)
        S1 = at(28, 8).rearrange("p (h k) -> p h k", h=H)
        xn = at(28, 8).rearrange("p (i d) -> p i d", i=NT)
        attn = at(36, 4).rearrange("p (i n) -> p i n", i=NT)
        wsp_raw = at(36, 4).rearrange("p (g s) -> p g s", g=G)
        sgu = at(40, 4).rearrange("p (i n) -> p i n", i=NT)
        wT = at(44, 4).rearrange("p (g t) -> p g t", g=G)
        neg_pick = at(48, 4).rearrange("p (h q) -> p h q", h=H)
        g_v_sb = at(52, 2)
        LT = at(54, 1)
        tmp = at(20, 8).rearrange("p (i d) -> p i d", i=NT)
        junk = at(56, 2).bitcast(BF16)
        mT = hT
        vec_raw = at(20, 1).rearrange("p (a b) -> p a b", a=2)
        act_d = at(12, 4).rearrange("p (b t) -> p b t", b=4)
        sil_d = at(16, 2).rearrange("p (b t) -> p b t", b=2)
        htok = at(0, 8).rearrange("p (i d) -> p i d", i=NT)
        xTe = at(8, 8).rearrange("p (k s) -> p k s", k=KC)
        yTe = at(16, 8).rearrange("p (k s) -> p k s", k=KC)
        ye = at(24, 8).rearrange("p (b d) -> p b d", b=NT)
        yacc = at(32, 8).rearrange("p (i d) -> p i d", i=NT)
        act_e = at(40, 4).rearrange("p (b t) -> p b t", b=4)
        sil_e = at(44, 2).rearrange("p (b t) -> p b t", b=2)
        pick = at(46, 2).rearrange("p (i s) -> p i s", i=NT)
        pickg = at(48, 2).rearrange("p (i s) -> p i s", i=NT)
        pickgT = at(50, 2).rearrange("p (b t) -> p b t", b=NT)
        iota = at(52, 1)
        tri_strict = at(53, 0.5)
        before = at(53.5, 0.25).rearrange("p (a b) -> p a b", a=E)
        cmp1 = at(54, 0.5).rearrange("p (i a b) -> p i a b", i=NT, a=E)
        cmp2 = at(54.5, 0.5).rearrange("p (i a b) -> p i a b", i=NT, a=E)
        tmp_e = at(16, 8).rearrange("p (i d) -> p i d", i=NT)

        ps = ctx.enter_context(nc.psum_tensor("ps", [P, 8, 512], F32))

        def bank(b, n=1):
            return ps[:, b:b + n, :].rearrange("p b n -> p (b n)")

        landed = [sem(f"landed{i}") for i in range(SLOTS)]
        freed = [sem(f"freed{i}") for i in range(SLOTS)]
        x_landed = sem("x_landed")
        vec_landed = sem("vec_landed")
        small_landed = sem("small_landed")
        row_landed = [sem(f"row_landed{i}") for i in range(2)]
        seed_landed = [sem(f"seed_landed{i}") for i in range(2)]
        wsp_landed = sem("wsp_landed")
        g_v_landed = sem("g_v_landed")
        out_stored = sem("out_stored")
        consts = sem("consts")
        seed_zero = sem("seed_zero")
        zeros = sem("zeros")
        vecT = sem("vecT")
        vec_ready = sem("vec_ready")
        c_ready = sem("c_ready")
        ada_summed = sem("ada_summed")
        ada_out = sem("ada_out")
        ada_done = sem("ada_done")
        dve_seq = sem("dve_seq")
        act_seq = sem("act_seq")
        pool_seq = sem("pool_seq")
        ss_ready = sem("ss_ready")
        ms_ready = sem("ms_ready")
        rstd_ready = sem("rstd_ready")
        xn_ready = sem("xn_ready")
        xT_ready = sem("xT_ready")
        hT_act = sem("hT_act")
        hT_dve = sem("hT_dve")
        x_new = sem("x_new")
        wsp_masked = sem("wsp_masked")
        wT_ps = sem("wT_ps")
        wT_ready = sem("wT_ready")
        proj = sem("proj")
        qk_ready = sem("qk_ready")
        z_ready = sem("z_ready")
        lnz_ready = sem("lnz_ready")
        logf_ready = sem("logf_ready")
        v_ready = sem("v_ready")
        L_ps = sem("L_ps")
        L_ready = sem("L_ready")
        score_ps = sem("score_ps")
        score_sb = sem("score_sb")
        masked = sem("masked")
        max_ready = sem("max_ready")
        exp_ready = sem("exp_ready")
        PT_ps = sem("PT_ps")
        PT_act = sem("PT_act")
        PT_dve = sem("PT_dve")
        gelu_ready = sem("gelu_ready")
        mean_ready = sem("mean_ready")
        s_ready = sem("s_ready")
        pv_ps = sem("pv_ps")
        attn_raw = sem("attn_raw")
        attn_ready = sem("attn_ready")
        mix_ps = sem("mix_ps")
        sgu_raw = sem("sgu_raw")
        sgu_ready = sem("sgu_ready")
        mT_ps = sem("mT_ps")
        mT_act = sem("mT_act")
        mT_dve = sem("mT_dve")
        y_ps = sem("y_ps")
        gu_ps = sem("gu_ps")
        sil_ready = sem("sil_ready")
        act_ready = sem("act_ready")
        act_used = sem("act_used")
        htok_ps = sem("htok_ps")
        htok_act = sem("htok_act")
        htok_dve = sem("htok_dve")
        logit_ps = sem("logit_ps")
        lmax_ready = sem("lmax_ready")
        gexp_ready = sem("gexp_ready")
        sel_ready = sem("sel_ready")
        pos_ps = sem("pos_ps")
        route_ready = sem("route_ready")
        moe_consts = sem("moe_consts")
        pick_ready = sem("pick_ready")
        pick_used = sem("pick_used")
        gath_ps = sem("gath_ps")
        xTe_act = sem("xTe_act")
        xTe_dve = sem("xTe_dve")
        yT_act = sem("yT_act")
        yT_dve = sem("yT_dve")
        ye_ps = sem("ye_ps")
        ye_act = sem("ye_act")
        ye_dve = sem("ye_dve")
        scat_ps = sem("scat_ps")
        yacc_done = sem("yacc_done")

        NORM_MIX, SV, ATTN, SGU, POST_MIX, NORM_FFN, POST_FFN = range(NR)

        rows0, r0 = {}, 0
        for name, ap, n in (("c", c, KC), ("g_pre_mix", g_pre_mix, DEPTH * KC), ("g_pre_ffn", g_pre_ffn, DEPTH * KC),
                            ("g_out_attn", g_out_attn, DEPTH * AC), ("g_out_sgu", g_out_sgu, DEPTH * AC)):
            rows0[name] = (ap.rearrange("l (k p) -> (l k) p", p=P), r0, n)
            r0 += n
        rows0["b_spatial"] = (b_spatial.rearrange("l g t -> (l g) t"), r0, DEPTH * G)
        R0 = r0 + DEPTH * G
        NB = DEPTH * 6 * KC
        assert R0 <= P and NB <= P

        def col(name, layer, k, n=1):
            at0 = rows0[name][1] + layer * (rows0[name][2] // DEPTH) + k
            return vec[:, 0, at0:at0 + n]

        def b_ada_col(layer, kind, k, n):
            at0 = (layer * 6 + kind) * KC + k
            return vec[:, 1, at0:at0 + n]

        def ring3(slot, w=HALF):
            return ring[:, slot * SLOT:(slot + 1) * SLOT].rearrange("p (k n) -> p k n", k=KC)[:, :, 0:w]

        def down3(slot):
            return ring[:, slot * SLOT:(slot + 1) * SLOT].rearrange("p (k n) -> p k n", k=TPC)

        def arrived(eng, key):
            slot, _, value = slot_of(key)
            eng.wait_ge(landed[slot], value)
            return slot

        ACT_KC = (0, 1, 4, 5)
        DVE_KC = (2, 3, 6, 7)

        ada_order = [k for k in stream if k[0] == "ada"]
        gate_order = [k for k in ada_order if KINDS[k[2]].startswith("gate")]

        def ada_bank(n):
            if n < 4:
                return 2 + n % 2
            if ada_order[n][0:3] in (("ada", 0, 2), ("ada", 1, 5)):
                return n % 2
            return 2 + n % 2

        block = ctx.enter_context(nc.Block())

        @block.sync
        def _(sp):
            in_col = {"q": 0, "k": AW, "v": 2 * AW, "u": 3 * AW + H, "s": 4 * AW + H}

            def source(key):
                kind, layer = key[:2]
                if kind == "ada":
                    a = key[2] * D + key[3] * HALF
                    return w_ada[layer, :, a:a + HALF].rearrange("(k p) n -> p k n", p=P)
                if kind == "in":
                    a = in_col[key[2]]
                    return w_in[layer, :, a:a + HALF].rearrange("(k p) n -> p k n", p=P)
                if kind == "out":
                    return w_out[layer, :, key[2] * HALF:(key[2] + 1) * HALF].rearrange("(k p) n -> p k n", p=P)
                a = key[2] * HALF
                w = min(HALF, FD - a)
                if kind == "down":
                    return w_down_dense[0, a:a + w, :].rearrange("(k p) n -> p k n", p=P)
                a += FD if kind == "up" else 0
                return w_gate_up_dense[0, :, a:a + w].rearrange("(k p) n -> p k n", p=P)

            for key in stream:
                slot, before_load, _ = slot_of(key)
                if before_load:
                    sp.wait_ge(freed[slot], before_load)
                src = source(key)
                dst = down3(slot)[:, 0:src.shape[1], :] if key[0] == "down" else ring3(slot, src.shape[2])
                sp.dma_start(dst, src).then_inc(landed[slot], 16)
            with sp.Fori(0, E) as e:
                for j in range(3 * SE):
                    slot, before_load, _ = slot_of(("exp", e, j))
                    sp.wait_ge(freed[slot], before_load)
                    s = j // 3
                    if j % 3 == 2:
                        dst, src = down3(slot), w_down_exp[0, bass.ds(e, 1), s * HALF:(s + 1) * HALF, :]
                    else:
                        a = s * HALF + (j % 3) * FE
                        dst, src = ring3(slot), w_gate_up_exp[0, bass.ds(e, 1), :, a:a + HALF]
                    sp.dma_start(dst, src.rearrange("a (k p) n -> p (a k) n", p=P)).then_inc(landed[slot], 16)

            for i in range(NT):
                sp.wait_ge(x_new, NT * 3 + i + 1)
                sp.dma_start(out[0, i * P:(i + 1) * P, :], x_sb[:, i, :]).then_inc(out_stored, 16)
            sp.wait_ge(out_stored, 16 * NT)

        @block.scalar
        def _(act):
            act.dma_start(vec_raw[0:KC, 0, :], rows0["c"][0]).then_inc(vec_landed, 16)
            for name in list(rows0)[1:]:
                src, r, n = rows0[name]
                act.dma_start(vec_raw[r:r + n, 0, :], src).then_inc(vec_landed, 16)
            act.dma_start(vec_raw[0:NB, 1, :], b_ada.rearrange("l (k p) -> (l k) p", p=P)).then_inc(vec_landed, 16)
            act.dma_start(x_sb[:, :, :], x[0].rearrange("(i p) d -> p i d", p=P)).then_inc(x_landed, 16)
            act.dma_start(w_r[:, :, :], w_router[0].rearrange("(k p) e -> p k e", p=P)).then_inc(small_landed, 16)

            def load_forget(layer):
                act.dma_start(w_f[:, :, :], w_in[layer, :, 3 * AW:3 * AW + H].rearrange("(k p) e -> p k e", p=P)).then_inc(small_landed, 16)
                act.dma_start(b_f[:, :], b_forget[layer:layer + 1, :].to_broadcast([P, H])).then_inc(small_landed, 16)

            def load_row(which, layer):
                src = (g_post_mix, g_post_ffn)[which]
                act.dma_start(row[:, which, :], src[layer:layer + 1, :].to_broadcast([P, D])).then_inc(row_landed[which], 16)

            def load_seed(n):
                _, layer, kind, half = gate_order[n]
                a = kind * D + half * HALF
                act.dma_start(ada_seed[0:1, n % 2, :], b_ada[layer:layer + 1, a:a + HALF]).then_inc(seed_landed[n % 2], 16)

            def load_spatial(layer):
                act.dma_start(wsp_raw, w_spatial[layer].rearrange("g t s -> t g s")).then_inc(wsp_landed, 16)
                act.dma_start(g_v_sb, g_v[layer:layer + 1, :].to_broadcast([P, AW])).then_inc(g_v_landed, 16)

            load_forget(0)
            load_spatial(0)
            load_row(0, 0)
            load_row(1, 0)
            act.wait_ge(seed_zero, 1)
            load_seed(0)
            load_seed(1)

            act.wait_ge(vec_ready, 1)
            act.activation(c_act[:, :], vec[:, 0, 0:KC], ACT.Silu).then_inc(c_ready, 1)

            def squares(src_of):
                def one(i, request):
                    src, bias = src_of(i)
                    kw = {} if bias is None else {"bias": bias}
                    if 2 * request + i:
                        act.wait_ge(ss_ready, 2 * request + i)
                    act.activation(junk[:, 0:src.shape[1]], src, ACT.Square, accum_out=ss[:, request, i:i + 1], **kw).then_inc(ss_ready, 1)
                return one

            def norm_input(n, layer, ffn, first):
                sq = squares(lambda i: (x_sb[:, i, :], None))
                for i in range(NT):
                    if first:
                        act.wait_ge(x_landed, 16)
                    else:
                        act.wait_ge(x_new, NT * (n - 1) + i + 1)
                    sq(i, layer * NR + (NORM_FFN if ffn else NORM_MIX))
                for kc in ACT_KC:
                    act.wait_ge(xT_ready, n * KC // 2 + kc // 2 + 1)
                    act.activation(hT[:, kc, :], bank(kc // 2)[:, (kc % 2) * T:(kc % 2 + 1) * T], ACT.Identity,
                                   bias=mod[:, layer, 2 * ffn, kc:kc + 1], scale=mod[:, layer, 2 * ffn + 1, kc:kc + 1]).then_inc(hT_act, 1)

            for layer in range(DEPTH):
                L = layer
                act.wait_ge(ada_done, 4 if L == 0 else len(ada_order) - 2)
                norm_input(2 * L, L, 0, L == 0)
                act.wait_ge(zeros, L + 1)
                for m in range(2):
                    act.wait_ge(proj, 11 * L + m + 1)
                    src = bank(4 + m).rearrange("p (a t) -> p a t", a=2)
                    for r in range(2):
                        a = act.activation(qz[64 * r:64 * r + 64, 4 * m + r:4 * m + r + 3:2, :], src[64 * r:64 * r + 64], ACT.Copy, scale=QSCALE)
                    a.then_inc(qk_ready, 1)
                for m in range(2):
                    act.wait_ge(proj, 11 * L + m + 3)
                    act.activation(kT[:, 2 * m:2 * m + 2, :], bank(6 + m).rearrange("p (a t) -> p a t", a=2), ACT.Copy).then_inc(qk_ready, 1)
                act.wait_ge(z_ready, L + 1)
                act.activation(fz[:, 3, :], fz[:, 1, :], ACT.Exp).then_inc(act_seq, 1)
                act.wait_ge(act_seq, L + 1)
                act.activation(fz[:, 3, :], fz[:, 3, :], ACT.Ln, bias=1.0).then_inc(lnz_ready, 1)
                for qb, S in enumerate((S0, S1)):
                    act.wait_ge(max_ready, 2 * L + qb + 1)
                    for h in range(H):
                        a = act.activation(S[:, h, :], S[:, h, :], ACT.Exp, bias=nmax[:, qb, h:h + 1], accum_out=psums[:, qb, h:h + 1])
                    a.then_inc(exp_ready, 1)
                for i in range(NT):
                    act.wait_ge(proj, 11 * L + 8 + i)
                    act.activation(u_sb[:, i, :], bank(6 + i), ACT.Gelu_apprx_tanh).then_inc(gelu_ready, 1)
                for i in range(NT):
                    act.wait_ge(proj, 11 * L + 10 + i)
                    act.activation(s_sb[:, i, :], bank(4 + i), ACT.Gelu_apprx_tanh, accum_out=ssum[:, i:i + 1]).then_inc(gelu_ready, 1)
                for n in range(0, 6, 2):
                    act.wait_ge(PT_ps, 6 * L + n + 1)
                    b = (0, 1, 2, 3, 6, 7)[n]
                    act.activation(PT[:, 4 * n:4 * n + 4, :], bank(b).rearrange("p (a t) -> p a t", t=P), ACT.Copy).then_inc(PT_act, 1)
                act.wait_ge(mean_ready, L + 1)
                sq = squares(lambda i: (s_sb[:, i, :], nmean[:, i:i + 1]))
                for i in range(NT):
                    sq(i, L * NR + SV)
                sq = squares(lambda i: (attn[:, i, :], None))
                for i in range(NT):
                    act.wait_ge(attn_raw, 2 * L + i + 1)
                    sq(i, L * NR + ATTN)
                sq = squares(lambda i: (sgu[:, i, :], None))
                for i in range(NT):
                    act.wait_ge(sgu_raw, 2 * L + i + 1)
                    sq(i, L * NR + SGU)
                for kc in ACT_KC:
                    act.wait_ge(mT_ps, 4 * L + kc // 2 + 1)
                    g = col("g_out_attn", L, kc) if kc < AC else col("g_out_sgu", L, kc - AC)
                    act.activation(mT[:, kc, :], bank(kc // 2)[:, (kc % 2) * T:(kc % 2 + 1) * T], ACT.Copy, scale=g).then_inc(mT_act, 1)
                if L == 0:
                    load_forget(1)
                    load_spatial(1)
                for i in range(NT):
                    act.wait_ge(y_ps, NT * 2 * L + i + 1)
                    squares(lambda i: (bank(4 + 2 * i, 2), None))(i, L * NR + POST_MIX)
                if L == 0:
                    act.wait_ge(ada_done, 4 + 2 + 4)
                norm_input(2 * L + 1, L, 1, False)
                if L == 0:
                    load_row(0, 1)
                    load_seed(2)
                    load_seed(3)
                    for t in range(DT):
                        act.wait_ge(gu_ps, t + 1)
                        if t >= 2:
                            act.wait_ge(act_ready, t - 1)
                        act.activation(sil_d[:, t % 2, :], bank(t % 2)[:, 0:T], ACT.Silu).then_inc(sil_ready, 1)
                        if t == 5:
                            act.wait_ge(ada_done, 12)
                            load_seed(4)
                            load_seed(5)
                    for i in range(NT):
                        act.wait_ge(y_ps, NT + i + 1)
                        squares(lambda i: (bank(4 + 2 * i, 2), None))(i, POST_FFN)
                    act.wait_ge(x_new, NT * 2)
                    load_row(1, 1)
                    act.wait_ge(ada_done, 18)
                    load_seed(6)
                    load_seed(7)

            act.wait_ge(htok_ps, 1)
            act.activation(htok[:, 0, :], bank(0, 2), ACT.Copy).then_inc(htok_act, 1)
            act.wait_ge(lmax_ready, 1)
            for i in range(NT):
                a = act.activation(gate[:, i, :], lg[:, i, :], ACT.Exp, bias=lmax[:, i:i + 1])
            a.then_inc(gexp_ready, 1)
            with act.Fori(0, E) as e:
                act.wait_ge(gath_ps, e * 4 + 2)
                act.activation(xTe[:, 0:4, :], bank(0, 2).rearrange("p (k s) -> p k s", s=T), ACT.Copy).then_inc(xTe_act, 1)
                for t in range(ET):
                    act.wait_ge(gu_ps, e * ET + DT + t + 1)
                    act.wait_ge(act_ready, e * ET + DT + t - 1)
                    act.activation(sil_e[:, t % 2, :], bank(t % 2)[:, 0:T], ACT.Silu).then_inc(sil_ready, 1)
                act.wait_ge(act_used, e * ET + DT + ET)
                act.activation(yTe[:, 0:4, :], bank(4, 2).rearrange("p (k s) -> p k s", s=T), ACT.Copy).then_inc(yT_act, 1)
                act.wait_ge(ye_ps, e + 1)
                act.activation(ye[:, 0, :], bank(0, 2), ACT.Copy).then_inc(ye_act, 1)
            for i in range(NT):
                act.wait_ge(yacc_done, NT * (E - 1) + i + 1 + 1)
                squares(lambda i: (yacc[:, i, :], None))(i, NR + POST_FFN)

        @block.gpsimd
        def _(pool):
            links = [0]

            def link(ins):
                links[0] += 1
                ins.then_inc(pool_seq, 1)
                pool.wait_ge(pool_seq, links[0])

            nc.gpsimd.memset(ident[:, :], 0.0)
            nc.gpsimd.memset(ones[:, :], 1.0)
            nc.gpsimd.memset(neg_half[:, :], -0.5)
            link(nc.gpsimd.memset(ada_seed[:, :, :], 0.0))
            nc.gpsimd.nop().then_inc(seed_zero, 1)
            nc.gpsimd.affine_select(out=ident[:, :], in_=ident[:, :], compare_op=ALU.not_equal, fill=1.0, base=0,
                                    pattern=[[-1, P]], channel_multiplier=1)
            nc.gpsimd.affine_select(out=tri[:, :], in_=ones[:, :], compare_op=ALU.is_ge, fill=0.0, base=0,
                                    pattern=[[1, P]], channel_multiplier=-1)
            nc.gpsimd.memset(LT, 0.0)
            link(nc.gpsimd.memset(neg_pick, 0.0))
            nc.gpsimd.affine_select(out=neg_pick, in_=neg_pick, compare_op=ALU.not_equal, fill=-1.0, base=0,
                                    pattern=[[-1, H], [0, P]], channel_multiplier=1).then_inc(consts, 1)

            def inverse(request):
                pool.wait_ge(ms_ready, request + 1)
                nc.gpsimd.tensor_tensor(rstd[:, request, :], ms[:, request, :], neg_half[:, :], ALU.pow).then_inc(rstd_ready, 1)

            for L in range(DEPTH):
                if L:
                    pool.wait_ge(pv_ps, 2 * L)
                nc.gpsimd.memset(qz, 0.0).then_inc(zeros, 1)
                pool.wait_ge(wsp_landed, 16 * (L + 1))
                nc.gpsimd.affine_select(out=wsp_raw, in_=wsp_raw, compare_op=ALU.is_ge, fill=0.0, base=0,
                                        pattern=[[0, G], [-1, P]], channel_multiplier=1).then_inc(wsp_masked, 1)
                inverse(L * NR + NORM_MIX)
                for qb, S in enumerate((S0, S1)):
                    pool.wait_ge(score_sb, 2 * L + qb + 1)
                    d = S[:, :, qb * P:(qb + 1) * P]
                    nc.gpsimd.affine_select(out=d, in_=d, compare_op=ALU.is_ge, fill=MASKED, base=0,
                                            pattern=[[0, H], [-1, P]], channel_multiplier=1).then_inc(masked, 1)
                for request in (SV, ATTN, SGU, POST_MIX, NORM_FFN):
                    inverse(L * NR + request)
                if L == 0:
                    inverse(POST_FFN)
            nc.gpsimd.iota(iota, pattern=[[1, T]], base=0, channel_multiplier=0, allow_small_or_imprecise_dtypes=True)
            nc.gpsimd.affine_select(out=tri_strict, in_=ones[:, :], compare_op=ALU.is_gt, fill=0.0, base=0,
                                    pattern=[[1, P]], channel_multiplier=-1)
            nc.gpsimd.affine_select(out=before, in_=ones[:, 0:E * E].rearrange("p (a b) -> p a b", a=E), compare_op=ALU.is_gt,
                                    fill=0.0, base=0, pattern=[[1, E], [-1, E]], channel_multiplier=0).then_inc(moe_consts, 1)
            inverse(NR + POST_FFN)

        @block.vector
        def _(dve):
            links = [0]

            def link(ins):
                links[0] += 1
                ins.then_inc(dve_seq, 1)
                dve.wait_ge(dve_seq, links[0])

            V = nc.vector
            dve.wait_ge(vecT, 1)
            V.tensor_copy(vec[:, 0, 0:R0], bank(0)[:, 0:R0])
            V.tensor_copy(vec[:, 1, 0:NB], bank(0)[:, P:P + NB]).then_inc(vec_ready, 1)

            def ada_sum(n):
                key = ada_order[n]
                is_gate = key in gate_order
                if n == 0:
                    dve.wait_ge(c_ready, 1)
                if n >= 2:
                    dve.wait_ge(ada_out, n - 1)
                if is_gate:
                    m = gate_order.index(key)
                    dve.wait_ge(seed_landed[m % 2], 16 * (m // 2 + 1))
                slot = arrived(dve, key)
                acc = ada_acc[:, n % 2, :]
                w = ring3(slot)
                if is_gate:
                    link(V.scalar_tensor_tensor(acc, w[:, 0, :], c_act[:, 0:1], ada_seed[:, m % 2, :], ALU.mult, ALU.add))
                else:
                    link(V.tensor_scalar(acc, w[:, 0, :], c_act[:, 0:1], None, ALU.mult))
                for k in range(1, KC):
                    link(V.scalar_tensor_tensor(acc, w[:, k, :], c_act[:, k:k + 1], acc, ALU.mult, ALU.add))
                V.nop().then_inc(freed[slot], 1)
                V.nop().then_inc(ada_summed, 1)

            def ada_finish(n):
                _, layer, kind, half = ada_order[n]
                dve.wait_ge(ada_out, n + 1)
                name = KINDS[kind]
                ffn = int(name.endswith("ffn"))
                ks = half * 4
                src = bank(ada_bank(n))
                if name.startswith("gate"):
                    dve.wait_ge(row_landed[ffn], 16 * (layer + 1))
                    r = row[:, ffn, half * HALF:(half + 1) * HALF]
                    V.scalar_tensor_tensor(r, src, 1.0, r, ALU.add, ALU.mult).then_inc(ada_done, 1)
                elif name.startswith("shift"):
                    V.tensor_tensor(mod[:, layer, 2 * ffn, ks:ks + 4], src[:, 0:4], b_ada_col(layer, kind, ks, 4), ALU.add).then_inc(ada_done, 1)
                else:
                    link(V.tensor_tensor(modt[:, :], src[:, 0:4], b_ada_col(layer, kind, ks, 4), ALU.add))
                    V.scalar_tensor_tensor(mod[:, layer, 2 * ffn + 1, ks:ks + 4], modt[:, :], 1.0,
                                           col("g_pre_ffn" if ffn else "g_pre_mix", layer, ks, 4), ALU.add, ALU.mult).then_inc(ada_done, 1)

            def mean_square(request, width):
                dve.wait_ge(ss_ready, 2 * (request + 1))
                V.tensor_scalar(ms[:, request, :], ss[:, request, :], 1.0 / width, EPS, ALU.mult, ALU.add).then_inc(ms_ready, 1)

            def norm_input(n, layer, ffn):
                request = layer * NR + (NORM_FFN if ffn else NORM_MIX)
                mean_square(request, D)
                dve.wait_ge(rstd_ready, request + 1)
                for i in range(NT):
                    V.tensor_scalar(xn[:, i, :], x_sb[:, i, :], rstd[:, request, i:i + 1], None, ALU.mult).then_inc(xn_ready, 1)
                for kc in DVE_KC:
                    dve.wait_ge(xT_ready, n * KC // 2 + kc // 2 + 1)
                    V.tensor_scalar(hT[:, kc, :], bank(kc // 2)[:, (kc % 2) * T:(kc % 2 + 1) * T], mod[:, layer, 2 * ffn + 1, kc:kc + 1],
                                    mod[:, layer, 2 * ffn, kc:kc + 1], ALU.mult, ALU.add).then_inc(hT_dve, 1)

            def post(request, which, ys, tmp_, n):
                mean_square(request, D)
                dve.wait_ge(rstd_ready, request + 1)
                for i in range(NT):
                    link(V.scalar_tensor_tensor(tmp_[:, i, :], ys[i], rstd[:, request, i:i + 1], row[:, which, :], ALU.mult, ALU.mult))
                    V.tensor_tensor(x_sb[:, i, :], x_sb[:, i, :], tmp_[:, i, :], ALU.add).then_inc(x_new, 1)

            nada = 0
            for n in range(4):
                ada_sum(n)
                ada_finish(n)
            nada = 4
            for L in range(DEPTH):
                if L:
                    dve.wait_ge(ada_done, len(ada_order) - 2)
                else:
                    dve.wait_ge(ada_done, 4)
                norm_input(2 * L, L, 0)
                for n in range(2):
                    dve.wait_ge(wT_ps, 2 * L + n + 1)
                    V.tensor_copy(wT[:, 4 * n:4 * n + 4, :], bank(6 + n).rearrange("p (a t) -> p a t", t=P)).then_inc(wT_ready, 1)
                dve.wait_ge(proj, 11 * L + 5)
                dve.wait_ge(small_landed, 16 * (3 + 2 * L))
                link(V.tensor_tensor(fz[:, 0, :].rearrange("p (i h) -> p i h", i=NT), bank(0)[:, 0:NT * H].rearrange("p (i h) -> p i h", i=NT),
                                     b_f[:, :].unsqueeze(1).to_broadcast([P, NT, H]), ALU.add))
                V.tensor_scalar(fz[:, 2, :], fz[:, 0, :], 0.0, None, ALU.min)
                V.scalar_tensor_tensor(fz[:, 1, :], fz[:, 0, :], -1.0, fz[:, 0, :], ALU.mult, ALU.min).then_inc(z_ready, 1)
                for i in range(NT):
                    dve.wait_ge(proj, 11 * L + 6 + i)
                    V.tensor_copy(v_sb[:, i, :], bank(2 + i)).then_inc(v_ready, 1)
                dve.wait_ge(lnz_ready, L + 1)
                V.tensor_tensor(logf[:, :, :].rearrange("p i h -> p (i h)"), fz[:, 2, :], fz[:, 3, :], ALU.subtract).then_inc(logf_ready, 1)
                dve.wait_ge(L_ps, L + 1)
                dve.wait_ge(consts, 1)
                V.tensor_copy(LT[0:H, :], bank(1)[0:H, 0:T])
                V.tensor_copy(Lq[:, :, :].rearrange("p i h -> p (i h)"), bank(1)[:, T:T + NT * H]).then_inc(L_ready, 1)
                dve.wait_ge(L_ready, L + 1)
                dve.wait_ge(score_ps, 2 * L + 1)
                V.tensor_tensor(S0, bank(4, 2).rearrange("p (h k) -> p h k", h=H), Lq[:, 0, :].unsqueeze(2).to_broadcast([P, H, P]), ALU.add).then_inc(score_sb, 1)
                dve.wait_ge(score_ps, 2 * L + 2)
                V.tensor_tensor(S1, bank(0, 4).rearrange("p (h k) -> p h k", h=H), Lq[:, 1, :].unsqueeze(2).to_broadcast([P, H, T]), ALU.add).then_inc(score_sb, 1)
                for qb, S in enumerate((S0, S1)):
                    dve.wait_ge(masked, 2 * L + qb + 1)
                    V.tensor_reduce(nmax[:, qb, :], S, AX_X, ALU.max, negate=True).then_inc(max_ready, 1)
                for _ in range(2):
                    ada_sum(nada)
                    ada_finish(nada)
                    nada += 1
                dve.wait_ge(exp_ready, 2 * L + 2)
                link(V.reciprocal(rsums[:, :, :], psums[:, :, :]))
                for n in range(1, 6, 2):
                    dve.wait_ge(PT_ps, 6 * L + n + 1)
                    b = (0, 1, 2, 3, 6, 7)[n]
                    V.tensor_copy(PT[:, 4 * n:4 * n + 4, :], bank(b).rearrange("p (a t) -> p a t", t=P)).then_inc(PT_dve, 1)
                dve.wait_ge(gelu_ready, 4 * L + 4)
                V.tensor_scalar(nmean[:, :], ssum[:, :], -1.0 / AW, None, ALU.mult).then_inc(mean_ready, 1)
                mean_square(L * NR + SV, AW)
                dve.wait_ge(rstd_ready, L * NR + SV + 1)
                dve.wait_ge(g_v_landed, 16 * (L + 1))
                for i in range(NT):
                    link(V.tensor_scalar(s_sb[:, i, :], s_sb[:, i, :], nmean[:, i:i + 1], rstd[:, L * NR + SV, i:i + 1], ALU.add, ALU.mult))
                    V.tensor_tensor(s_sb[:, i, :], s_sb[:, i, :], g_v_sb, ALU.mult).then_inc(s_ready, 1)
                for i in range(NT):
                    dve.wait_ge(pv_ps, 2 * L + i + 1)
                    V.tensor_tensor(attn[:, i, :].rearrange("p (h d) -> p h d", h=H), bank(4 + i).rearrange("p (h d) -> p h d", h=H),
                                    rsums[:, i, :].unsqueeze(2).to_broadcast([P, H, DH]), ALU.mult).then_inc(attn_raw, 1)
                mean_square(L * NR + ATTN, AW)
                for i in range(NT):
                    dve.wait_ge(mix_ps, 2 * L + i + 1)
                    link(V.tensor_tensor(sgu[:, i, :].rearrange("p (g d) -> p g d", g=G), bank(6 + i).rearrange("p (g d) -> p g d", g=G),
                                         col("b_spatial", L, 0, G).unsqueeze(2).to_broadcast([P, G, DH]), ALU.add))
                    V.tensor_tensor(sgu[:, i, :], sgu[:, i, :], u_sb[:, i, :], ALU.mult).then_inc(sgu_raw, 1)
                dve.wait_ge(rstd_ready, L * NR + ATTN + 1)
                for i in range(NT):
                    V.tensor_scalar(attn[:, i, :], attn[:, i, :], rstd[:, L * NR + ATTN, i:i + 1], None, ALU.mult).then_inc(attn_ready, 1)
                mean_square(L * NR + SGU, AW)
                dve.wait_ge(rstd_ready, L * NR + SGU + 1)
                for i in range(NT):
                    V.tensor_scalar(sgu[:, i, :], sgu[:, i, :], rstd[:, L * NR + SGU, i:i + 1], None, ALU.mult).then_inc(sgu_ready, 1)
                for kc in DVE_KC:
                    dve.wait_ge(mT_ps, 4 * L + kc // 2 + 1)
                    g = col("g_out_attn", L, kc) if kc < AC else col("g_out_sgu", L, kc - AC)
                    V.tensor_scalar(mT[:, kc, :], bank(kc // 2)[:, (kc % 2) * T:(kc % 2 + 1) * T], g, None, ALU.mult).then_inc(mT_dve, 1)
                if L == 0:
                    for _ in range(4):
                        ada_sum(nada)
                        ada_finish(nada)
                        nada += 1
                post(L * NR + POST_MIX, 0, [bank(4 + 2 * i, 2) for i in range(NT)], tmp, 2 * L)
                norm_input(2 * L + 1, L, 1)
                if L == 0:
                    for t in range(DT):
                        dve.wait_ge(sil_ready, t + 1)
                        if t >= 4:
                            dve.wait_ge(act_used, t - 3)
                        V.tensor_tensor(act_d[:, t % 4, :], sil_d[:, t % 2, :], bank(t % 2)[:, T:2 * T], ALU.mult).then_inc(act_ready, 1)
                        for key in ada_after.get(t, []):
                            ada_sum(nada)
                            ada_finish(nada)
                            nada += 1
                    post(POST_FFN, 1, [bank(4 + 2 * i, 2) for i in range(NT)], tmp, 1)

            dve.wait_ge(htok_ps, 2)
            V.tensor_copy(htok[:, 1, :], bank(2, 2)).then_inc(htok_dve, 1)
            dve.wait_ge(logit_ps, 1)
            link(V.tensor_copy(lg[:, :, :].rearrange("p i e -> p (i e)"), bank(4)[:, 0:NT * E]))
            V.tensor_reduce(lmax[:, :], lg[:, :, :], AX_X, ALU.max, negate=True).then_inc(lmax_ready, 1)
            other = lg[:, :, :].unsqueeze(2).to_broadcast([P, NT, E, E])
            own = lg[:, :, :].unsqueeze(3).to_broadcast([P, NT, E, E])
            V.tensor_tensor(cmp1, other, own, ALU.is_gt)
            link(V.tensor_tensor(cmp2, other, own, ALU.is_equal))
            dve.wait_ge(moe_consts, 1)
            for i in range(NT):
                l = V.tensor_tensor(cmp2[:, i], cmp2[:, i], before, ALU.mult)
            link(l)
            link(V.tensor_tensor(cmp1, cmp1, cmp2, ALU.add))
            link(V.tensor_reduce(rank[:, :, :], cmp1, AX_X, ALU.add))
            V.tensor_scalar(sel[:, :, :], rank[:, :, :], 2.0, None, ALU.is_lt).then_inc(sel_ready, 1)
            dve.wait_ge(sel_ready, 1)
            dve.wait_ge(gexp_ready, 1)
            link(V.tensor_tensor(gate[:, :, :], gate[:, :, :], sel[:, :, :], ALU.mult))
            link(V.tensor_reduce(gden[:, :], gate[:, :, :], AX_X, ALU.add))
            link(V.reciprocal(gden[:, :], gden[:, :]))
            for i in range(NT):
                V.tensor_scalar(gate[:, i, :], gate[:, i, :], gden[:, i:i + 1], None, ALU.mult)
            dve.wait_ge(pos_ps, 1)
            link(V.scalar_tensor_tensor(posm[:, :, :].rearrange("p i e -> p (i e)"), bank(4)[:, 0:NT * E], 1.0,
                                        sel[:, :, :].rearrange("p i e -> p (i e)"), ALU.add, ALU.mult))
            V.tensor_scalar(posm[:, :, :], posm[:, :, :], -1.0, None, ALU.add)
            count = bank(4)[0:1, NT * E:NT * E + E]
            link(V.tensor_scalar(clsf[:, 0, :], count, float(WIDTHS[0]), None, ALU.is_gt))
            for n, w in enumerate(WIDTHS[1:-1]):
                link(V.scalar_tensor_tensor(clsf[:, (n + 1) % 2, :], count, float(w), clsf[:, n % 2, :], ALU.is_gt, ALU.add))
            link(V.tensor_copy(cls[:, :], clsf[:, (len(WIDTHS) - 2) % 2, :]))
            V.nop().then_inc(route_ready, 1)
            V.memset(yacc, 0.0).then_inc(yacc_done, 1)
            with dve.Fori(0, E) as e:
                dve.wait_ge(yacc_done, e * NT + 1)
                for i in range(NT):
                    V.tensor_scalar(pick[:, i, :], iota, posm[:, i, bass.ds(e, 1)], None, ALU.is_equal)
                    l = V.tensor_scalar(pickg[:, i, :], iota, posm[:, i, bass.ds(e, 1)], gate[:, i, bass.ds(e, 1)], ALU.is_equal, ALU.mult)
                l.then_inc(pick_ready, 1)
                dve.wait_ge(gath_ps, e * 4 + 4)
                V.tensor_copy(xTe[:, 4:8, :], bank(2, 2).rearrange("p (k s) -> p k s", s=T)).then_inc(xTe_dve, 1)
                dve.wait_ge(pick_used, e + 1)
                V.tensor_copy(pickgT, bank(4).rearrange("p (b t) -> p b t", b=NT)).then_inc(xTe_dve, 1)
                for t in range(ET):
                    dve.wait_ge(sil_ready, e * ET + DT + t + 1)
                    dve.wait_ge(act_used, e * ET + DT + t - 3)
                    V.tensor_tensor(act_e[:, t % 4, :], sil_e[:, t % 2, :], bank(t % 2)[:, T:2 * T], ALU.mult).then_inc(act_ready, 1)
                dve.wait_ge(act_used, e * ET + DT + ET)
                V.tensor_copy(yTe[:, 4:8, :], bank(6, 2).rearrange("p (k s) -> p k s", s=T)).then_inc(yT_dve, 1)
                dve.wait_ge(ye_ps, e + 1)
                V.tensor_copy(ye[:, 1, :], bank(2, 2)).then_inc(ye_dve, 1)
                for i in range(NT):
                    dve.wait_ge(scat_ps, e * NT + i + 1)
                    V.tensor_tensor(yacc[:, i, :], yacc[:, i, :], bank(4 + 2 * i, 2), ALU.add).then_inc(yacc_done, 1)
            post(NR + POST_FFN, 1, [yacc[:, i, :] for i in range(NT)], tmp_e, 3)

        @block.tensor
        def _(pe):
            mm = nc.tensor.matmul

            pe.wait_ge(consts, 1)
            pe.wait_ge(vec_landed, 16 * (len(rows0) + 1))
            for a, n in enumerate((R0, NB)):
                l = nc.tensor.transpose(bank(0)[:, a * P:a * P + n], vec_raw[0:n, a, :], ident[0:n, 0:n])
            l.then_inc(vecT, 1)
            nada = [0]

            def ada_reduce():
                n = nada[0]
                nada[0] += 1
                pe.wait_ge(ada_summed, n + 1)
                if n >= 2:
                    pe.wait_ge(ada_done, n - 1)
                acc = ada_acc[:, n % 2, :]
                dst = bank(ada_bank(n))
                if ada_order[n] in gate_order:
                    mm(dst, ones[:, :], acc, start=True, stop=True).then_inc(ada_out, 1)
                else:
                    for j in range(4):
                        l = mm(dst[:, j:j + 1], acc[:, j * P:(j + 1) * P], ones[:, 0:1], start=True, stop=True)
                    l.then_inc(ada_out, 1)

            for _ in range(4):
                ada_reduce()
            pe.wait_ge(ada_done, 4)

            def norm_input(n):
                for kc in range(KC):
                    for i in range(NT):
                        if kc == 0:
                            pe.wait_ge(xn_ready, NT * n + i + 1)
                        l = nc.tensor.transpose(bank(kc // 2)[:, (kc % 2) * T + i * P:(kc % 2) * T + (i + 1) * P],
                                                xn[:, i, kc * P:(kc + 1) * P], ident[:, :])
                    if kc % 2:
                        l.then_inc(xT_ready, 1)
                pe.wait_ge(hT_act, 4 * (n + 1))
                pe.wait_ge(hT_dve, 4 * (n + 1))

            gu = [0]

            for L in range(DEPTH):
                if L:
                    pe.wait_ge(x_new, NT * 2)
                pe.wait_ge(wsp_masked, L + 1)
                for g in range(G):
                    l = nc.tensor.transpose(bank(6 + g // 4)[:, (g % 4) * P:(g % 4 + 1) * P], wsp_raw[:, g, :], ident[:, :])
                    if g % 4 == 3:
                        l.then_inc(wT_ps, 1)
                norm_input(2 * L)
                pe.wait_ge(wT_ready, 2 * L + 2)
                for j, name in enumerate("qk"):
                    slot = arrived(pe, ("in", L, name))
                    w = ring3(slot)
                    for m in range(AC):
                        dst = bank(4 + 2 * j + m // 2)[:, (m % 2) * T:(m % 2 + 1) * T]
                        for k in range(KC):
                            l = mm(dst, w[:, k, m * P:(m + 1) * P], hT[:, k, :], start=(k == 0), stop=(k == KC - 1))
                        if m % 2:
                            l.then_inc(proj, 1)
                    pe.wait_ge(proj, 11 * L + 2 * j + 2)
                    pe.nop().then_inc(freed[slot], 1)
                pe.wait_ge(small_landed, 16 * (3 + 2 * L))
                for i in range(NT):
                    for k in range(KC):
                        l = mm(bank(0)[:, i * H:(i + 1) * H], hT[:, k, i * P:(i + 1) * P], w_f[:, k, :], start=(k == 0), stop=(k == KC - 1))
                l.then_inc(proj, 1)

                def project(name, first, count):
                    slot = arrived(pe, ("in", L, name))
                    w = ring3(slot)
                    for i in range(NT):
                        for k in range(KC):
                            l = mm(bank(first + i), hT[:, k, i * P:(i + 1) * P], w[:, k, :], start=(k == 0), stop=(k == KC - 1))
                        l.then_inc(proj, 1)
                    pe.wait_ge(proj, 11 * L + count)
                    pe.nop().then_inc(freed[slot], 1)

                project("v", 2, 7)
                pe.wait_ge(logf_ready, L + 1)
                pe.wait_ge(consts, 1)
                dst = bank(1)[0:H, 0:P]
                mm(dst, logf[:, 0, :], tri[:, :], start=True, stop=True)
                dst = bank(1)[0:H, P:T]
                mm(dst, logf[:, 0, :], ones[:, :], start=True, stop=False)
                mm(dst, logf[:, 1, :], tri[:, :], start=False, stop=True)
                mm(bank(1)[:, T:T + H], tri[:, :], logf[:, 0, :], start=True, stop=True)
                mm(bank(1)[:, T + H:T + 2 * H], ones[:, :], logf[:, 0, :], start=True, stop=False)
                mm(bank(1)[:, T + H:T + 2 * H], tri[:, :], logf[:, 1, :], start=False, stop=True).then_inc(L_ps, 1)
                pe.wait_ge(qk_ready, 4 * (L + 1))
                pe.wait_ge(L_ready, L + 1)
                pe.wait_ge(v_ready, 2 * (L + 1))
                for qb in range(NT):
                    nk = (qb + 1) * P
                    for h in range(H):
                        dst = bank(4, 2)[:, h * P:(h + 1) * P] if qb == 0 else bank(0, 4)[:, h * T:(h + 1) * T]
                        mm(dst, qz[:, h, qb * P:(qb + 1) * P], kT[:, h // 2, 0:nk], start=True, stop=False)
                        l = mm(dst, neg_pick[:, h, :], LT[:, 0:nk], start=False, stop=True)
                    l.then_inc(score_ps, 1)
                project("u", 6, 9)
                pe.wait_ge(score_sb, 2 * L + 1)
                project("s", 4, 11)
                pe.wait_ge(score_sb, 2 * L + 2)
                for _ in range(2):
                    ada_reduce()
                pe.wait_ge(ada_done, nada[0])
                pe.wait_ge(exp_ready, 2 * L + 2)
                for b in range(24):
                    n = b // 4
                    if b == 16:
                        pe.wait_ge(gelu_ready, 4 * L + 2)
                    src = S1[:, b // 2, (b % 2) * P:(b % 2 + 1) * P] if b < 16 else S0[:, b - 16, :]
                    l = nc.tensor.transpose(bank((0, 1, 2, 3, 6, 7)[n])[:, (b % 4) * P:(b % 4 + 1) * P], src, ident[:, :])
                    if b % 4 == 3:
                        l.then_inc(PT_ps, 1)
                pe.wait_ge(gelu_ready, 4 * L + 4)
                pe.wait_ge(PT_act, 3 * (L + 1))
                pe.wait_ge(PT_dve, 3 * (L + 1))
                for qb in range(NT):
                    for h in range(H):
                        dst = bank(4 + qb)[:, h * DH:(h + 1) * DH]
                        for kb in range(qb + 1):
                            l = mm(dst, PT[:, 2 * h + kb if qb else 16 + h, :], v_sb[:, kb, h * DH:(h + 1) * DH], start=(kb == 0), stop=(kb == qb))
                    l.then_inc(pv_ps, 1)
                for i in range(NT):
                    pe.wait_ge(s_ready, 2 * L + i + 1)
                    for g in range(G):
                        l = mm(bank(6 + i)[:, g * DH:(g + 1) * DH], wT[:, g, :], s_sb[:, i, g * DH:(g + 1) * DH], start=True, stop=True)
                    l.then_inc(mix_ps, 1)
                for branch, (src, ready) in enumerate(((attn, attn_ready), (sgu, sgu_ready))):
                    pe.wait_ge(ready, 2 * (L + 1))
                    for kc in range(AC):
                        for i in range(NT):
                            l = nc.tensor.transpose(bank(2 * branch + kc // 2)[:, (kc % 2) * T + i * P:(kc % 2) * T + (i + 1) * P],
                                                    src[:, i, kc * P:(kc + 1) * P], ident[:, :])
                        if kc % 2:
                            l.then_inc(mT_ps, 1)
                pe.wait_ge(mT_act, 4 * (L + 1))
                pe.wait_ge(mT_dve, 4 * (L + 1))
                slots = [arrived(pe, ("out", L, half)) for half in range(2)]
                for i in range(NT):
                    for half in range(2):
                        for k in range(KC):
                            l = mm(bank(4 + 2 * i + half), mT[:, k, i * P:(i + 1) * P], ring3(slots[half])[:, k, :], start=(k == 0), stop=(k == KC - 1))
                        if half == 1:
                            l.then_inc(y_ps, 1)
                        elif i == NT - 1:
                            l.then_inc(freed[slots[0]], 1)
                        if L == 0:
                            ada_reduce()
                pe.wait_ge(y_ps, NT * 2 * L + NT)
                pe.nop().then_inc(freed[slots[1]], 1)
                if L == 0:
                    pe.wait_ge(ada_done, nada[0])
                norm_input(2 * L + 1)
                if L == 0:
                    pe.wait_ge(x_new, NT)

                    def dense_up(t):
                        s, j = divmod(t, TPC)
                        slots = [arrived(pe, (k, 0, s)) for k in ("gate", "up")]
                        if t >= 2:
                            pe.wait_ge(act_ready, t - 1)
                        for n in range(2):
                            for k in range(KC):
                                l = mm(bank(t % 2)[:, n * T:(n + 1) * T], ring3(slots[n])[:, k, j * P:(j + 1) * P], hT[:, k, :],
                                       start=(k == 0), stop=(k == KC - 1))
                            if n == 0 and ends(t):
                                l.then_inc(freed[slots[0]], 1)
                        l.then_inc(gu_ps, 1)

                    def dense_down(t):
                        s, j = divmod(t, TPC)
                        slot = arrived(pe, ("down", 0, s))
                        pe.wait_ge(act_ready, t + 1)
                        for i in range(NT):
                            for half in range(2):
                                l = mm(bank(4 + 2 * i + half), act_d[:, t % 4, i * P:(i + 1) * P],
                                       down3(slot)[:, j, half * HALF:(half + 1) * HALF], start=(t == 0), stop=(t == DT - 1))
                            if t == DT - 1:
                                l.then_inc(y_ps, 1)
                        if t < DT - 1:
                            l.then_inc(act_used, 1)

                    def ends(t):
                        return t % TPC == TPC - 1 or t == DT - 1

                    for t in range(DT):
                        dense_up(t)
                        if t:
                            dense_down(t - 1)
                        if ends(t):
                            pe.wait_ge(gu_ps, t + 1)
                            pe.nop().then_inc(freed[slot_of(("up", 0, t // TPC))[0]], 1)
                        if t >= 2 and ends(t - 2):
                            pe.wait_ge(act_used, t - 1)
                            pe.nop().then_inc(freed[slot_of(("down", 0, (t - 2) // TPC))[0]], 1)
                        for _ in ada_after.get(t - 1, []):
                            ada_reduce()
                    dense_down(DT - 1)
                    pe.wait_ge(y_ps, 2 * NT)
                    pe.nop().then_inc(act_used, 1)
                    pe.nop().then_inc(freed[slot_of(("down", 0, SD - 1))[0]], 1)
                    pe.wait_ge(ada_done, nada[0])

            for i in range(NT):
                for k in range(KC):
                    l = nc.tensor.transpose(bank(2 * i, 2)[:, k * P:(k + 1) * P], hT[:, k, i * P:(i + 1) * P], ident[:, :])
                l.then_inc(htok_ps, 1)
            pe.wait_ge(x_new, NT * 3)
            for i in range(NT):
                for k in range(KC):
                    l = mm(bank(4)[:, i * E:(i + 1) * E], hT[:, k, i * P:(i + 1) * P], w_r[:, k, :], start=(k == 0), stop=(k == KC - 1))
            l.then_inc(logit_ps, 1)
            pe.wait_ge(sel_ready, 1)
            pe.wait_ge(moe_consts, 1)
            mm(bank(4)[:, 0:E], tri_strict, sel[:, 0, :], start=True, stop=True)
            mm(bank(4)[:, E:2 * E], ones[:, :], sel[:, 0, :], start=True, stop=False)
            mm(bank(4)[:, E:2 * E], tri_strict, sel[:, 1, :], start=False, stop=True)
            mm(bank(4)[:, 2 * E:3 * E], ones[:, :], sel[:, 0, :], start=True, stop=False)
            mm(bank(4)[:, 2 * E:3 * E], ones[:, :], sel[:, 1, :], start=False, stop=True).then_inc(pos_ps, 1)
            pe.wait_ge(route_ready, 1)
            pe.wait_ge(htok_act, 1)
            pe.wait_ge(htok_dve, 1)

            def expert(e, W):
                blocks = [(b, min(P, W - b * P)) for b in range(-(-W // P))]
                pe.wait_ge(pick_ready, e + 1)
                for k in range(KC):
                    for i in range(NT):
                        l = mm(bank(k // 2)[:, (k % 2) * T:(k % 2) * T + W], htok[:, i, k * P:(k + 1) * P], pick[:, i, 0:W],
                               start=(i == 0), stop=(i == NT - 1))
                    if k % 2:
                        l.then_inc(gath_ps, 1)
                for b, _ in blocks:
                    for i in range(NT):
                        l = nc.tensor.transpose(bank(4)[:, b * T + i * P:b * T + (i + 1) * P], pickg[:, i, b * P:(b + 1) * P], ident[:, :])
                l.then_inc(pick_used, 1)
                pe.wait_ge(xTe_act, e + 1)
                pe.wait_ge(xTe_dve, e * 2 + 2)

                def up(t):
                    s, j = divmod(t, TPC)
                    slots = [arrived(pe, ("exp", e, 3 * s + n)) for n in range(2)]
                    if t >= 2:
                        pe.wait_ge(act_ready, e * ET + DT + t - 1)
                    for n in range(2):
                        for k in range(KC):
                            l = mm(bank(t % 2)[:, n * T:n * T + W], ring3(slots[n])[:, k, j * P:(j + 1) * P], xTe[:, k, 0:W],
                                   start=(k == 0), stop=(k == KC - 1))
                        if n == 0 and j == TPC - 1:
                            l.then_inc(freed[slots[0]], 1)
                    l.then_inc(gu_ps, 1)

                def down(t):
                    s, j = divmod(t, TPC)
                    slot = arrived(pe, ("exp", e, 3 * s + 2))
                    pe.wait_ge(act_ready, e * ET + DT + t + 1)
                    for k in range(KC):
                        l = mm(bank(4 + k // 2)[:, (k % 2) * T:(k % 2) * T + W], down3(slot)[:, j, k * P:(k + 1) * P], act_e[:, t % 4, 0:W],
                               start=(t == 0 and k % 2 == 0), stop=(t == ET - 1), skip_group_check=True)
                    l.then_inc(act_used, 1)

                def give_back(n, s):
                    pe.nop().then_inc(freed[slot_of(("exp", e, 3 * s + n))[0]], 1)

                for t in range(ET):
                    up(t)
                    if t:
                        down(t - 1)
                    if t % TPC == TPC - 1:
                        pe.wait_ge(gu_ps, e * ET + DT + t + 1)
                        give_back(1, t // TPC)
                    if t >= TPC and (t - 2) % TPC == TPC - 1:
                        pe.wait_ge(act_used, e * ET + DT + t - 1)
                        give_back(2, (t - 2) // TPC)
                down(ET - 1)
                pe.wait_ge(act_used, e * ET + DT + ET)
                give_back(2, SE - 1)
                pe.wait_ge(yT_act, e + 1)
                pe.wait_ge(yT_dve, e + 1)
                for b, _ in blocks:
                    for k in range(KC):
                        l = nc.tensor.transpose(bank(2 * b, 2)[:, k * P:(k + 1) * P], yTe[:, k, b * P:(b + 1) * P], ident[:, :])
                l.then_inc(ye_ps, 1)
                pe.wait_ge(ye_act, e + 1)
                pe.wait_ge(ye_dve, e + 1)
                for i in range(NT):
                    for half in range(2):
                        for b, w in blocks:
                            l = mm(bank(4 + 2 * i + half), pickgT[0:w, b, i * P:(i + 1) * P], ye[0:w, b, half * HALF:(half + 1) * HALF],
                                   start=(b == 0), stop=(b == len(blocks) - 1))
                    l.then_inc(scat_ps, 1)

            with pe.Fori(0, E) as e:
                size = pe.value_load(cls[0:1, bass.ds(e, 1)], min_val=0, max_val=len(WIDTHS) - 1)
                for n, W in enumerate(WIDTHS):
                    with pe.If(size == n):
                        expert(e, W)
                    with pe.Else():
                        pe.nop()


_INS = ["x", "c", "w_ada", "b_ada", "g_pre_mix", "g_post_mix", "g_pre_ffn", "g_post_ffn", "w_in", "b_forget", "g_v",
        "w_spatial", "b_spatial", "g_out_attn", "g_out_sgu", "w_out", "w_gate_up_dense", "w_down_dense", "w_router",
        "w_gate_up_exp", "w_down_exp"]


def kernel(**inputs):
    import numpy as _np
    import concourse.bacc as _bacc
    from concourse import mybir as _mybir
    from concourse.bass_utils import run_bass_kernel_spmd as _run

    nc = _bacc.Bacc("TRN2", target_bir_lowering=False, num_devices=1)
    arrays, args = {}, []
    for name in _INS:
        a = _np.ascontiguousarray(inputs[name])
        arrays[f"in_{name}_dram"] = a
        args.append(nc.dram_tensor(f"in_{name}_dram", a.shape, _mybir.dt.from_np(a.dtype), kind="ExternalInput").ap())
    o = nc.dram_tensor("out_0_dram", inputs["x"].shape, _mybir.dt.float32, kind="ExternalOutput").ap()
    hybrid_fox_sgu_moe(nc, *args, o)
    r = _run(nc, [arrays], core_ids=[0])
    return r.results[0]["out_0_dram"]
```

```python
from contextlib import ExitStack

import concourse.bass as bass
from concourse import mybir

F32 = mybir.dt.float32
F32R = mybir.dt.float32r
BF16 = mybir.dt.bfloat16
I32 = mybir.dt.int32
ALU = mybir.AluOpType
ACT = mybir.ActivationFunctionType
AX_X = mybir.AxisListType.X

P = 128
RAW = 6
STAGED = 3
AHEAD = STAGED
PIECE = 2048
EPS = 1e-6
MASKED = -1e38
KINDS = ("shift_mix", "scale_mix", "gate_mix", "shift_ffn", "scale_ffn", "gate_ffn")


def ada(layer, *names):
    return [("ada", layer, KINDS.index(n), half) for n in names for half in range(2)]


def ffn_order(steps, down_pieces):
    order = []
    for s in range(steps + 1):
        if s < steps:
            order += [(kind, s, h) for kind in ("gate", "up") for h in range(2)]
        if s:
            order += [("down", s - 1, h) for h in range(down_pieces(s - 1))]
    return order


def hybrid_fox_sgu_moe(nc, x, c, w_ada, b_ada, g_pre_mix, g_post_mix, g_pre_ffn, g_post_ffn,
                       w_in, b_forget, g_v, w_spatial, b_spatial, g_out_attn, g_out_sgu, w_out,
                       w_gate_up_dense, w_down_dense, w_router, w_gate_up_exp, w_down_exp, out):
    _, T, D = x.shape
    DEPTH = w_ada.shape[0]
    AW = g_out_attn.shape[1]
    H = b_forget.shape[1]
    G = w_spatial.shape[1]
    DH = AW // H
    FD = w_down_dense.shape[1]
    E = w_router.shape[2]
    FE = w_down_exp.shape[2]
    KC = D // P
    NT = T // P
    AC = AW // P
    HALF = 512
    TPC = HALF // P
    DT = FD // P
    ET = FE // P
    SE = FE // HALF
    SD = -(-DT // TPC)
    QSCALE = float(DH) ** -0.5
    assert KC * HALF == 2 * PIECE and DEPTH == 2 and T == 2 * P and D == 1024 and FE % HALF == 0

    def dense_tiles(s):
        return min(TPC, DT - s * TPC)

    stream = []

    def put(*chunks):
        for key in chunks:
            stream.extend(key + (h,) for h in range(2))

    put(*ada(0, "shift_mix", "scale_mix"))
    mixer_ada = (dict(zip("qkvu", ada(0, "gate_mix", "shift_ffn"))), dict(zip("qk", ada(1, "gate_ffn"))))
    out_ada = ada(0, "scale_ffn")
    dense_ada = ada(0, "gate_ffn") + ada(1, "shift_mix", "scale_mix", "gate_mix", "shift_ffn", "scale_ffn")
    assert len(dense_ada) == 2 * SD
    for layer in range(DEPTH):
        for name in ("q", "k", "v", "u", "s"):
            put(("in", layer, name))
            if name in mixer_ada[layer]:
                put(mixer_ada[layer][name])
        for half in range(2):
            for h in range(2):
                stream.append(("out", layer, half, h))
                if layer == 0 and half == 0:
                    put(out_ada[h])
        if layer == 0:
            for kind, s, h in ffn_order(SD, lambda s: dense_tiles(s) // 2):
                stream.append(("ffn", kind, s, h))
                if h == 1 and kind != "down":
                    put(dense_ada[2 * s + (kind == "up")])
    raw_at = {key: n for n, key in enumerate(stream)}
    staged_at = {key: m for m, key in enumerate(k for k in stream if k[0] != "ada")}
    staged_keys = list(staged_at)
    ada_order = [k[:4] for k in stream if k[0] == "ada" and k[4] == 0]
    gate_order = [k for k in ada_order if KINDS[k[2]].startswith("gate")]
    expert_order = ffn_order(SE, lambda s: 2)
    expert_at = {k: j for j, k in enumerate(expert_order)}
    N0, M0, PE_ = len(stream), len(staged_at), len(expert_order)
    GATHERED = 3 * DEPTH * KC // 2
    assert PE_ % RAW == 0 and PE_ % STAGED == 0

    def raw_index(key):
        return (N0 + expert_at[key[2:]], key[1] * PE_) if key[0] == "exp" else (raw_at[key], 0)

    def staged_index(key):
        return (M0 + expert_at[key[2:]], key[1] * PE_) if key[0] == "exp" else (staged_at[key], 0)

    ctx = ExitStack()
    with ctx:
        def sb(name, shape, dt=F32):
            return ctx.enter_context(nc.sbuf_tensor(name, shape, dt))

        def sem(name):
            return ctx.enter_context(nc.semaphore(name))

        raw = sb("raw", [P, RAW, PIECE])
        w_hi = sb("w_hi", [P, STAGED, PIECE], F32R)
        w_lo = sb("w_lo", [P, STAGED, PIECE], F32R)
        hT_hi = sb("hT_hi", [P, KC, T], F32R)
        hT_lo = sb("hT_lo", [P, KC, T], F32R)
        actT_hi = sb("actT_hi", [P, TPC, T], F32R)
        actT_lo = sb("actT_lo", [P, TPC, T], F32R)
        x_sb = sb("x_sb", [P, NT, D])
        row = sb("row", [P, 2, D])
        ada_acc = sb("ada_acc", [P, 2, HALF])
        ada_seed = sb("ada_seed", [P, 2, HALF])
        ident = sb("ident", [P, P])
        tri = sb("tri", [P, P])
        ones = sb("ones", [P, P])
        vec = sb("vec", [P, 2, P])
        mod = sb("mod", [P, DEPTH, 4, KC])
        modt = sb("modt", [P, 4])
        w_f = sb("w_f", [P, KC, H])
        w_r = sb("w_r", [P, KC, E])
        b_f = sb("b_f", [P, H])
        c_act = sb("c_act", [P, KC])
        NR = 7
        ss = sb("ss", [P, DEPTH * NR, NT])
        ms = sb("ms", [P, DEPTH * NR, NT])
        rstd = sb("rstd", [P, DEPTH * NR, NT])
        neg_half = sb("neg_half", [P, NT])
        ssum = sb("ssum", [P, NT])
        nmean = sb("nmean", [P, NT])
        fz = sb("fz", [P, 4, NT * H])
        logf = sb("logf", [P, NT, H])
        Lq = sb("Lq", [P, NT, H])
        nmax = sb("nmax", [P, NT, H])
        psums = sb("psums", [P, NT, H])
        rsums = sb("rsums", [P, NT, H])
        lg = sb("lg", [P, NT, E])
        lmax = sb("lmax", [P, NT])
        rank = sb("rank", [P, NT, E])
        sel = sb("sel", [P, NT, E])
        gate = sb("gate", [P, NT, E + 1])
        gden = sb("gden", [P, NT])
        posm = sb("posm", [P, NT, E + 1])
        wide = sb("wide", [1, E], I32)
        KIB = 256
        scratch = sb("scratch", [P, 58 * KIB])

        def at(kib, size_kib):
            return scratch[:, int(kib * KIB):int((kib + size_kib) * KIB)]

        qz = at(0, 8).rearrange("p (h t) -> p h t", h=H)
        kT = at(8, 4).rearrange("p (m t) -> p m t", m=AC)
        PT = at(0, 12).rearrange("p (b t) -> p b t", t=P)
        v_sb = at(12, 4).rearrange("p (i n) -> p i n", i=NT)
        u_sb = at(16, 4).rearrange("p (i n) -> p i n", i=NT)
        s_sb = at(20, 4).rearrange("p (i n) -> p i n", i=NT)
        S0 = at(24, 4).rearrange("p (h k) -> p h k", h=H)
        S1 = at(28, 8).rearrange("p (h k) -> p h k", h=H)
        xn = at(28, 8).rearrange("p (i d) -> p i d", i=NT)
        attn = at(36, 4).rearrange("p (i n) -> p i n", i=NT)
        wsp_raw = at(36, 4).rearrange("p (g s) -> p g s", g=G)
        sgu = at(40, 4).rearrange("p (i n) -> p i n", i=NT)
        wT = at(44, 4).rearrange("p (g t) -> p g t", g=G)
        neg_pick = at(48, 4).rearrange("p (h q) -> p h q", h=H)
        g_v_sb = at(52, 2)
        LT = at(54, 1)
        tmp = at(20, 8).rearrange("p (i d) -> p i d", i=NT)
        junk = at(56, 2).bitcast(BF16)
        hT = at(16, 8).rearrange("p (k t) -> p k t", k=KC)
        vec_raw = at(20, 1).rearrange("p (a b) -> p a b", a=2)
        sil = at(8, 4).rearrange("p (b n) -> p b n", b=NT)
        act_t = at(12, 4).rearrange("p (b n) -> p b n", b=NT)
        htok = at(0, 8).rearrange("p (i d) -> p i d", i=NT)
        ye = at(24, 8).rearrange("p (b d) -> p b d", b=NT)
        yacc = at(32, 8).rearrange("p (i d) -> p i d", i=NT)
        pick = at(46, 2).rearrange("p (i s) -> p i s", i=NT)
        pickg = at(48, 2).rearrange("p (i s) -> p i s", i=NT)
        pickgT = at(50, 2).rearrange("p (b t) -> p b t", b=NT)
        iota = at(52, 1)
        tri_strict = at(53, 0.5)
        before = at(53.5, 0.25).rearrange("p (a b) -> p a b", a=E)
        cmp1 = at(54, 0.5).rearrange("p (i a b) -> p i a b", i=NT, a=E)
        cmp2 = at(54.5, 0.5).rearrange("p (i a b) -> p i a b", i=NT, a=E)
        tmp_e = at(16, 8).rearrange("p (i d) -> p i d", i=NT)

        ps = ctx.enter_context(nc.psum_tensor("ps", [P, 8, 512], F32))

        def bank(b, n=1):
            return ps[:, b:b + n, :].rearrange("p b n -> p (b n)")

        landed = [sem(f"landed{i}") for i in range(RAW)]
        raw_used = sem("raw_used")
        hi_ready = sem("hi_ready")
        used = sem("used")
        hTf_act = sem("hTf_act")
        hTf_dve = sem("hTf_dve")
        hT_hi_ready = sem("hT_hi_ready")
        hT_lo_ready = sem("hT_lo_ready")
        T_ps = sem("T_ps")
        actT_hi_ready = sem("actT_hi_ready")
        actT_lo_ready = sem("actT_lo_ready")
        f_ps = sem("f_ps")
        k_ready = sem("k_ready")
        pickg_ready = sem("pickg_ready")
        pickgT_ps = sem("pickgT_ps")
        pickgT_ready = sem("pickgT_ready")
        x_landed = sem("x_landed")
        vec_landed = sem("vec_landed")
        small_landed = sem("small_landed")
        row_landed = [sem(f"row_landed{i}") for i in range(2)]
        seed_landed = [sem(f"seed_landed{i}") for i in range(2)]
        wsp_landed = sem("wsp_landed")
        g_v_landed = sem("g_v_landed")
        out_stored = sem("out_stored")
        consts = sem("consts")
        seed_zero = sem("seed_zero")
        zeros = sem("zeros")
        vecT = sem("vecT")
        vec_ready = sem("vec_ready")
        c_ready = sem("c_ready")
        ada_out = sem("ada_out")
        ada_done = sem("ada_done")
        dve_seq = sem("dve_seq")
        act_seq = sem("act_seq")
        pool_seq = sem("pool_seq")
        ss_ready = sem("ss_ready")
        ms_ready = sem("ms_ready")
        rstd_ready = sem("rstd_ready")
        xn_ready = sem("xn_ready")
        xT_ready = sem("xT_ready")
        x_new = sem("x_new")
        wsp_masked = sem("wsp_masked")
        wT_ps = sem("wT_ps")
        wT_ready = sem("wT_ready")
        qk_ready = sem("qk_ready")
        z_ready = sem("z_ready")
        lnz_ready = sem("lnz_ready")
        logf_ready = sem("logf_ready")
        v_ready = sem("v_ready")
        L_ps = sem("L_ps")
        L_ready = sem("L_ready")
        score_ps = sem("score_ps")
        score_sb = sem("score_sb")
        masked = sem("masked")
        max_ready = sem("max_ready")
        exp_ready = sem("exp_ready")
        PT_ps = sem("PT_ps")
        PT_act = sem("PT_act")
        PT_dve = sem("PT_dve")
        gelu_ready = sem("gelu_ready")
        mean_ready = sem("mean_ready")
        s_ready = sem("s_ready")
        pv_ps = sem("pv_ps")
        attn_raw = sem("attn_raw")
        attn_ready = sem("attn_ready")
        mix_ps = sem("mix_ps")
        sgu_raw = sem("sgu_raw")
        sgu_ready = sem("sgu_ready")
        mT_ps = sem("mT_ps")
        y_ps = sem("y_ps")
        sil_ready = sem("sil_ready")
        act_ready = sem("act_ready")
        htok_ps = sem("htok_ps")
        htok_act = sem("htok_act")
        htok_dve = sem("htok_dve")
        logit_ps = sem("logit_ps")
        lmax_ready = sem("lmax_ready")
        gexp_ready = sem("gexp_ready")
        sel_ready = sem("sel_ready")
        pos_ps = sem("pos_ps")
        route_ready = sem("route_ready")
        moe_consts = sem("moe_consts")
        pick_ready = sem("pick_ready")
        gath_ps = sem("gath_ps")
        second_ps = sem("second_ps")
        second_hi = sem("second_hi")
        second_lo = sem("second_lo")
        ye_act = sem("ye_act")
        ye_dve = sem("ye_dve")
        scat_ps = sem("scat_ps")
        yacc_done = sem("yacc_done")

        NORM_MIX, SV, ATTN, SGU, POST_MIX, NORM_FFN, POST_FFN = range(NR)

        rows0, r0 = {}, 0
        for name, ap, n in (("c", c, KC), ("g_pre_mix", g_pre_mix, DEPTH * KC), ("g_pre_ffn", g_pre_ffn, DEPTH * KC),
                            ("g_out_attn", g_out_attn, DEPTH * AC), ("g_out_sgu", g_out_sgu, DEPTH * AC)):
            rows0[name] = (ap.rearrange("l (k p) -> (l k) p", p=P), r0, n)
            r0 += n
        rows0["b_spatial"] = (b_spatial.rearrange("l g t -> (l g) t"), r0, DEPTH * G)
        R0 = r0 + DEPTH * G
        NB = DEPTH * 6 * KC
        assert R0 <= P and NB <= P

        def col(name, layer, k, n=1):
            at0 = rows0[name][1] + layer * (rows0[name][2] // DEPTH) + k
            return vec[:, 0, at0:at0 + n]

        def b_ada_col(layer, kind, k, n):
            at0 = (layer * 6 + kind) * KC + k
            return vec[:, 1, at0:at0 + n]

        def raw3(slot, w=HALF):
            return raw[:, slot, :].rearrange("p (k n) -> p k n", n=HALF)[:, :, 0:w]

        def shaped(t, slot, key):
            if key[-3] == "down":
                return t[:, slot, :].rearrange("p (k n) -> p k n", n=D)
            w = P * dense_tiles(key[2]) if key[0] == "ffn" else HALF
            return t[:, slot, :].rearrange("p (k n) -> p k n", n=HALF)[:, :, 0:w]

        def arrived(eng, key):
            n, part = raw_index(key)
            eng.wait_ge(landed[n % RAW], 16 * (n // RAW + 1) + part * 16 // RAW if key[0] != "exp" else 16 * (n // RAW + 1) + key[1] * (16 * PE_ // RAW))
            return n % RAW

        def write_hi(act, key):
            slot = arrived(act, key)
            m, part = staged_index(key)
            if m >= STAGED:
                act.wait_ge(used, m - STAGED + 1 + part)
            act.activation(shaped(w_hi, m % STAGED, key), shaped(raw, slot, key), ACT.Copy).then_inc(hi_ready, 1)

        def write_lo(dve, key):
            n, _ = raw_index(key)
            m, part = staged_index(key)
            dve.wait_ge(hi_ready, m + 1 + part)
            nc.vector.tensor_tensor(shaped(w_lo, m % STAGED, key), shaped(raw, n % RAW, key),
                                    shaped(w_hi, m % STAGED, key).bitcast(F32), ALU.subtract).then_inc(raw_used, 1)

        def staged(pe, key):
            n, part = raw_index(key)
            pe.wait_ge(raw_used, n + 1 + part)
            m, _ = staged_index(key)
            return shaped(w_hi, m % STAGED, key), shaped(w_lo, m % STAGED, key)

        def products_done(eng, key):
            m, part = staged_index(key)
            eng.wait_ge(used, m + 1 + part)

        def slots(t, b, block):
            return t[:, 4 * b:4 * b + 4, block * P:(block + 1) * P]

        def act_column(B, s):
            return (s % 2) * P if B == 1 else 0

        ACT_BANKS = (0, 2)
        DVE_BANKS = (1, 3)

        def ada_bank(n):
            key = ada_order[n]
            for beside in mixer_ada:
                for name, chunk in beside.items():
                    if key == chunk:
                        return {"q": 2, "k": 1, "v": 0, "u": 1}[name]
            if key in dense_ada:
                return 2 * (n % 2) + int(key in dense_ada[:2])
            return (4 if n < 4 else 2) + n % 2

        block = ctx.enter_context(nc.Block())

        @block.sync
        def _(sp):
            in_col = {"q": 0, "k": AW, "v": 2 * AW, "u": 3 * AW + H, "s": 4 * AW + H}

            def source(key):
                kind, layer = key[:2]
                h = key[-1]
                rows = slice(h * D // 2, (h + 1) * D // 2)
                if kind == "ada":
                    a = key[2] * D + key[3] * HALF
                    return w_ada[layer, rows, a:a + HALF]
                if kind == "in":
                    a = in_col[key[2]]
                    return w_in[layer, rows, a:a + HALF]
                if kind == "out":
                    return w_out[layer, rows, key[2] * HALF:(key[2] + 1) * HALF]
                kind, s = key[1:3]
                a = s * HALF
                if kind == "down":
                    return w_down_dense[0, a + h * 2 * P:a + (h + 1) * 2 * P, :]
                w = P * dense_tiles(s)
                a += FD if kind == "up" else 0
                return w_gate_up_dense[0, rows, a:a + w]

            for src, r, n in rows0.values():
                sp.dma_start(vec_raw[r:r + n, 0, :], src).then_inc(vec_landed, 16)
            sp.dma_start(vec_raw[0:NB, 1, :], b_ada.rearrange("l (k p) -> (l k) p", p=P)).then_inc(vec_landed, 16)
            for n, key in enumerate(stream):
                if n == 2:
                    sp.dma_start(x_sb[:, :, :], x[0].rearrange("(i p) d -> p i d", p=P)).then_inc(x_landed, 16)
                if n >= RAW:
                    sp.wait_ge(raw_used, n - RAW + 1)
                dst = raw3(n % RAW) if key[0] == "ada" else shaped(raw, n % RAW, key)
                sp.dma_start(dst, source(key).rearrange("(k p) n -> p k n", p=P)).then_inc(landed[n % RAW], 16)
            with sp.Fori(0, E) as e:
                for j, (kind, s, h) in enumerate(expert_order):
                    n = N0 + j
                    sp.wait_ge(raw_used, n - RAW + 1 + e * PE_)
                    if kind == "down":
                        a = s * HALF + h * 2 * P
                        src = w_down_exp[0, bass.ds(e, 1), a:a + 2 * P, :]
                    else:
                        a = s * HALF + (FE if kind == "up" else 0)
                        src = w_gate_up_exp[0, bass.ds(e, 1), h * D // 2:(h + 1) * D // 2, a:a + HALF]
                    sp.dma_start(shaped(raw, n % RAW, ("exp", e, kind, s, h)),
                                 src.rearrange("a (k p) n -> p (a k) n", p=P)).then_inc(landed[n % RAW], 16)

            for i in range(NT):
                sp.wait_ge(x_new, NT * 3 + i + 1)
                sp.dma_start(out[0, i * P:(i + 1) * P, :], x_sb[:, i, :]).then_inc(out_stored, 16)
            sp.wait_ge(out_stored, 16 * NT)

        @block.scalar
        def _(act):
            act.dma_start(w_r[:, :, :], w_router[0].rearrange("(k p) e -> p k e", p=P)).then_inc(small_landed, 16)

            def load_forget(layer):
                act.dma_start(w_f[:, :, :], w_in[layer, :, 3 * AW:3 * AW + H].rearrange("(k p) e -> p k e", p=P)).then_inc(small_landed, 16)
                act.dma_start(b_f[:, :], b_forget[layer:layer + 1, :].to_broadcast([P, H])).then_inc(small_landed, 16)

            def load_row(which, layer):
                src = (g_post_mix, g_post_ffn)[which]
                act.dma_start(row[:, which, :], src[layer:layer + 1, :].to_broadcast([P, D])).then_inc(row_landed[which], 16)

            def load_seed(n):
                _, layer, kind, half = gate_order[n]
                a = kind * D + half * HALF
                act.dma_start(ada_seed[0:1, n % 2, :], b_ada[layer:layer + 1, a:a + HALF]).then_inc(seed_landed[n % 2], 16)

            def load_spatial(layer):
                act.dma_start(wsp_raw, w_spatial[layer].rearrange("g t s -> t g s")).then_inc(wsp_landed, 16)
                act.dma_start(g_v_sb, g_v[layer:layer + 1, :].to_broadcast([P, AW])).then_inc(g_v_landed, 16)

            load_forget(0)
            load_spatial(0)
            load_row(0, 0)
            load_row(1, 0)
            act.wait_ge(seed_zero, 1)
            load_seed(0)
            load_seed(1)

            act.wait_ge(vec_ready, 1)
            act.activation(c_act[:, :], vec[:, 0, 0:KC], ACT.Silu).then_inc(c_ready, 1)

            def squares(src_of):
                def one(i, request):
                    src, bias = src_of(i)
                    kw = {} if bias is None else {"bias": bias}
                    if 2 * request + i:
                        act.wait_ge(ss_ready, 2 * request + i)
                    act.activation(junk[:, 0:src.shape[1]], src, ACT.Square, accum_out=ss[:, request, i:i + 1], **kw).then_inc(ss_ready, 1)
                return one

            done = [0]

            def advance(key):
                while done[0] <= staged_at[key]:
                    write_hi(act, staged_keys[done[0]])
                    done[0] += 1

            def input_squares(n, layer, ffn):
                sq = squares(lambda i: (x_sb[:, i, :], None))
                for i in range(NT):
                    if n == 0:
                        act.wait_ge(x_landed, 16)
                    else:
                        act.wait_ge(x_new, NT * (n - 1) + i + 1)
                    sq(i, layer * NR + (NORM_FFN if ffn else NORM_MIX))

            def input_parts(n, scale_bias, ps_ready):
                for b in ACT_BANKS:
                    act.wait_ge(ps_ready[0], ps_ready[1] + b + 1)
                    for kc in (2 * b, 2 * b + 1):
                        scale, bias = scale_bias(kc)
                        a = act.activation(hT[:, kc, :], bank(b)[:, (kc % 2) * T:(kc % 2 + 1) * T],
                                           ACT.Identity if bias is not None else ACT.Copy, scale=scale, **({} if bias is None else {"bias": bias}))
                    a.then_inc(hTf_act, 1)
                for b in range(4):
                    if b in ACT_BANKS:
                        act.wait_ge(hTf_act, 2 * n + b // 2 + 1)
                    else:
                        act.wait_ge(hTf_dve, 2 * n + b // 2 + 1)
                    act.activation(hT_hi[:, 2 * b:2 * b + 2, :], hT[:, 2 * b:2 * b + 2, :], ACT.Copy).then_inc(hT_hi_ready, 1)

            def modulation(layer, ffn):
                return lambda kc: (mod[:, layer, 2 * ffn + 1, kc:kc + 1], mod[:, layer, 2 * ffn, kc:kc + 1])

            def branch_gain(layer):
                return lambda kc: (col("g_out_attn", layer, kc) if kc < AC else col("g_out_sgu", layer, kc - AC), None)

            def silu(step, B, w, key):
                products_done(act, key)
                act.wait_ge(act_ready, step)
                for b in range(B):
                    a = act.activation(sil[:, b, 0:w], bank(2 * b)[:, 0:w], ACT.Silu)
                a.then_inc(sil_ready, 1)

            def act_hi(step, B, w, tbank, c0=0):
                act.wait_ge(T_ps, step + 1)
                for b in range(B):
                    a = act.activation(actT_hi[:, 0:w // P, c0 + b * P:c0 + (b + 1) * P], bank(tbank(b))[:, 0:w].rearrange("p (t n) -> p t n", n=P), ACT.Copy)
                a.then_inc(actT_hi_ready, 1)

            for layer in range(DEPTH):
                L = layer
                input_squares(2 * L, L, 0)
                act.wait_ge(ada_done, 4 if L == 0 else len(ada_order) - 2)
                input_parts(3 * L, modulation(L, 0), (xT_ready, 8 * L))
                advance(("in", L, "k", 0))
                act.wait_ge(zeros, L + 1)
                products_done(act, ("in", L, "q", 1))
                for m in range(2):
                    src = bank(4 + m).rearrange("p (a t) -> p a t", a=2)
                    for r in range(2):
                        a = act.activation(qz[64 * r:64 * r + 64, 4 * m + r:4 * m + r + 3:2, :], src[64 * r:64 * r + 64], ACT.Copy, scale=QSCALE)
                a.then_inc(qk_ready, 1)
                advance(("in", L, "v", 1))
                products_done(act, ("in", L, "k", 1))
                act.activation(kT, bank(6, 2).rearrange("p (a t) -> p a t", a=AC), ACT.Copy).then_inc(k_ready, 1)
                act.wait_ge(z_ready, L + 1)
                act.activation(fz[:, 3, :], fz[:, 1, :], ACT.Exp).then_inc(act_seq, 1)
                act.wait_ge(act_seq, L + 1)
                act.activation(fz[:, 3, :], fz[:, 3, :], ACT.Ln, bias=1.0).then_inc(lnz_ready, 1)
                advance(("in", L, "s", 0))
                for qb, S in enumerate((S0, S1)):
                    act.wait_ge(max_ready, 2 * L + qb + 1)
                    for h in range(H):
                        a = act.activation(S[:, h, :], S[:, h, :], ACT.Exp, bias=nmax[:, qb, h:h + 1], accum_out=psums[:, qb, h:h + 1])
                    a.then_inc(exp_ready, 1)
                    if qb == 0:
                        advance(("in", L, "s", 1))
                products_done(act, ("in", L, "u", 1))
                for i in range(NT):
                    act.activation(u_sb[:, i, :], bank(6 + i), ACT.Gelu_apprx_tanh).then_inc(gelu_ready, 1)
                products_done(act, ("in", L, "s", 1))
                for i in range(NT):
                    act.activation(s_sb[:, i, :], bank(4 + i), ACT.Gelu_apprx_tanh, accum_out=ssum[:, i:i + 1]).then_inc(gelu_ready, 1)
                for n in range(0, 6, 2):
                    act.wait_ge(PT_ps, 6 * L + n + 1)
                    b = (0, 1, 2, 3, 6, 7)[n]
                    act.activation(PT[:, 4 * n:4 * n + 4, :], bank(b).rearrange("p (a t) -> p a t", t=P), ACT.Copy).then_inc(PT_act, 1)
                act.wait_ge(mean_ready, L + 1)
                sq = squares(lambda i: (s_sb[:, i, :], nmean[:, i:i + 1]))
                for i in range(NT):
                    sq(i, L * NR + SV)
                advance(("out", L, 0, 0))
                sq = squares(lambda i: (attn[:, i, :], None))
                for i in range(NT):
                    act.wait_ge(attn_raw, 2 * L + i + 1)
                    sq(i, L * NR + ATTN)
                sq = squares(lambda i: (sgu[:, i, :], None))
                for i in range(NT):
                    act.wait_ge(sgu_raw, 2 * L + i + 1)
                    sq(i, L * NR + SGU)
                input_parts(3 * L + 1, branch_gain(L), (mT_ps, 4 * L))
                advance(("out", L, 1, 1))
                if L == 0:
                    load_forget(1)
                    load_spatial(1)
                    advance(("ffn", "gate", 0, 1))
                products_done(act, ("out", L, 1, 1))
                for i in range(NT):
                    squares(lambda i: (bank(4 + 2 * i, 2), None))(i, L * NR + POST_MIX)
                if L == 0:
                    advance(("ffn", "up", 0, 0))
                input_squares(2 * L + 1, L, 1)
                act.wait_ge(ada_done, 10 if L == 0 else len(ada_order))
                input_parts(3 * L + 2, modulation(L, 1), (xT_ready, 8 * L + 4))
                if L == 0:
                    load_row(0, 1)
                    load_seed(2)
                    load_seed(3)
                    order = ffn_order(SD, lambda s: dense_tiles(s) // 2)
                    for j, (kind, s, h) in enumerate(order):
                        advance(("ffn", kind, s, h))
                        for kind, s, h in ((order[j - STAGED + 1],) if j >= STAGED - 1 else ()) if j < len(order) - 1 else order[j - STAGED + 1:]:
                            w = P * dense_tiles(s)
                            if kind == "up" and h == 1:
                                silu(s, NT, w, ("ffn", "up", s, 1))
                                if s == 0:
                                    act_hi(s, NT, w, lambda b: 2 * b + 1)
                            if kind == "down" and h == dense_tiles(s) // 2 - 1 and s < SD - 1:
                                act_hi(s + 1, NT, P * dense_tiles(s + 1), lambda b: 2 * b + 1)
                                if s == 0:
                                    act.wait_ge(ada_done, 12)
                                    load_seed(4)
                                    load_seed(5)
                    products_done(act, ("ffn", "down", SD - 1, 0))
                    for i in range(NT):
                        squares(lambda i: (bank(4 + 2 * i, 2), None))(i, POST_FFN)
                    advance(("in", 1, "q", 1))
                    act.wait_ge(x_new, NT * 2)
                    load_row(1, 1)
                    act.wait_ge(ada_done, 18)
                    load_seed(6)
                    load_seed(7)

            act.wait_ge(htok_ps, 1)
            act.activation(htok[:, 0, :], bank(0, 2), ACT.Copy).then_inc(htok_act, 1)
            act.wait_ge(lmax_ready, 1)
            for i in range(NT):
                a = act.activation(gate[:, i, 0:E], lg[:, i, :], ACT.Exp, bias=lmax[:, i:i + 1])
            a.then_inc(gexp_ready, 1)

            def gathered(e, first):
                act.wait_ge(gath_ps, e + 1)
                for b in range(2):
                    act.activation(slots(hT_hi, b, 0), bank(first + b).rearrange("p (k t) -> p k t", t=P), ACT.Copy).then_inc(hT_hi_ready, 1)

            def expert(e, B, last):
                order, step0 = expert_order, SD + e * SE
                if B == 2:
                    act.wait_ge(second_ps, e + 1)
                    for b in range(2):
                        a = act.activation(slots(hT_hi, b, 1), bank(2 + b).rearrange("p (k t) -> p k t", t=P), ACT.Copy)
                    a.then_inc(second_hi, 1)
                else:
                    act.nop().then_inc(second_hi, 1)
                for j, (kind, s, h) in enumerate(order):
                    if j >= AHEAD:
                        write_hi(act, ("exp", e, kind, s, h))
                    for kind, s, h in ((order[j - STAGED + 1],) if j >= STAGED - 1 else ()) if j < PE_ - 1 else order[j - STAGED + 1:]:
                        if kind == "up" and h == 1:
                            silu(step0 + s, B, HALF, ("exp", e, "up", s, 1))
                            if s == 0 and B == 2:
                                act_hi(step0 + s, B, HALF, lambda b: 2 * b + 1)
                            if s == SE - 1 and B == 1:
                                gathered(e + 1, 6)
                        if B == 1 and kind == "gate" and s == 1 and h == 1:
                            act_hi(step0, B, HALF, lambda b: 2)
                        if kind == "down" and s < SE - 1 and h == B - 1:
                            act_hi(step0 + s + 1, B, HALF, (lambda b: 2) if B == 1 else (lambda b: 2 * b + 1), act_column(B, s + 1))
                if not last:
                    write_hi(act, ("exp", e + 1) + order[0])
                products_done(act, ("exp", e, "down", SE - 1, 1))
                for b in range(B):
                    a = act.activation(ye[:, b, 0:HALF], bank(4 + 2 * b), ACT.Copy)
                a.then_inc(ye_act, 1)
                if B == 2:
                    gathered(e + 1, 0)
                if not last:
                    for key in order[1:AHEAD]:
                        write_hi(act, ("exp", e + 1) + key)

            def routed(e, last):
                size = act.value_load(wide[0:1, bass.ds(e, 1)], min_val=0, max_val=1)
                with act.If(size == 0):
                    expert(e, 1, last)
                with act.Else():
                    expert(e, 2, last)

            gathered(0, 6)
            for key in expert_order[:AHEAD]:
                write_hi(act, ("exp", 0) + key)
            act.wait_ge(route_ready, 1)
            with act.Fori(0, E - 1) as e:
                routed(e, False)
            routed(E - 1, True)
            for i in range(NT):
                act.wait_ge(yacc_done, NT * E + i + 1)
                squares(lambda i: (yacc[:, i, :], None))(i, NR + POST_FFN)

        @block.gpsimd
        def _(pool):
            links = [0]

            def link(ins):
                links[0] += 1
                ins.then_inc(pool_seq, 1)
                pool.wait_ge(pool_seq, links[0])

            nc.gpsimd.memset(ident[:, :], 0.0)
            nc.gpsimd.memset(ones[:, :], 1.0)
            nc.gpsimd.memset(neg_half[:, :], -0.5)
            link(nc.gpsimd.memset(ada_seed[:, :, :], 0.0))
            nc.gpsimd.nop().then_inc(seed_zero, 1)
            nc.gpsimd.affine_select(out=ident[:, :], in_=ident[:, :], compare_op=ALU.not_equal, fill=1.0, base=0,
                                    pattern=[[-1, P]], channel_multiplier=1)
            nc.gpsimd.affine_select(out=tri[:, :], in_=ones[:, :], compare_op=ALU.is_ge, fill=0.0, base=0,
                                    pattern=[[1, P]], channel_multiplier=-1)
            nc.gpsimd.memset(LT, 0.0)
            link(nc.gpsimd.memset(neg_pick, 0.0))
            nc.gpsimd.affine_select(out=neg_pick, in_=neg_pick, compare_op=ALU.not_equal, fill=-1.0, base=0,
                                    pattern=[[-1, H], [0, P]], channel_multiplier=1).then_inc(consts, 1)

            def inverse(request):
                pool.wait_ge(ms_ready, request + 1)
                nc.gpsimd.tensor_tensor(rstd[:, request, :], ms[:, request, :], neg_half[:, :], ALU.pow).then_inc(rstd_ready, 1)

            for L in range(DEPTH):
                if L:
                    pool.wait_ge(pv_ps, 2 * L)
                nc.gpsimd.memset(qz, 0.0).then_inc(zeros, 1)
                pool.wait_ge(wsp_landed, 16 * (L + 1))
                nc.gpsimd.affine_select(out=wsp_raw, in_=wsp_raw, compare_op=ALU.is_ge, fill=0.0, base=0,
                                        pattern=[[0, G], [-1, P]], channel_multiplier=1).then_inc(wsp_masked, 1)
                inverse(L * NR + NORM_MIX)
                for qb, S in enumerate((S0, S1)):
                    pool.wait_ge(score_sb, 2 * L + qb + 1)
                    d = S[:, :, qb * P:(qb + 1) * P]
                    nc.gpsimd.affine_select(out=d, in_=d, compare_op=ALU.is_ge, fill=MASKED, base=0,
                                            pattern=[[0, H], [-1, P]], channel_multiplier=1).then_inc(masked, 1)
                for request in (SV, ATTN, SGU, POST_MIX, NORM_FFN):
                    inverse(L * NR + request)
                if L == 0:
                    inverse(POST_FFN)
            nc.gpsimd.iota(iota, pattern=[[1, T]], base=0, channel_multiplier=0, allow_small_or_imprecise_dtypes=True)
            nc.gpsimd.affine_select(out=tri_strict, in_=ones[:, :], compare_op=ALU.is_gt, fill=0.0, base=0,
                                    pattern=[[1, P]], channel_multiplier=-1)
            nc.gpsimd.affine_select(out=before, in_=ones[:, 0:E * E].rearrange("p (a b) -> p a b", a=E), compare_op=ALU.is_gt,
                                    fill=0.0, base=0, pattern=[[1, E], [-1, E]], channel_multiplier=0).then_inc(moe_consts, 1)
            inverse(NR + POST_FFN)

        @block.vector
        def _(dve):
            links = [0]

            def link(ins):
                links[0] += 1
                ins.then_inc(dve_seq, 1)
                dve.wait_ge(dve_seq, links[0])

            V = nc.vector
            dve.wait_ge(vecT, 1)
            V.tensor_copy(vec[:, 0, 0:R0], bank(0)[:, 0:R0])
            V.tensor_copy(vec[:, 1, 0:NB], bank(0)[:, P:P + NB]).then_inc(vec_ready, 1)

            def ada_sum(key):
                n = ada_order.index(key[:4])
                h = key[4]
                if n == 0 and h == 0:
                    dve.wait_ge(c_ready, 1)
                if n >= 2 and h == 0:
                    dve.wait_ge(ada_out, n - 1)
                acc = ada_acc[:, n % 2, :]
                w = raw3(arrived(dve, key))
                for k in range(KC // 2):
                    kc = h * KC // 2 + k
                    if kc == 0 and key[:4] in gate_order:
                        m = gate_order.index(key[:4])
                        dve.wait_ge(seed_landed[m % 2], 16 * (m // 2 + 1))
                        ins = V.scalar_tensor_tensor(acc, w[:, k, :], c_act[:, 0:1], ada_seed[:, m % 2, :], ALU.mult, ALU.add)
                    elif kc == 0:
                        ins = V.tensor_scalar(acc, w[:, k, :], c_act[:, 0:1], None, ALU.mult)
                    else:
                        ins = V.scalar_tensor_tensor(acc, w[:, k, :], c_act[:, kc:kc + 1], acc, ALU.mult, ALU.add)
                    if k < KC // 2 - 1:
                        link(ins)
                ins.then_inc(raw_used, 1)
                dve.wait_ge(raw_used, raw_at[key] + 1)

            done = [0]
            finished = [0]

            def finish(n):
                while finished[0] < n:
                    ada_finish(finished[0])
                    finished[0] += 1

            def advance(*key):
                while done[0] <= raw_at[key]:
                    k = stream[done[0]]
                    if k[0] == "ada":
                        n = ada_order.index(k[:4])
                        if k[4] == 0:
                            finish(n if k[:4] in dense_ada and n % 2 == 0 else n - 1)
                        ada_sum(k)
                    else:
                        write_lo(dve, k)
                    done[0] += 1

            def ada_finish(n):
                _, layer, kind, half = ada_order[n]
                dve.wait_ge(ada_out, n + 1)
                name = KINDS[kind]
                ffn = int(name.endswith("ffn"))
                ks = half * 4
                src = bank(ada_bank(n))
                if name.startswith("gate"):
                    dve.wait_ge(row_landed[ffn], 16 * (layer + 1))
                    r = row[:, ffn, half * HALF:(half + 1) * HALF]
                    V.scalar_tensor_tensor(r, src, 1.0, r, ALU.add, ALU.mult).then_inc(ada_done, 1)
                elif name.startswith("shift"):
                    V.tensor_tensor(mod[:, layer, 2 * ffn, ks:ks + 4], src[:, 0:4], b_ada_col(layer, kind, ks, 4), ALU.add).then_inc(ada_done, 1)
                else:
                    dve.wait_ge(ada_done, n)
                    link(V.tensor_tensor(modt[:, :], src[:, 0:4], b_ada_col(layer, kind, ks, 4), ALU.add))
                    V.scalar_tensor_tensor(mod[:, layer, 2 * ffn + 1, ks:ks + 4], modt[:, :], 1.0,
                                           col("g_pre_ffn" if ffn else "g_pre_mix", layer, ks, 4), ALU.add, ALU.mult).then_inc(ada_done, 1)

            def mean_square(request, width):
                dve.wait_ge(ss_ready, 2 * (request + 1))
                V.tensor_scalar(ms[:, request, :], ss[:, request, :], 1.0 / width, EPS, ALU.mult, ALU.add).then_inc(ms_ready, 1)

            def scaled_input(n, layer, ffn):
                request = layer * NR + (NORM_FFN if ffn else NORM_MIX)
                mean_square(request, D)
                dve.wait_ge(rstd_ready, request + 1)
                for i in range(NT):
                    V.tensor_scalar(xn[:, i, :], x_sb[:, i, :], rstd[:, request, i:i + 1], None, ALU.mult).then_inc(xn_ready, 1)

            def input_parts(n, scale_bias, ps_ready):
                for b in DVE_BANKS:
                    dve.wait_ge(ps_ready[0], ps_ready[1] + b + 1)
                    for kc in (2 * b, 2 * b + 1):
                        scale, bias = scale_bias(kc)
                        l = V.tensor_scalar(hT[:, kc, :], bank(b)[:, (kc % 2) * T:(kc % 2 + 1) * T], scale, bias, ALU.mult,
                                            *(() if bias is None else (ALU.add,)))
                    l.then_inc(hTf_dve, 1)

            def input_lo(n):
                for b in range(4):
                    dve.wait_ge(hT_hi_ready, 4 * n + b + 1)
                    V.tensor_tensor(hT_lo[:, 2 * b:2 * b + 2, :], hT[:, 2 * b:2 * b + 2, :], hT_hi[:, 2 * b:2 * b + 2, :].bitcast(F32),
                                    ALU.subtract).then_inc(hT_lo_ready, 1)

            def modulation(layer, ffn):
                return lambda kc: (mod[:, layer, 2 * ffn + 1, kc:kc + 1], mod[:, layer, 2 * ffn, kc:kc + 1])

            def branch_gain(layer):
                return lambda kc: (col("g_out_attn", layer, kc) if kc < AC else col("g_out_sgu", layer, kc - AC), None)

            def gated(step, B, w):
                dve.wait_ge(sil_ready, step + 1)
                for b in range(B):
                    l = V.tensor_tensor(act_t[:, b, 0:w], sil[:, b, 0:w], bank(2 * b + 1)[:, 0:w], ALU.mult)
                l.then_inc(act_ready, 1)

            def act_lo(step, B, w, tbank, c0=0):
                dve.wait_ge(actT_hi_ready, step + 1)
                for b in range(B):
                    l = V.tensor_tensor(actT_lo[:, 0:w // P, c0 + b * P:c0 + (b + 1) * P], bank(tbank(b))[:, 0:w].rearrange("p (t n) -> p t n", n=P),
                                        actT_hi[:, 0:w // P, c0 + b * P:c0 + (b + 1) * P].bitcast(F32), ALU.subtract)
                l.then_inc(actT_lo_ready, 1)

            def post(request, which, ys, tmp_, n):
                mean_square(request, D)
                dve.wait_ge(rstd_ready, request + 1)
                for i in range(NT):
                    link(V.scalar_tensor_tensor(tmp_[:, i, :], ys[i], rstd[:, request, i:i + 1], row[:, which, :], ALU.mult, ALU.mult))
                    V.tensor_tensor(x_sb[:, i, :], x_sb[:, i, :], tmp_[:, i, :], ALU.add).then_inc(x_new, 1)

            for L in range(DEPTH):
                if L == 0:
                    advance(*ada(0, "shift_mix")[1], 0)
                scaled_input(2 * L, L, 0)
                if L == 0:
                    advance(*ada(0, "scale_mix")[1], 1)
                    finish(4)
                dve.wait_ge(ada_done, 4 if L == 0 else len(ada_order) - 2)
                input_parts(3 * L, modulation(L, 0), (xT_ready, 8 * L))
                for n in range(2):
                    dve.wait_ge(wT_ps, 2 * L + n + 1)
                    V.tensor_copy(wT[:, 4 * n:4 * n + 4, :], bank(6 + n).rearrange("p (a t) -> p a t", t=P)).then_inc(wT_ready, 1)
                input_lo(3 * L)
                advance("in", L, "v", 0)
                mixer_chunks = [ada_order.index(k) for k in mixer_ada[L].values()]
                finish(mixer_chunks[0] + 1)
                dve.wait_ge(f_ps, L + 1)
                dve.wait_ge(small_landed, 16 * (3 + 2 * L))
                link(V.tensor_tensor(fz[:, 0, :].rearrange("p (i h) -> p i h", i=NT), bank(0)[:, 0:NT * H].rearrange("p (i h) -> p i h", i=NT),
                                     b_f[:, :].unsqueeze(1).to_broadcast([P, NT, H]), ALU.add))
                V.tensor_scalar(fz[:, 2, :], fz[:, 0, :], 0.0, None, ALU.min)
                V.scalar_tensor_tensor(fz[:, 1, :], fz[:, 0, :], -1.0, fz[:, 0, :], ALU.mult, ALU.min).then_inc(z_ready, 1)
                finish(mixer_chunks[1] + 1)
                advance("in", L, "v", 1)
                dve.wait_ge(lnz_ready, L + 1)
                V.tensor_tensor(logf[:, :, :].rearrange("p i h -> p (i h)"), fz[:, 2, :], fz[:, 3, :], ALU.subtract).then_inc(logf_ready, 1)
                dve.wait_ge(L_ps, L + 1)
                dve.wait_ge(consts, 1)
                V.tensor_copy(LT[0:H, :], bank(1)[0:H, 0:T])
                V.tensor_copy(Lq[:, :, :].rearrange("p i h -> p (i h)"), bank(1)[:, T:T + NT * H]).then_inc(L_ready, 1)
                advance("in", L, "u", 0)
                products_done(dve, ("in", L, "v", 1))
                for i in range(NT):
                    V.tensor_copy(v_sb[:, i, :], bank(2 + i)).then_inc(v_ready, 1)
                advance("in", L, "s", 0)
                dve.wait_ge(L_ready, L + 1)
                dve.wait_ge(score_ps, 2 * L + 1)
                V.tensor_tensor(S0, bank(4, 2).rearrange("p (h k) -> p h k", h=H), Lq[:, 0, :].unsqueeze(2).to_broadcast([P, H, P]), ALU.add).then_inc(score_sb, 1)
                dve.wait_ge(score_ps, 2 * L + 2)
                V.tensor_tensor(S1, bank(0, 4).rearrange("p (h k) -> p h k", h=H), Lq[:, 1, :].unsqueeze(2).to_broadcast([P, H, T]), ALU.add).then_inc(score_sb, 1)
                for qb, S in enumerate((S0, S1)):
                    dve.wait_ge(masked, 2 * L + qb + 1)
                    V.tensor_reduce(nmax[:, qb, :], S, AX_X, ALU.max, negate=True).then_inc(max_ready, 1)
                advance("in", L, "s", 1)
                finish(mixer_chunks[-1] + 1)
                dve.wait_ge(exp_ready, 2 * L + 2)
                link(V.reciprocal(rsums[:, :, :], psums[:, :, :]))
                for n in range(1, 6, 2):
                    dve.wait_ge(PT_ps, 6 * L + n + 1)
                    b = (0, 1, 2, 3, 6, 7)[n]
                    V.tensor_copy(PT[:, 4 * n:4 * n + 4, :], bank(b).rearrange("p (a t) -> p a t", t=P)).then_inc(PT_dve, 1)
                dve.wait_ge(gelu_ready, 4 * L + 4)
                V.tensor_scalar(nmean[:, :], ssum[:, :], -1.0 / AW, None, ALU.mult).then_inc(mean_ready, 1)
                mean_square(L * NR + SV, AW)
                dve.wait_ge(rstd_ready, L * NR + SV + 1)
                dve.wait_ge(g_v_landed, 16 * (L + 1))
                for i in range(NT):
                    link(V.tensor_scalar(s_sb[:, i, :], s_sb[:, i, :], nmean[:, i:i + 1], rstd[:, L * NR + SV, i:i + 1], ALU.add, ALU.mult))
                    V.tensor_tensor(s_sb[:, i, :], s_sb[:, i, :], g_v_sb, ALU.mult).then_inc(s_ready, 1)
                for i in range(NT):
                    dve.wait_ge(pv_ps, 2 * L + i + 1)
                    V.tensor_tensor(attn[:, i, :].rearrange("p (h d) -> p h d", h=H), bank(4 + i).rearrange("p (h d) -> p h d", h=H),
                                    rsums[:, i, :].unsqueeze(2).to_broadcast([P, H, DH]), ALU.mult).then_inc(attn_raw, 1)
                for i in range(NT):
                    dve.wait_ge(mix_ps, 2 * L + i + 1)
                    link(V.tensor_tensor(sgu[:, i, :].rearrange("p (g d) -> p g d", g=G), bank(6 + i).rearrange("p (g d) -> p g d", g=G),
                                         col("b_spatial", L, 0, G).unsqueeze(2).to_broadcast([P, G, DH]), ALU.add))
                    V.tensor_tensor(sgu[:, i, :], sgu[:, i, :], u_sb[:, i, :], ALU.mult).then_inc(sgu_raw, 1)
                mean_square(L * NR + ATTN, AW)
                advance("out", L, 0, 0)
                dve.wait_ge(rstd_ready, L * NR + ATTN + 1)
                for i in range(NT):
                    V.tensor_scalar(attn[:, i, :], attn[:, i, :], rstd[:, L * NR + ATTN, i:i + 1], None, ALU.mult).then_inc(attn_ready, 1)
                mean_square(L * NR + SGU, AW)
                dve.wait_ge(rstd_ready, L * NR + SGU + 1)
                for i in range(NT):
                    V.tensor_scalar(sgu[:, i, :], sgu[:, i, :], rstd[:, L * NR + SGU, i:i + 1], None, ALU.mult).then_inc(sgu_ready, 1)
                input_parts(3 * L + 1, branch_gain(L), (mT_ps, 4 * L))
                input_lo(3 * L + 1)
                advance("out", L, 1, 1)
                if L == 0:
                    finish(10)
                    advance("ffn", "gate", 0, 1)
                post(L * NR + POST_MIX, 0, [bank(4 + 2 * i, 2) for i in range(NT)], tmp, 2 * L)
                scaled_input(2 * L + 1, L, 1)
                if L == 1:
                    dve.wait_ge(ada_done, len(ada_order))
                input_parts(3 * L + 2, modulation(L, 1), (xT_ready, 8 * L + 4))
                input_lo(3 * L + 2)
                if L == 0:
                    order = ffn_order(SD, lambda s: dense_tiles(s) // 2)
                    for j, (kind, s, h) in enumerate(order):
                        advance("ffn", kind, s, h)
                        for kind, s, h in ((order[j - STAGED + 1],) if j >= STAGED - 1 else ()) if j < len(order) - 1 else order[j - STAGED + 1:]:
                            w = P * dense_tiles(s)
                            if kind == "up" and h == 1:
                                gated(s, NT, w)
                                if s == 0:
                                    act_lo(s, NT, w, lambda b: 2 * b + 1)
                            if kind == "down" and h == 0 and s < SD - 1:
                                finish(10 + 2 * (s + 2))
                            if kind == "down" and h == dense_tiles(s) // 2 - 1 and s < SD - 1:
                                act_lo(s + 1, NT, P * dense_tiles(s + 1), lambda b: 2 * b + 1)
                    finish(22)
                    advance("in", 1, "q", 1)
                    post(POST_FFN, 1, [bank(4 + 2 * i, 2) for i in range(NT)], tmp, 1)

            dve.wait_ge(htok_ps, 2)
            V.tensor_copy(htok[:, 1, :], bank(2, 2)).then_inc(htok_dve, 1)
            dve.wait_ge(logit_ps, 1)
            link(V.tensor_copy(lg[:, :, :].rearrange("p i e -> p (i e)"), bank(4)[:, 0:NT * E]))
            V.tensor_reduce(lmax[:, :], lg[:, :, :], AX_X, ALU.max, negate=True).then_inc(lmax_ready, 1)
            other = lg[:, :, :].unsqueeze(2).to_broadcast([P, NT, E, E])
            own = lg[:, :, :].unsqueeze(3).to_broadcast([P, NT, E, E])
            V.tensor_tensor(cmp1, other, own, ALU.is_gt)
            link(V.tensor_tensor(cmp2, other, own, ALU.is_equal))
            dve.wait_ge(moe_consts, 1)
            for i in range(NT):
                l = V.tensor_tensor(cmp2[:, i], cmp2[:, i], before, ALU.mult)
            link(l)
            link(V.tensor_tensor(cmp1, cmp1, cmp2, ALU.add))
            link(V.tensor_reduce(rank[:, :, :], cmp1, AX_X, ALU.add))
            V.tensor_scalar(sel[:, :, :], rank[:, :, :], 2.0, None, ALU.is_lt).then_inc(sel_ready, 1)
            dve.wait_ge(sel_ready, 1)
            dve.wait_ge(gexp_ready, 1)
            link(V.tensor_tensor(gate[:, :, 0:E], gate[:, :, 0:E], sel[:, :, :], ALU.mult))
            link(V.tensor_reduce(gden[:, :], gate[:, :, 0:E], AX_X, ALU.add))
            link(V.reciprocal(gden[:, :], gden[:, :]))
            for i in range(NT):
                V.tensor_scalar(gate[:, i, 0:E], gate[:, i, 0:E], gden[:, i:i + 1], None, ALU.mult)
            dve.wait_ge(pos_ps, 1)
            V.memset(posm[:, :, E:E + 1], -1.0)
            V.memset(gate[:, :, E:E + 1], 0.0)
            link(V.scalar_tensor_tensor(posm[:, :, 0:E], bank(4)[:, 0:NT * E].rearrange("p (i e) -> p i e", i=NT), 1.0, sel[:, :, :], ALU.add, ALU.mult))
            V.tensor_scalar(posm[:, :, 0:E], posm[:, :, 0:E], -1.0, None, ALU.add)
            V.tensor_scalar(wide[:, :], bank(4)[0:1, NT * E:NT * E + E], float(P), None, ALU.is_gt).then_inc(route_ready, 1)
            for i in range(NT):
                V.memset(yacc[:, i, :], 0.0).then_inc(yacc_done, 1)

            def pick_slots(dst, e, gated_, ready):
                for i in range(NT):
                    if gated_:
                        l = V.tensor_scalar(dst[:, i, :], iota, posm[:, i, bass.ds(e, 1)], gate[:, i, bass.ds(e, 1)], ALU.is_equal, ALU.mult)
                    else:
                        l = V.tensor_scalar(dst[:, i, :], iota, posm[:, i, bass.ds(e, 1)], None, ALU.is_equal)
                l.then_inc(ready, 1)

            def gathered_lo(e, first):
                for b in range(2):
                    dve.wait_ge(hT_hi_ready, GATHERED + 2 * e + b + 1)
                    V.tensor_tensor(slots(hT_lo, b, 0), bank(first + b).rearrange("p (k t) -> p k t", t=P),
                                    slots(hT_hi, b, 0).bitcast(F32), ALU.subtract).then_inc(hT_lo_ready, 1)

            def expert(e, B, last):
                order, step0 = expert_order, SD + e * SE
                if B == 2:
                    dve.wait_ge(second_hi, e + 1)
                    for b in range(2):
                        l = V.tensor_tensor(slots(hT_lo, b, 1), bank(2 + b).rearrange("p (k t) -> p k t", t=P),
                                            slots(hT_hi, b, 1).bitcast(F32), ALU.subtract)
                    l.then_inc(second_lo, 1)
                else:
                    V.nop().then_inc(second_lo, 1)
                for j, (kind, s, h) in enumerate(order):
                    if j >= AHEAD:
                        write_lo(dve, ("exp", e, kind, s, h))
                    if j == 3:
                        pick_slots(pickg, e, True, pickg_ready)
                    if j == 6:
                        dve.wait_ge(pickgT_ps, e + 1)
                        V.tensor_copy(pickgT, bank(7).rearrange("p (b t) -> p b t", b=NT)).then_inc(pickgT_ready, 1)
                        pick_slots(pick, e + 1, False, pick_ready)
                    for kind, s, h in ((order[j - STAGED + 1],) if j >= STAGED - 1 else ()) if j < PE_ - 1 else order[j - STAGED + 1:]:
                        if kind == "up" and h == 1:
                            gated(step0 + s, B, HALF)
                            if s == 0 and B == 2:
                                act_lo(step0 + s, B, HALF, lambda b: 2 * b + 1)
                            if s == SE - 1 and B == 1:
                                gathered_lo(e + 1, 6)
                        if B == 1 and kind == "gate" and s == 1 and h == 1:
                            act_lo(step0, B, HALF, lambda b: 2)
                        if kind == "down" and s < SE - 1 and h == B - 1:
                            act_lo(step0 + s + 1, B, HALF, (lambda b: 2) if B == 1 else (lambda b: 2 * b + 1), act_column(B, s + 1))
                if not last:
                    write_lo(dve, ("exp", e + 1) + order[0])
                products_done(dve, ("exp", e, "down", SE - 1, 1))
                for b in range(B):
                    l = V.tensor_copy(ye[:, b, HALF:D], bank(5 + 2 * b))
                l.then_inc(ye_dve, 1)
                if B == 2:
                    gathered_lo(e + 1, 0)
                if not last:
                    for key in order[1:AHEAD]:
                        write_lo(dve, ("exp", e + 1) + key)
                for i in range(NT):
                    dve.wait_ge(scat_ps, e * NT + i + 1)
                    dve.wait_ge(yacc_done, e * NT + i + 1)
                    V.tensor_tensor(yacc[:, i, :], yacc[:, i, :], bank((6, 4)[i], 2), ALU.add).then_inc(yacc_done, 1)

            def routed(e, last):
                size = dve.value_load(wide[0:1, bass.ds(e, 1)], min_val=0, max_val=1)
                with dve.If(size == 0):
                    expert(e, 1, last)
                with dve.Else():
                    expert(e, 2, last)

            dve.wait_ge(route_ready, 1)
            pick_slots(pick, 0, False, pick_ready)
            gathered_lo(0, 6)
            for key in expert_order[:AHEAD]:
                write_lo(dve, ("exp", 0) + key)
            with dve.Fori(0, E - 1) as e:
                routed(e, False)
            routed(E - 1, True)
            post(NR + POST_FFN, 1, [yacc[:, i, :] for i in range(NT)], tmp_e, 3)

        @block.tensor
        def _(pe):
            mm = nc.tensor.matmul

            pe.wait_ge(consts, 1)
            pe.wait_ge(vec_landed, 16 * (len(rows0) + 1))
            for a, n in enumerate((R0, NB)):
                l = nc.tensor.transpose(bank(0)[:, a * P:a * P + n], vec_raw[0:n, a, :], ident[0:n, 0:n])
            l.then_inc(vecT, 1)
            nada = [0]

            def ada_reduce():
                n = nada[0]
                nada[0] += 1
                pe.wait_ge(raw_used, raw_at[ada_order[n] + (1,)] + 1)
                if n >= 2:
                    pe.wait_ge(ada_done, n - 1)
                acc = ada_acc[:, n % 2, :]
                dst = bank(ada_bank(n))
                if ada_order[n] in gate_order:
                    mm(dst, ones[:, :], acc, start=True, stop=True).then_inc(ada_out, 1)
                else:
                    for j in range(4):
                        l = mm(dst[:, j:j + 1], acc[:, j * P:(j + 1) * P], ones[:, 0:1], start=True, stop=True)
                    l.then_inc(ada_out, 1)

            def input_transposed(n):
                for kc in range(KC):
                    for i in range(NT):
                        if kc == 0:
                            pe.wait_ge(xn_ready, NT * n + i + 1)
                        l = nc.tensor.transpose(bank(kc // 2)[:, (kc % 2) * T + i * P:(kc % 2) * T + (i + 1) * P],
                                                xn[:, i, kc * P:(kc + 1) * P], ident[:, :])
                    if kc % 2:
                        l.then_inc(xT_ready, 1)

            def input_ready(n, b=3):
                pe.wait_ge(hT_lo_ready, 4 * n + b + 1)

            def product(dst, stationary, moving, first, last, start=None):
                s_hi, s_lo = stationary
                m_hi, m_lo = moving
                start = first if start is None else start
                mm(dst, s_hi, m_hi, start=start, stop=False, skip_group_check=True)
                mm(dst, s_hi, m_lo, start=False, stop=False, skip_group_check=True)
                return mm(dst, s_lo, m_hi, start=False, stop=last, skip_group_check=True)

            def tokens(k, i):
                return hT_hi[:, k, i * P:(i + 1) * P], hT_lo[:, k, i * P:(i + 1) * P]

            def moving_weights(key, dst_of, B, ready=None):
                h = key[-1]
                hi, lo = staged(pe, key)
                for k in range(KC // 2):
                    kc = h * KC // 2 + k
                    if ready is not None and k % 2 == 0:
                        pe.wait_ge(hT_lo_ready, ready(kc))
                    for b in range(B):
                        l = product(dst_of(b), tokens(kc, b), (hi[:, k, :], lo[:, k, :]), kc == 0, kc == KC - 1)
                l.then_inc(used, 1)

            def ffn_piece(key, B, s_first, s_last, ready=None, w=HALF):
                kind, s, h = key[-3:]
                if kind == "down":
                    hi, lo = staged(pe, key)
                    c0 = act_column(B, s)
                    for b in range(B):
                        for t in range(2):
                            tt = 2 * h + t
                            for half in range(2):
                                cols = slice(half * HALF, (half + 1) * HALF)
                                l = product(bank(4 + 2 * b + half), (actT_hi[:, tt, c0 + b * P:c0 + (b + 1) * P], actT_lo[:, tt, c0 + b * P:c0 + (b + 1) * P]),
                                            (hi[:, t, cols], lo[:, t, cols]), s_first and tt == 0, s_last(tt))
                    l.then_inc(used, 1)
                else:
                    u = int(kind == "up")
                    moving_weights(key, lambda b: bank(2 * b + u)[:, 0:w], B, ready)

            def act_transposed(step, B, tiles, tbank):
                pe.wait_ge(act_ready, step + 1)
                for b in range(B):
                    for t in range(tiles):
                        l = nc.tensor.transpose(bank(tbank(b))[:, t * P:(t + 1) * P], act_t[:, b, t * P:(t + 1) * P], ident[:, :])
                l.then_inc(T_ps, 1)

            for L in range(DEPTH):
                if L:
                    pe.wait_ge(x_new, NT * 2)
                    pe.wait_ge(ada_done, nada[0])
                pe.wait_ge(wsp_masked, L + 1)
                for g in range(G):
                    l = nc.tensor.transpose(bank(6 + g // 4)[:, (g % 4) * P:(g % 4 + 1) * P], wsp_raw[:, g, :], ident[:, :])
                    if g % 4 == 3:
                        l.then_inc(wT_ps, 1)
                pe.wait_ge(vec_ready, 1)
                input_transposed(2 * L)
                if L == 0:
                    for _ in range(4):
                        ada_reduce()
                for j, name in enumerate("qk"):
                    for h in range(2):
                        hi, lo = staged(pe, ("in", L, name, h))
                        for k in range(KC // 2):
                            kc = h * KC // 2 + k
                            if j == 0 and k % 2 == 0:
                                input_ready(3 * L, kc // 2)
                            if j == 1 and kc == 0:
                                pe.wait_ge(wT_ready, 2 * L + 2)
                            for m in range(AC):
                                cols = slice(m * P, (m + 1) * P)
                                l = product(bank(4 + 2 * j + m // 2)[:, (m % 2) * T:(m % 2 + 1) * T], (hi[:, k, cols], lo[:, k, cols]),
                                            (hT_hi[:, kc, :], hT_lo[:, kc, :]), kc == 0, kc == KC - 1, start=(kc == 0 and m % 2 == 0))
                        l.then_inc(used, 1)
                        if j == 1:
                            ada_reduce()
                pe.wait_ge(small_landed, 16 * (3 + 2 * L))
                for i in range(NT):
                    for k in range(KC):
                        l = mm(bank(0)[:, i * H:(i + 1) * H], hT[:, k, i * P:(i + 1) * P], w_f[:, k, :], start=(k == 0), stop=(k == KC - 1))
                l.then_inc(f_ps, 1)

                def project(name, first):
                    for h in range(2):
                        moving_weights(("in", L, name, h), lambda b: bank(first + b), NT)

                pe.wait_ge(ada_done, nada[0] - 1)
                project("v", 2)
                pe.wait_ge(logf_ready, L + 1)
                pe.wait_ge(ada_done, nada[0])
                dst = bank(1)[0:H, 0:P]
                mm(dst, logf[:, 0, :], tri[:, :], start=True, stop=True)
                dst = bank(1)[0:H, P:T]
                mm(dst, logf[:, 0, :], ones[:, :], start=True, stop=False)
                mm(dst, logf[:, 1, :], tri[:, :], start=False, stop=True)
                mm(bank(1)[:, T:T + H], tri[:, :], logf[:, 0, :], start=True, stop=True)
                mm(bank(1)[:, T + H:T + 2 * H], ones[:, :], logf[:, 0, :], start=True, stop=False)
                mm(bank(1)[:, T + H:T + 2 * H], tri[:, :], logf[:, 1, :], start=False, stop=True).then_inc(L_ps, 1)
                pe.wait_ge(qk_ready, L + 1)
                pe.wait_ge(k_ready, L + 1)
                pe.wait_ge(L_ready, L + 1)
                for qb in range(NT):
                    nk = (qb + 1) * P
                    if qb:
                        pe.wait_ge(v_ready, 2 * (L + 1))
                    for h in range(H):
                        dst = bank(4, 2)[:, h * P:(h + 1) * P] if qb == 0 else bank(0, 4)[:, h * T:(h + 1) * T]
                        mm(dst, qz[:, h, qb * P:(qb + 1) * P], kT[:, h // 2, 0:nk], start=True, stop=False)
                        l = mm(dst, neg_pick[:, h, :], LT[:, 0:nk], start=False, stop=True)
                    l.then_inc(score_ps, 1)
                project("u", 6)
                if L == 0:
                    pe.wait_ge(score_sb, 2 * L + 2)
                    for _ in range(2):
                        ada_reduce()
                pe.wait_ge(score_sb, 2 * L + 1)
                project("s", 4)
                pe.wait_ge(score_sb, 2 * L + 2)
                pe.wait_ge(ada_done, nada[0])
                pe.wait_ge(exp_ready, 2 * L + 2)
                for b in range(24):
                    n = b // 4
                    if b == 16:
                        pe.wait_ge(gelu_ready, 4 * L + 2)
                    src = S1[:, b // 2, (b % 2) * P:(b % 2 + 1) * P] if b < 16 else S0[:, b - 16, :]
                    l = nc.tensor.transpose(bank((0, 1, 2, 3, 6, 7)[n])[:, (b % 4) * P:(b % 4 + 1) * P], src, ident[:, :])
                    if b % 4 == 3:
                        l.then_inc(PT_ps, 1)
                pe.wait_ge(gelu_ready, 4 * L + 4)
                pe.wait_ge(PT_act, 3 * (L + 1))
                pe.wait_ge(PT_dve, 3 * (L + 1))
                for qb in range(NT):
                    for h in range(H):
                        dst = bank(4 + qb)[:, h * DH:(h + 1) * DH]
                        for kb in range(qb + 1):
                            l = mm(dst, PT[:, 2 * h + kb if qb else 16 + h, :], v_sb[:, kb, h * DH:(h + 1) * DH], start=(kb == 0), stop=(kb == qb))
                    l.then_inc(pv_ps, 1)
                for i in range(NT):
                    pe.wait_ge(s_ready, 2 * L + i + 1)
                    for g in range(G):
                        l = mm(bank(6 + i)[:, g * DH:(g + 1) * DH], wT[:, g, :], s_sb[:, i, g * DH:(g + 1) * DH], start=True, stop=True)
                    l.then_inc(mix_ps, 1)
                for branch, (src, ready) in enumerate(((attn, attn_ready), (sgu, sgu_ready))):
                    pe.wait_ge(ready, 2 * (L + 1))
                    for kc in range(AC):
                        for i in range(NT):
                            l = nc.tensor.transpose(bank(2 * branch + kc // 2)[:, (kc % 2) * T + i * P:(kc % 2) * T + (i + 1) * P],
                                                    src[:, i, kc * P:(kc + 1) * P], ident[:, :])
                        if kc % 2:
                            l.then_inc(mT_ps, 1)
                for half in range(2):
                    for h in range(2):
                        moving_weights(("out", L, half, h), lambda b: bank(4 + 2 * b + half), NT, (lambda kc: 4 * (3 * L + 1) + kc // 2 + 1) if half == 0 else None)
                        if L == 0 and half != h:
                            ada_reduce()
                if L == 0:
                    pe.wait_ge(ada_done, nada[0])
                input_transposed(2 * L + 1)
                if L == 0:
                    pe.wait_ge(x_new, NT)
                    for kind, s, h in ffn_order(SD, lambda s: dense_tiles(s) // 2):
                        tiles = dense_tiles(s)
                        if kind == "down" and h == 0:
                            pe.wait_ge(actT_lo_ready, s + 1)
                        if kind == "gate" and h == 0:
                            pe.wait_ge(hT_lo_ready, 12)
                        if s and kind == "gate" and h == 0:
                            pe.wait_ge(sil_ready, s)
                            pe.wait_ge(ada_done, nada[0])
                        if s and kind == "up" and h == 0:
                            pe.wait_ge(actT_lo_ready, s)
                            pe.wait_ge(ada_done, nada[0])
                        ffn_piece(("ffn", kind, s, h), NT, s == 0, lambda tt: s == SD - 1 and tt == tiles - 1, w=tiles * P)
                        if s == 0 and kind == "up" and h == 1:
                            act_transposed(0, NT, tiles, lambda b: 2 * b + 1)
                        if kind == "down" and h == tiles // 2 - 1 and s < SD - 1:
                            act_transposed(s + 1, NT, dense_tiles(s + 1), lambda b: 2 * b + 1)
                        if s == 1 and kind == "gate" and h == 0:
                            pe.wait_ge(actT_lo_ready, s)
                            for _ in range(2):
                                ada_reduce()
                        if kind == "down" and h == 0 and s < SD - 1:
                            pe.wait_ge(sil_ready, s + 2)
                            for _ in range(2):
                                ada_reduce()

            input_ready(5)
            pe.wait_ge(hTf_act, 12)
            pe.wait_ge(hTf_dve, 12)
            for i in range(NT):
                for k in range(KC):
                    l = nc.tensor.transpose(bank(2 * i, 2)[:, k * P:(k + 1) * P], hT[:, k, i * P:(i + 1) * P], ident[:, :])
                l.then_inc(htok_ps, 1)
            pe.wait_ge(x_new, NT * 3)
            for i in range(NT):
                for k in range(KC):
                    l = mm(bank(4)[:, i * E:(i + 1) * E], hT[:, k, i * P:(i + 1) * P], w_r[:, k, :], start=(k == 0), stop=(k == KC - 1))
            l.then_inc(logit_ps, 1)
            pe.wait_ge(sel_ready, 1)
            pe.wait_ge(moe_consts, 1)
            mm(bank(4)[:, 0:E], tri_strict, sel[:, 0, :], start=True, stop=True)
            mm(bank(4)[:, E:2 * E], ones[:, :], sel[:, 0, :], start=True, stop=False)
            mm(bank(4)[:, E:2 * E], tri_strict, sel[:, 1, :], start=False, stop=True)
            mm(bank(4)[:, 2 * E:3 * E], ones[:, :], sel[:, 0, :], start=True, stop=False)
            mm(bank(4)[:, 2 * E:3 * E], ones[:, :], sel[:, 1, :], start=False, stop=True).then_inc(pos_ps, 1)
            pe.wait_ge(route_ready, 1)
            pe.wait_ge(htok_act, 1)
            pe.wait_ge(htok_dve, 1)

            def gather(block, first):
                for k in range(KC):
                    for i in range(NT):
                        l = mm(bank(first + k // 4)[:, (k % 4) * P:(k % 4 + 1) * P], htok[:, i, k * P:(k + 1) * P],
                               pick[:, i, block * P:(block + 1) * P], start=(i == 0), stop=(i == NT - 1))
                return l

            def expert(e, B):
                step0 = SD + e * SE
                tbank = (lambda b: 2) if B == 1 else (lambda b: 2 * b + 1)
                if B == 2:
                    pe.wait_ge(actT_lo_ready, step0)
                    gather(1, 2).then_inc(second_ps, 1)
                    pe.wait_ge(second_lo, e + 1)
                else:
                    nc.tensor.nop().then_inc(second_ps, 1)
                for kind, s, h in expert_order:
                    if kind == "down" and h == 0:
                        pe.wait_ge(actT_lo_ready, step0 + s + 1)
                        if s == 0:
                            pe.wait_ge(pickgT_ready, e + 1)
                    if kind == "gate" and s and h == 0:
                        pe.wait_ge(sil_ready, step0 + s)
                    if kind == "up" and s and h == 0:
                        pe.wait_ge(act_ready, step0 + s)
                        if B == 2:
                            pe.wait_ge(actT_lo_ready, step0 + s)
                    ffn_piece(("exp", e, kind, s, h), B, s == 0, lambda tt: s == SE - 1 and tt == TPC - 1,
                              ready=(lambda kc: GATHERED + 2 * e + kc // 4 + 1) if kind == "gate" and s == 0 else None)
                    if B == 1 and s == SE - 1 and kind == "up" and h == 1:
                        pe.wait_ge(pick_ready, e + 2)
                        gather(0, 6).then_inc(gath_ps, 1)
                    if s == 0 and h == 1 and kind == ("gate" if B == 2 else "up"):
                        pe.wait_ge(pickg_ready, e + 1)
                        pe.wait_ge(yacc_done, (e + 1) * NT)
                        for b in range(NT):
                            for i in range(NT):
                                l = nc.tensor.transpose(bank(7)[:, b * T + i * P:b * T + (i + 1) * P], pickg[:, i, b * P:(b + 1) * P], ident[:, :])
                        l.then_inc(pickgT_ps, 1)
                    if (B == 2 and s == 0 and kind == "up" and h == 1) or (B == 1 and s == 1 and kind == "gate" and h == 1):
                        act_transposed(step0, B, TPC, tbank)
                    if kind == "down" and s < SE - 1 and h == B - 1:
                        act_transposed(step0 + s + 1, B, TPC, tbank)
                if B == 2:
                    pe.wait_ge(pick_ready, e + 2)
                    gather(0, 0).then_inc(gath_ps, 1)
                pe.wait_ge(ye_act, e + 1)
                pe.wait_ge(ye_dve, e + 1)
                pe.wait_ge(pickgT_ready, e + 1)
                for i in range(NT):
                    for half in range(2):
                        for b in range(B):
                            l = mm(bank((6, 4)[i] + half), pickgT[:, b, i * P:(i + 1) * P], ye[:, b, half * HALF:(half + 1) * HALF],
                                   start=(b == 0), stop=(b == B - 1))
                    l.then_inc(scat_ps, 1)

            pe.wait_ge(pick_ready, 1)
            gather(0, 6).then_inc(gath_ps, 1)
            with pe.Fori(0, E) as e:
                size = pe.value_load(wide[0:1, bass.ds(e, 1)], min_val=0, max_val=1)
                with pe.If(size == 0):
                    expert(e, 1)
                with pe.Else():
                    expert(e, 2)


_INS = ["x", "c", "w_ada", "b_ada", "g_pre_mix", "g_post_mix", "g_pre_ffn", "g_post_ffn", "w_in", "b_forget", "g_v",
        "w_spatial", "b_spatial", "g_out_attn", "g_out_sgu", "w_out", "w_gate_up_dense", "w_down_dense", "w_router",
        "w_gate_up_exp", "w_down_exp"]


def kernel(**inputs):
    import numpy as _np
    import concourse.bacc as _bacc
    from concourse import mybir as _mybir
    from concourse.bass_utils import run_bass_kernel_spmd as _run

    nc = _bacc.Bacc("TRN2", target_bir_lowering=False, num_devices=1)
    arrays, args = {}, []
    for name in _INS:
        a = _np.ascontiguousarray(inputs[name])
        arrays[f"in_{name}_dram"] = a
        args.append(nc.dram_tensor(f"in_{name}_dram", a.shape, _mybir.dt.from_np(a.dtype), kind="ExternalInput").ap())
    o = nc.dram_tensor("out_0_dram", inputs["x"].shape, _mybir.dt.float32, kind="ExternalOutput").ap()
    hybrid_fox_sgu_moe(nc, *args, o)
    r = _run(nc, [arrays], core_ids=[0])
    return r.results[0]["out_0_dram"]
```

```python
from contextlib import ExitStack

import concourse.bass as bass
from concourse import mybir

F32 = mybir.dt.float32
F32R = mybir.dt.float32r
BF16 = mybir.dt.bfloat16
I32 = mybir.dt.int32
ALU = mybir.AluOpType
ACT = mybir.ActivationFunctionType
AX_X = mybir.AxisListType.X

P = 128
RAW = 6
STAGED = 3
AHEAD = STAGED
PIECE = 2048
EPS = 1e-6
MASKED = -1e38
KINDS = ("shift_mix", "scale_mix", "gate_mix", "shift_ffn", "scale_ffn", "gate_ffn")


def ada(layer, *names):
    return [("ada", layer, KINDS.index(n), half) for n in names for half in range(2)]


def ffn_order(steps, down_pieces):
    order = []
    for s in range(steps + 1):
        if s < steps:
            order += [(kind, s, h) for kind in ("gate", "up") for h in range(2)]
        if s:
            order += [("down", s - 1, h) for h in range(down_pieces(s - 1))]
    return order


def hybrid_fox_sgu_moe(nc, x, c, w_ada, b_ada, g_pre_mix, g_post_mix, g_pre_ffn, g_post_ffn,
                       w_in, b_forget, g_v, w_spatial, b_spatial, g_out_attn, g_out_sgu, w_out,
                       w_gate_up_dense, w_down_dense, w_router, w_gate_up_exp, w_down_exp, out):
    _, T, D = x.shape
    DEPTH = w_ada.shape[0]
    AW = g_out_attn.shape[1]
    H = b_forget.shape[1]
    G = w_spatial.shape[1]
    DH = AW // H
    FD = w_down_dense.shape[1]
    E = w_router.shape[2]
    FE = w_down_exp.shape[2]
    KC = D // P
    NT = T // P
    AC = AW // P
    HALF = 512
    TPC = HALF // P
    DT = FD // P
    SE = FE // HALF
    SD = -(-DT // TPC)
    QSCALE = float(DH) ** -0.5
    assert KC * HALF == 2 * PIECE and DEPTH == 2 and T == 2 * P and D == 1024 and FE % HALF == 0

    def dense_tiles(s):
        return min(TPC, DT - s * TPC)

    stream = []

    def put(*chunks):
        for key in chunks:
            stream.extend(key + (h,) for h in range(2))

    put(*ada(0, "shift_mix", "scale_mix"))
    mixer_ada = (dict(zip("qkvu", ada(0, "gate_mix", "shift_ffn"))), dict(zip("qkvu", ada(1, "gate_ffn", "scale_ffn"))))
    out_ada = ada(0, "scale_ffn")
    dense_ada = ada(0, "gate_ffn") + ada(1, "shift_mix", "scale_mix", "gate_mix", "shift_ffn")
    assert len(dense_ada) == 2 * (SD - 1)
    for layer in range(DEPTH):
        for name in ("q", "k", "v", "u", "s"):
            put(("in", layer, name))
            if name in mixer_ada[layer]:
                put(mixer_ada[layer][name])
        if layer == 0:
            put(out_ada[0])
        for half in range(2):
            for h in range(2):
                stream.append(("out", layer, half, h))
                if (layer, half, h) == (0, 0, 1):
                    put(out_ada[1])
        if layer == 0:
            for kind, s, h in ffn_order(SD, lambda s: dense_tiles(s) // 2):
                stream.append(("ffn", kind, s, h))
                if h == 1 and kind != "down" and s < SD - 1:
                    put(dense_ada[2 * s + (kind == "up")])
    raw_at = {key: n for n, key in enumerate(stream)}
    staged_at = {key: m for m, key in enumerate(k for k in stream if k[0] != "ada")}
    staged_keys = list(staged_at)
    ada_order = [k[:4] for k in stream if k[0] == "ada" and k[4] == 0]
    gate_order = [k for k in ada_order if KINDS[k[2]].startswith("gate")]
    expert_order = ffn_order(SE, lambda s: 2)
    expert_at = {k: j for j, k in enumerate(expert_order)}
    MIX_DONE = 4
    FFN_DONE = MIX_DONE + len(mixer_ada[0]) + len(out_ada)
    DENSE_DONE = FFN_DONE + len(dense_ada)

    def gate_done(m):
        return ada_order.index(gate_order[m]) + 1

    N0, M0, PE_ = len(stream), len(staged_at), len(expert_order)
    GATHERED = (3 * DEPTH - 1) * KC // 2
    assert PE_ % RAW == 0 and PE_ % STAGED == 0

    def raw_index(key):
        return (N0 + expert_at[key[2:]], key[1] * PE_) if key[0] == "exp" else (raw_at[key], 0)

    def staged_index(key):
        return (M0 + expert_at[key[2:]], key[1] * PE_) if key[0] == "exp" else (staged_at[key], 0)

    ctx = ExitStack()
    with ctx:
        def sb(name, shape, dt=F32):
            return ctx.enter_context(nc.sbuf_tensor(name, shape, dt))

        def sem(name):
            return ctx.enter_context(nc.semaphore(name))

        raw = sb("raw", [P, RAW, PIECE])
        w_hi = sb("w_hi", [P, STAGED, PIECE], F32R)
        w_lo = sb("w_lo", [P, STAGED, PIECE], F32R)
        hT_hi = sb("hT_hi", [P, KC, T], F32R)
        hT_lo = sb("hT_lo", [P, KC, T], F32R)
        actT_hi = sb("actT_hi", [P, TPC, T], F32R)
        actT_lo = sb("actT_lo", [P, TPC, T], F32R)
        x_sb = sb("x_sb", [P, NT, D])
        row = sb("row", [P, 2, D])
        ada_acc = sb("ada_acc", [P, 2, HALF])
        ada_seed = sb("ada_seed", [P, 2, HALF])
        ident = sb("ident", [P, P])
        tri = sb("tri", [P, P])
        ones = sb("ones", [P, P])
        vec = sb("vec", [P, 2, P])
        mod = sb("mod", [P, DEPTH, 4, KC])
        modt = sb("modt", [P, 4])
        w_f = sb("w_f", [P, KC, H])
        w_r = sb("w_r", [P, KC, E])
        b_f = sb("b_f", [P, H])
        c_act = sb("c_act", [P, KC])
        NR = 7
        ss = sb("ss", [P, DEPTH * NR, NT])
        ms = sb("ms", [P, DEPTH * NR, NT])
        rstd = sb("rstd", [P, DEPTH * NR, NT])
        neg_half = sb("neg_half", [P, NT])
        ssum = sb("ssum", [P, NT])
        nmean = sb("nmean", [P, NT])
        fz = sb("fz", [P, 4, NT * H])
        logf = sb("logf", [P, NT, H])
        Lq = sb("Lq", [P, NT, H])
        nmax = sb("nmax", [P, NT, H])
        psums = sb("psums", [P, NT, H])
        rsums = sb("rsums", [P, NT, H])
        lg = sb("lg", [P, NT, E])
        lmax = sb("lmax", [P, NT])
        rank = sb("rank", [P, NT, E])
        sel = sb("sel", [P, NT, E])
        gate = sb("gate", [P, NT, E + 1])
        gden = sb("gden", [P, NT])
        posm = sb("posm", [P, NT, E + 1])
        wide = sb("wide", [1, E], I32)
        KIB = 256
        scratch = sb("scratch", [P, 58 * KIB])

        def at(kib, size_kib):
            return scratch[:, int(kib * KIB):int((kib + size_kib) * KIB)]

        qz = at(0, 8).rearrange("p (h t) -> p h t", h=H)
        kT = at(8, 4).rearrange("p (m t) -> p m t", m=AC)
        PT = at(0, 12).rearrange("p (b t) -> p b t", t=P)
        v_sb = at(12, 4).rearrange("p (i n) -> p i n", i=NT)
        u_sb = at(16, 4).rearrange("p (i n) -> p i n", i=NT)
        s_sb = at(20, 4).rearrange("p (i n) -> p i n", i=NT)
        S0 = at(24, 4).rearrange("p (h k) -> p h k", h=H)
        S1 = at(28, 8).rearrange("p (h k) -> p h k", h=H)
        xn = at(28, 8).rearrange("p (i d) -> p i d", i=NT)
        attn = at(36, 4).rearrange("p (i n) -> p i n", i=NT)
        wsp_raw = at(36, 4).rearrange("p (g s) -> p g s", g=G)
        sgu = at(40, 4).rearrange("p (i n) -> p i n", i=NT)
        wT = at(44, 4).rearrange("p (g t) -> p g t", g=G)
        neg_pick = at(48, 4).rearrange("p (h q) -> p h q", h=H)
        g_v_sb = at(52, 2)
        LT = at(54, 1)
        tmp = at(20, 8).rearrange("p (i d) -> p i d", i=NT)
        junk = at(56, 2).bitcast(BF16)
        hT = at(16, 8).rearrange("p (k t) -> p k t", k=KC)
        vec_raw = at(20, 1).rearrange("p (a b) -> p a b", a=2)
        sil = at(8, 4).rearrange("p (b n) -> p b n", b=NT)
        act_t = at(12, 4).rearrange("p (b n) -> p b n", b=NT)
        htok = at(0, 8).rearrange("p (i d) -> p i d", i=NT)
        ye = at(24, 8).rearrange("p (b d) -> p b d", b=NT)
        yacc = at(32, 8).rearrange("p (i d) -> p i d", i=NT)
        pick = at(46, 2).rearrange("p (i s) -> p i s", i=NT)
        pickg = at(48, 2).rearrange("p (i s) -> p i s", i=NT)
        pickgT = at(50, 2).rearrange("p (b t) -> p b t", b=NT)
        iota = at(52, 1)
        tri_strict = at(53, 0.5)
        before = at(53.5, 0.25).rearrange("p (a b) -> p a b", a=E)
        cmp1 = at(54, 0.5).rearrange("p (i a b) -> p i a b", i=NT, a=E)
        cmp2 = at(54.5, 0.5).rearrange("p (i a b) -> p i a b", i=NT, a=E)
        tmp_e = at(16, 8).rearrange("p (i d) -> p i d", i=NT)

        ps = ctx.enter_context(nc.psum_tensor("ps", [P, 8, 512], F32))

        def bank(b, n=1):
            return ps[:, b:b + n, :].rearrange("p b n -> p (b n)")

        landed = [sem(f"landed{i}") for i in range(RAW)]
        raw_used = sem("raw_used")
        hi_ready = sem("hi_ready")
        used = sem("used")
        hTf_act = sem("hTf_act")
        hTf_dve = sem("hTf_dve")
        hT_hi_ready = sem("hT_hi_ready")
        hT_lo_ready = sem("hT_lo_ready")
        T_ps = sem("T_ps")
        actT_hi_ready = sem("actT_hi_ready")
        actT_lo_ready = sem("actT_lo_ready")
        f_ps = sem("f_ps")
        k_ready = sem("k_ready")
        pickg_ready = sem("pickg_ready")
        pickgT_ps = sem("pickgT_ps")
        pickgT_ready = sem("pickgT_ready")
        x_landed = sem("x_landed")
        c_landed = sem("c_landed")
        vec_landed = sem("vec_landed")
        small_landed = sem("small_landed")
        router_landed = sem("router_landed")
        row_landed = [sem(f"row_landed{i}") for i in range(2)]
        seed_landed = [sem(f"seed_landed{i}") for i in range(2)]
        wsp_landed = sem("wsp_landed")
        g_v_landed = sem("g_v_landed")
        out_stored = sem("out_stored")
        consts = sem("consts")
        seed_zero = sem("seed_zero")
        zeros = sem("zeros")
        vecT = sem("vecT")
        vec_ready = sem("vec_ready")
        c_ready = sem("c_ready")
        ada_out = sem("ada_out")
        ada_done = sem("ada_done")
        dve_seq = sem("dve_seq")
        act_seq = sem("act_seq")
        pool_seq = sem("pool_seq")
        ss_ready = sem("ss_ready")
        ms_ready = sem("ms_ready")
        rstd_ready = sem("rstd_ready")
        xn_ready = sem("xn_ready")
        xT_ready = sem("xT_ready")
        x_new = sem("x_new")
        wsp_masked = sem("wsp_masked")
        wT_ps = sem("wT_ps")
        wT_ready = sem("wT_ready")
        qk_ready = sem("qk_ready")
        z_ready = sem("z_ready")
        lnz_ready = sem("lnz_ready")
        logf_ready = sem("logf_ready")
        v_ready = sem("v_ready")
        L_ps = sem("L_ps")
        L_ready = sem("L_ready")
        score_ps = sem("score_ps")
        score_sb = sem("score_sb")
        masked = sem("masked")
        max_ready = sem("max_ready")
        exp_ready = sem("exp_ready")
        PT_ps = sem("PT_ps")
        PT_act = sem("PT_act")
        PT_dve = sem("PT_dve")
        gelu_ready = sem("gelu_ready")
        mean_ready = sem("mean_ready")
        s_ready = sem("s_ready")
        pv_ps = sem("pv_ps")
        attn_raw = sem("attn_raw")
        attn_ready = sem("attn_ready")
        mix_ps = sem("mix_ps")
        sgu_raw = sem("sgu_raw")
        sgu_ready = sem("sgu_ready")
        mT_ps = sem("mT_ps")
        y_ps = sem("y_ps")
        y_row = sem("y_row")
        sil_ready = sem("sil_ready")
        act_ready = sem("act_ready")
        htok_ps = sem("htok_ps")
        htok_act = sem("htok_act")
        htok_dve = sem("htok_dve")
        logit_ps = sem("logit_ps")
        lmax_ready = sem("lmax_ready")
        gexp_ready = sem("gexp_ready")
        sel_ready = sem("sel_ready")
        pos_ps = sem("pos_ps")
        route_ready = sem("route_ready")
        moe_consts = sem("moe_consts")
        pick_ready = sem("pick_ready")
        gath_ps = sem("gath_ps")
        second_ps = sem("second_ps")
        second_hi = sem("second_hi")
        second_lo = sem("second_lo")
        ye_act = sem("ye_act")
        ye_dve = sem("ye_dve")
        scat_ps = sem("scat_ps")
        yacc_done = sem("yacc_done")

        NORM_MIX, SV, ATTN, SGU, POST_MIX, NORM_FFN, POST_FFN = range(NR)

        rows0, r0 = {}, 0
        for name, ap, n in (("c", c, KC), ("g_pre_mix", g_pre_mix, DEPTH * KC), ("g_pre_ffn", g_pre_ffn, DEPTH * KC),
                            ("g_out_attn", g_out_attn, DEPTH * AC), ("g_out_sgu", g_out_sgu, DEPTH * AC)):
            rows0[name] = (ap.rearrange("l (k p) -> (l k) p", p=P), r0, n)
            r0 += n
        rows0["b_spatial"] = (b_spatial.rearrange("l g t -> (l g) t"), r0, DEPTH * G)
        R0 = r0 + DEPTH * G
        NB = DEPTH * 6 * KC
        assert R0 <= P and NB <= P

        def col(name, layer, k, n=1):
            at0 = rows0[name][1] + layer * (rows0[name][2] // DEPTH) + k
            return vec[:, 0, at0:at0 + n]

        def b_ada_col(layer, kind, k, n):
            at0 = (layer * 6 + kind) * KC + k
            return vec[:, 1, at0:at0 + n]

        def raw3(slot, w=HALF):
            return raw[:, slot, :].rearrange("p (k n) -> p k n", n=HALF)[:, :, 0:w]

        def shaped(t, slot, key):
            if key[-3] == "down":
                return t[:, slot, :].rearrange("p (k n) -> p k n", n=D)
            w = P * dense_tiles(key[2]) if key[0] == "ffn" else HALF
            return t[:, slot, :].rearrange("p (k n) -> p k n", n=HALF)[:, :, 0:w]

        def arrived(eng, key):
            n, part = raw_index(key)
            eng.wait_ge(landed[n % RAW], 16 * (n // RAW + 1) + part * 16 // RAW if key[0] != "exp" else 16 * (n // RAW + 1) + key[1] * (16 * PE_ // RAW))
            return n % RAW

        def write_hi(act, key):
            slot = arrived(act, key)
            m, part = staged_index(key)
            if m >= STAGED:
                act.wait_ge(used, m - STAGED + 1 + part)
            act.activation(shaped(w_hi, m % STAGED, key), shaped(raw, slot, key), ACT.Copy).then_inc(hi_ready, 1)

        def write_lo(dve, key):
            n, _ = raw_index(key)
            m, part = staged_index(key)
            dve.wait_ge(hi_ready, m + 1 + part)
            nc.vector.tensor_tensor(shaped(w_lo, m % STAGED, key), shaped(raw, n % RAW, key),
                                    shaped(w_hi, m % STAGED, key).bitcast(F32), ALU.subtract).then_inc(raw_used, 1)

        def staged(pe, key):
            n, part = raw_index(key)
            pe.wait_ge(raw_used, n + 1 + part)
            m, _ = staged_index(key)
            return shaped(w_hi, m % STAGED, key), shaped(w_lo, m % STAGED, key)

        def products_done(eng, key):
            m, part = staged_index(key)
            eng.wait_ge(used, m + 1 + part)

        def slots(t, b, block):
            return t[:, 4 * b:4 * b + 4, block * P:(block + 1) * P]

        def act_column(B, s):
            return (s % 2) * P if B == 1 else 0

        ACT_BANKS = (0, 2)
        DVE_BANKS = (1, 3)

        def ada_bank(n):
            key = ada_order[n]
            for beside in mixer_ada:
                for name, chunk in beside.items():
                    if key == chunk:
                        return {"q": 2, "k": 1, "v": 0, "u": 1}[name]
            if key in dense_ada:
                return 4 + n % 2 if key in dense_ada[:2] else 2 * (n % 2)
            return (4 if n < MIX_DONE else 2) + n % 2

        block = ctx.enter_context(nc.Block())

        @block.sync
        def _(sp):
            in_col = {"q": 0, "k": AW, "v": 2 * AW, "u": 3 * AW + H, "s": 4 * AW + H}

            def source(key):
                kind, layer = key[:2]
                h = key[-1]
                rows = slice(h * D // 2, (h + 1) * D // 2)
                if kind == "ada":
                    a = key[2] * D + key[3] * HALF
                    return w_ada[layer, rows, a:a + HALF]
                if kind == "in":
                    a = in_col[key[2]]
                    return w_in[layer, rows, a:a + HALF]
                if kind == "out":
                    return w_out[layer, rows, key[2] * HALF:(key[2] + 1) * HALF]
                kind, s = key[1:3]
                a = s * HALF
                if kind == "down":
                    return w_down_dense[0, a + h * 2 * P:a + (h + 1) * 2 * P, :]
                w = P * dense_tiles(s)
                a += FD if kind == "up" else 0
                return w_gate_up_dense[0, rows, a:a + w]

            sp.dma_start(vec_raw[0:KC, 0, :], rows0["c"][0]).then_inc(c_landed, 16)
            for n, key in enumerate(stream):
                if n == 1:
                    for name, (src, r, rows) in rows0.items():
                        if name != "c":
                            sp.dma_start(vec_raw[r:r + rows, 0, :], src).then_inc(vec_landed, 16)
                    sp.dma_start(vec_raw[0:NB, 1, :], b_ada.rearrange("l (k p) -> (l k) p", p=P)).then_inc(vec_landed, 16)
                if n == 4:
                    sp.dma_start(x_sb[:, :, :], x[0].rearrange("(i p) d -> p i d", p=P)).then_inc(x_landed, 16)
                if n >= RAW:
                    sp.wait_ge(raw_used, n - RAW + 1)
                dst = raw3(n % RAW) if key[0] == "ada" else shaped(raw, n % RAW, key)
                sp.dma_start(dst, source(key).rearrange("(k p) n -> p k n", p=P)).then_inc(landed[n % RAW], 16)
            with sp.Fori(0, E) as e:
                for j, (kind, s, h) in enumerate(expert_order):
                    n = N0 + j
                    sp.wait_ge(raw_used, n - RAW + 1 + e * PE_)
                    if kind == "down":
                        a = s * HALF + h * 2 * P
                        src = w_down_exp[0, bass.ds(e, 1), a:a + 2 * P, :]
                    else:
                        a = s * HALF + (FE if kind == "up" else 0)
                        src = w_gate_up_exp[0, bass.ds(e, 1), h * D // 2:(h + 1) * D // 2, a:a + HALF]
                    sp.dma_start(shaped(raw, n % RAW, ("exp", e, kind, s, h)),
                                 src.rearrange("a (k p) n -> p (a k) n", p=P)).then_inc(landed[n % RAW], 16)

            for i in range(NT):
                sp.wait_ge(x_new, NT * 3 + i + 1)
                sp.dma_start(out[0, i * P:(i + 1) * P, :], x_sb[:, i, :]).then_inc(out_stored, 16)
            sp.wait_ge(out_stored, 16 * NT)

        @block.scalar
        def _(act):

            def load_forget(layer):
                act.dma_start(w_f[:, :, :], w_in[layer, :, 3 * AW:3 * AW + H].rearrange("(k p) e -> p k e", p=P)).then_inc(small_landed, 16)
                act.dma_start(b_f[:, :], b_forget[layer:layer + 1, :].to_broadcast([P, H])).then_inc(small_landed, 16)

            def load_row(which, layer):
                src = (g_post_mix, g_post_ffn)[which]
                act.dma_start(row[:, which, :], src[layer:layer + 1, :].to_broadcast([P, D])).then_inc(row_landed[which], 16)

            def load_seed(n):
                _, layer, kind, half = gate_order[n]
                a = kind * D + half * HALF
                act.dma_start(ada_seed[0:1, n % 2, :], b_ada[layer:layer + 1, a:a + HALF]).then_inc(seed_landed[n % 2], 16)

            def load_spatial(layer):
                act.dma_start(wsp_raw, w_spatial[layer].rearrange("g t s -> t g s")).then_inc(wsp_landed, 16)
                act.dma_start(g_v_sb, g_v[layer:layer + 1, :].to_broadcast([P, AW])).then_inc(g_v_landed, 16)

            act.wait_ge(vec_ready, 1)
            act.activation(c_act[:, :], vec[:, 0, 0:KC], ACT.Silu).then_inc(c_ready, 1)

            def squares(src_of):
                def one(i, request):
                    src, bias = src_of(i)
                    kw = {} if bias is None else {"bias": bias}
                    if 2 * request + i:
                        act.wait_ge(ss_ready, 2 * request + i)
                    act.activation(junk[:, 0:src.shape[1]], src, ACT.Square, accum_out=ss[:, request, i:i + 1], **kw).then_inc(ss_ready, 1)
                return one

            done = [0]

            def advance(key):
                while done[0] <= staged_at[key]:
                    write_hi(act, staged_keys[done[0]])
                    done[0] += 1

            def input_squares(n, layer, ffn):
                sq = squares(lambda i: (x_sb[:, i, :], None))
                for i in range(NT):
                    if n == 0:
                        act.wait_ge(x_landed, 16)
                    else:
                        act.wait_ge(x_new, NT * (n - 1) + i + 1)
                    sq(i, layer * NR + (NORM_FFN if ffn else NORM_MIX))

            def input_parts(n, scale_bias, ps_ready, first=0, split=True):
                for b in range(4):
                    if b in ACT_BANKS:
                        act.wait_ge(ps_ready[0], ps_ready[1] + b + 1)
                        for kc in (2 * b, 2 * b + 1):
                            scale, bias = scale_bias(kc)
                            a = act.activation(hT[:, kc, :], bank(first + b)[:, (kc % 2) * T:(kc % 2 + 1) * T],
                                               ACT.Identity if bias is not None else ACT.Copy, scale=scale, **({} if bias is None else {"bias": bias}))
                        a.then_inc(hTf_act, 1)
                    if not split:
                        continue
                    if b in ACT_BANKS:
                        act.wait_ge(hTf_act, 2 * n + b // 2 + 1)
                    else:
                        act.wait_ge(hTf_dve, 2 * n + b // 2 + 1)
                    act.activation(hT_hi[:, 2 * b:2 * b + 2, :], hT[:, 2 * b:2 * b + 2, :], ACT.Copy).then_inc(hT_hi_ready, 1)

            def post_squares(n, request, key):
                for i in range(NT):
                    if i == 0:
                        act.wait_ge(y_ps, n + 1)
                    else:
                        products_done(act, key)
                    squares(lambda i: (bank(4 + 2 * i, 2), None))(i, request)

            def modulation(layer, ffn):
                return lambda kc: (mod[:, layer, 2 * ffn + 1, kc:kc + 1], mod[:, layer, 2 * ffn, kc:kc + 1])

            def branch_gain(layer):
                return lambda kc: (col("g_out_attn", layer, kc) if kc < AC else col("g_out_sgu", layer, kc - AC), None)

            def silu(step, B, w, key):
                products_done(act, key)
                act.wait_ge(act_ready, step)
                for b in range(B):
                    a = act.activation(sil[:, b, 0:w], bank(2 * b)[:, 0:w], ACT.Silu)
                a.then_inc(sil_ready, 1)

            def act_hi(step, B, w, tbank, c0=0):
                act.wait_ge(T_ps, step + 1)
                for b in range(B):
                    a = act.activation(actT_hi[:, 0:w // P, c0 + b * P:c0 + (b + 1) * P], bank(tbank(b))[:, 0:w].rearrange("p (t n) -> p t n", n=P), ACT.Copy)
                a.then_inc(actT_hi_ready, 1)

            for layer in range(DEPTH):
                L = layer
                input_squares(2 * L, L, 0)
                if L == 1:
                    act.wait_ge(x_new, NT * 2)
                    load_row(1, 1)
                    act.wait_ge(ada_done, gate_done(5))
                    load_seed(6)
                    load_seed(7)
                advance(("in", L, "q", 1))
                if L == 0:
                    act.wait_ge(seed_zero, 1)
                    load_seed(0)
                    load_seed(1)
                    act.wait_ge(raw_used, 2 * MIX_DONE - 1)
                    load_spatial(0)
                    load_forget(0)
                act.wait_ge(ada_done, DENSE_DONE if L else MIX_DONE)
                input_parts(3 * L, modulation(L, 0), (xT_ready, 8 * L))
                advance(("in", L, "k", 0))
                if L == 0:
                    load_row(0, 0)
                    load_row(1, 0)
                    act.dma_start(w_r[:, :, :], w_router[0].rearrange("(k p) e -> p k e", p=P)).then_inc(router_landed, 16)
                act.wait_ge(zeros, L + 1)
                products_done(act, ("in", L, "q", 1))
                for m in range(2):
                    src = bank(4 + m).rearrange("p (a t) -> p a t", a=2)
                    for r in range(2):
                        a = act.activation(qz[64 * r:64 * r + 64, 4 * m + r:4 * m + r + 3:2, :], src[64 * r:64 * r + 64], ACT.Copy, scale=QSCALE)
                a.then_inc(qk_ready, 1)
                advance(("in", L, "v", 1))
                products_done(act, ("in", L, "k", 1))
                act.activation(kT, bank(6, 2).rearrange("p (a t) -> p a t", a=AC), ACT.Copy).then_inc(k_ready, 1)
                act.wait_ge(z_ready, L + 1)
                act.activation(fz[:, 3, :], fz[:, 1, :], ACT.Exp).then_inc(act_seq, 1)
                act.wait_ge(act_seq, L + 1)
                act.activation(fz[:, 3, :], fz[:, 3, :], ACT.Ln, bias=1.0).then_inc(lnz_ready, 1)
                advance(("in", L, "s", 1))
                for qb, S in enumerate((S0, S1)):
                    act.wait_ge(max_ready, 2 * L + qb + 1)
                    for h in range(H):
                        a = act.activation(S[:, h, :], S[:, h, :], ACT.Exp, bias=nmax[:, qb, h:h + 1], accum_out=psums[:, qb, h:h + 1])
                    a.then_inc(exp_ready, 1)
                products_done(act, ("in", L, "u", 1))
                for i in range(NT):
                    act.activation(u_sb[:, i, :], bank(6 + i), ACT.Gelu_apprx_tanh).then_inc(gelu_ready, 1)
                products_done(act, ("in", L, "s", 1))
                for i in range(NT):
                    act.activation(s_sb[:, i, :], bank(4 + i), ACT.Gelu_apprx_tanh, accum_out=ssum[:, i:i + 1]).then_inc(gelu_ready, 1)
                for n in range(0, 6, 2):
                    act.wait_ge(PT_ps, 6 * L + n + 1)
                    b = (0, 1, 2, 3, 6, 7)[n]
                    act.activation(PT[:, 4 * n:4 * n + 4, :], bank(b).rearrange("p (a t) -> p a t", t=P), ACT.Copy).then_inc(PT_act, 1)
                act.wait_ge(mean_ready, L + 1)
                sq = squares(lambda i: (s_sb[:, i, :], nmean[:, i:i + 1]))
                for i in range(NT):
                    sq(i, L * NR + SV)
                advance(("out", L, 0, 0))
                sq = squares(lambda i: (attn[:, i, :], None))
                for i in range(NT):
                    act.wait_ge(attn_raw, 2 * L + i + 1)
                    sq(i, L * NR + ATTN)
                sq = squares(lambda i: (sgu[:, i, :], None))
                for i in range(NT):
                    act.wait_ge(sgu_raw, 2 * L + i + 1)
                    sq(i, L * NR + SGU)
                input_parts(3 * L + 1, branch_gain(L), (mT_ps, 4 * L))
                advance(("out", L, 1, 1))
                if L == 0:
                    load_forget(1)
                    load_spatial(1)
                    advance(("ffn", "gate", 0, 1))
                post_squares(2 * L, L * NR + POST_MIX, ("out", L, 1, 1))
                if L == 0:
                    advance(("ffn", "up", 0, 0))
                input_squares(2 * L + 1, L, 1)
                act.wait_ge(ada_done, len(ada_order) if L else FFN_DONE)
                input_parts(3 * L + 2, modulation(L, 1), (xT_ready, 8 * L + 4), 4, split=L == 0)
                if L == 0:
                    load_row(0, 1)
                    load_seed(2)
                    load_seed(3)
                    order = ffn_order(SD, lambda s: dense_tiles(s) // 2)
                    for j, (kind, s, h) in enumerate(order):
                        advance(("ffn", kind, s, h))
                        for kind, s, h in ((order[j - STAGED + 1],) if j >= STAGED - 1 else ()) if j < len(order) - 1 else order[j - STAGED + 1:]:
                            w = P * dense_tiles(s)
                            if kind == "up" and h == 1:
                                silu(s, NT, w, ("ffn", "up", s, 1))
                                if s == 0:
                                    act_hi(s, NT, w, lambda b: 2 * b + 1)
                            if kind == "down" and h == dense_tiles(s) // 2 - 1 and s < SD - 1:
                                act_hi(s + 1, NT, P * dense_tiles(s + 1), lambda b: 2 * b + 1)
                                if s == 0:
                                    act.wait_ge(ada_done, gate_done(3))
                                    load_seed(4)
                                    load_seed(5)
                    advance(("in", 1, "q", 1))
                    post_squares(1, POST_FFN, ("ffn", "down", SD - 1, 0))

            for key in expert_order[:AHEAD]:
                write_hi(act, ("exp", 0) + key)
            act.wait_ge(htok_ps, 1)
            act.activation(htok[:, 0, :], bank(0, 2), ACT.Copy).then_inc(htok_act, 1)
            act.wait_ge(lmax_ready, 1)
            for i in range(NT):
                a = act.activation(gate[:, i, 0:E], lg[:, i, :], ACT.Exp, bias=lmax[:, i:i + 1])
            a.then_inc(gexp_ready, 1)

            def gathered(e, first):
                act.wait_ge(gath_ps, e + 1)
                for b in range(2):
                    act.activation(slots(hT_hi, b, 0), bank(first + b).rearrange("p (k t) -> p k t", t=P), ACT.Copy).then_inc(hT_hi_ready, 1)

            def expert(e, B, last):
                order, step0 = expert_order, SD + e * SE
                if B == 2:
                    act.wait_ge(second_ps, e + 1)
                    for b in range(2):
                        a = act.activation(slots(hT_hi, b, 1), bank(2 + b).rearrange("p (k t) -> p k t", t=P), ACT.Copy)
                    a.then_inc(second_hi, 1)
                else:
                    act.nop().then_inc(second_hi, 1)
                for j, (kind, s, h) in enumerate(order):
                    if j >= AHEAD:
                        write_hi(act, ("exp", e, kind, s, h))
                    for kind, s, h in ((order[j - STAGED + 1],) if j >= STAGED - 1 else ()) if j < PE_ - 1 else order[j - STAGED + 1:]:
                        if kind == "up" and h == 1:
                            silu(step0 + s, B, HALF, ("exp", e, "up", s, 1))
                            if s == 0 and B == 2:
                                act_hi(step0 + s, B, HALF, lambda b: 2 * b + 1)
                            if s == SE - 1 and B == 1:
                                gathered(e + 1, 6)
                        if B == 1 and kind == "gate" and s == 1 and h == 1:
                            act_hi(step0, B, HALF, lambda b: 2)
                        if kind == "down" and s < SE - 1 and h == B - 1:
                            act_hi(step0 + s + 1, B, HALF, (lambda b: 2) if B == 1 else (lambda b: 2 * b + 1), act_column(B, s + 1))
                if not last:
                    write_hi(act, ("exp", e + 1) + order[0])
                products_done(act, ("exp", e, "down", SE - 1, 1))
                for b in range(B):
                    a = act.activation(ye[:, b, 0:HALF], bank(4 + 2 * b), ACT.Copy)
                a.then_inc(ye_act, 1)
                if B == 2:
                    gathered(e + 1, 0)
                if not last:
                    for key in order[1:AHEAD]:
                        write_hi(act, ("exp", e + 1) + key)

            def routed(e, last):
                size = act.value_load(wide[0:1, bass.ds(e, 1)], min_val=0, max_val=1)
                with act.If(size == 0):
                    expert(e, 1, last)
                with act.Else():
                    expert(e, 2, last)

            gathered(0, 6)
            act.wait_ge(route_ready, 1)
            with act.Fori(0, E - 1) as e:
                routed(e, False)
            routed(E - 1, True)
            for i in range(NT):
                act.wait_ge(yacc_done, NT * E + i + 1)
                squares(lambda i: (yacc[:, i, :], None))(i, NR + POST_FFN)

        @block.gpsimd
        def _(pool):
            links = [0]

            def link(ins):
                links[0] += 1
                ins.then_inc(pool_seq, 1)
                pool.wait_ge(pool_seq, links[0])

            nc.gpsimd.memset(ident[:, :], 0.0)
            nc.gpsimd.memset(ones[:, :], 1.0)
            nc.gpsimd.memset(neg_half[:, :], -0.5)
            link(nc.gpsimd.memset(ada_seed[:, :, :], 0.0))
            nc.gpsimd.nop().then_inc(seed_zero, 1)
            nc.gpsimd.affine_select(out=ident[:, :], in_=ident[:, :], compare_op=ALU.not_equal, fill=1.0, base=0,
                                    pattern=[[-1, P]], channel_multiplier=1)
            nc.gpsimd.affine_select(out=tri[:, :], in_=ones[:, :], compare_op=ALU.is_ge, fill=0.0, base=0,
                                    pattern=[[1, P]], channel_multiplier=-1)
            nc.gpsimd.memset(LT, 0.0)
            link(nc.gpsimd.memset(neg_pick, 0.0))
            nc.gpsimd.affine_select(out=neg_pick, in_=neg_pick, compare_op=ALU.not_equal, fill=-1.0, base=0,
                                    pattern=[[-1, H], [0, P]], channel_multiplier=1).then_inc(consts, 1)

            def inverse(request, by_tile=False):
                for i, tiles in enumerate((slice(0, 1), slice(1, 2)) if by_tile else (slice(0, NT),)):
                    n = 1 if by_tile else NT
                    pool.wait_ge(ms_ready, NT * request + i + n)
                    nc.gpsimd.tensor_tensor(rstd[:, request, tiles], ms[:, request, tiles], neg_half[:, tiles], ALU.pow).then_inc(rstd_ready, n)

            for L in range(DEPTH):
                inverse(L * NR + NORM_MIX, True)
                if L:
                    pool.wait_ge(pv_ps, 2 * L)
                nc.gpsimd.memset(qz, 0.0).then_inc(zeros, 1)
                pool.wait_ge(wsp_landed, 16 * (L + 1))
                nc.gpsimd.affine_select(out=wsp_raw, in_=wsp_raw, compare_op=ALU.is_ge, fill=0.0, base=0,
                                        pattern=[[0, G], [-1, P]], channel_multiplier=1).then_inc(wsp_masked, 1)
                for qb, S in enumerate((S0, S1)):
                    pool.wait_ge(score_sb, 2 * L + qb + 1)
                    d = S[:, :, qb * P:(qb + 1) * P]
                    nc.gpsimd.affine_select(out=d, in_=d, compare_op=ALU.is_ge, fill=MASKED, base=0,
                                            pattern=[[0, H], [-1, P]], channel_multiplier=1).then_inc(masked, 1)
                for request in (SV, ATTN, SGU, POST_MIX, NORM_FFN):
                    inverse(L * NR + request, request in (POST_MIX, NORM_FFN))
                if L == 0:
                    inverse(POST_FFN, True)
            nc.gpsimd.iota(iota, pattern=[[1, T]], base=0, channel_multiplier=0, allow_small_or_imprecise_dtypes=True)
            nc.gpsimd.affine_select(out=tri_strict, in_=ones[:, :], compare_op=ALU.is_gt, fill=0.0, base=0,
                                    pattern=[[1, P]], channel_multiplier=-1)
            nc.gpsimd.affine_select(out=before, in_=ones[:, 0:E * E].rearrange("p (a b) -> p a b", a=E), compare_op=ALU.is_gt,
                                    fill=0.0, base=0, pattern=[[1, E], [-1, E]], channel_multiplier=0).then_inc(moe_consts, 1)
            inverse(NR + POST_FFN, True)

        @block.vector
        def _(dve):
            links = [0]

            def link(ins):
                links[0] += 1
                ins.then_inc(dve_seq, 1)
                dve.wait_ge(dve_seq, links[0])

            V = nc.vector
            dve.wait_ge(vecT, 1)
            V.tensor_copy(vec[:, 0, 0:KC], bank(0)[:, 0:KC]).then_inc(vec_ready, 1)

            def ada_sum(key):
                n = ada_order.index(key[:4])
                h = key[4]
                if n == 0 and h == 0:
                    dve.wait_ge(c_ready, 1)
                if n >= 2 and h == 0:
                    dve.wait_ge(ada_out, n - 1)
                acc = ada_acc[:, n % 2, :]
                w = raw3(arrived(dve, key))
                for k in range(KC // 2):
                    kc = h * KC // 2 + k
                    if kc == 0 and key[:4] in gate_order:
                        m = gate_order.index(key[:4])
                        dve.wait_ge(seed_landed[m % 2], 16 * (m // 2 + 1))
                        ins = V.scalar_tensor_tensor(acc, w[:, k, :], c_act[:, 0:1], ada_seed[:, m % 2, :], ALU.mult, ALU.add)
                    elif kc == 0:
                        ins = V.tensor_scalar(acc, w[:, k, :], c_act[:, 0:1], None, ALU.mult)
                    else:
                        ins = V.scalar_tensor_tensor(acc, w[:, k, :], c_act[:, kc:kc + 1], acc, ALU.mult, ALU.add)
                    if k < KC // 2 - 1:
                        link(ins)
                ins.then_inc(raw_used, 1)
                dve.wait_ge(raw_used, raw_at[key] + 1)

            done = [0]
            finished = [0]

            def finish(n):
                while finished[0] < n:
                    ada_finish(finished[0])
                    finished[0] += 1

            def advance(*key):
                while done[0] <= raw_at[key]:
                    k = stream[done[0]]
                    if k[0] == "ada":
                        n = ada_order.index(k[:4])
                        if k[4] == 0:
                            finish(n if k[:4] in dense_ada and n % 2 == 0 else n - 1)
                        ada_sum(k)
                    else:
                        write_lo(dve, k)
                    done[0] += 1

            def ada_finish(n):
                _, layer, kind, half = ada_order[n]
                dve.wait_ge(ada_out, n + 1)
                name = KINDS[kind]
                ffn = int(name.endswith("ffn"))
                ks = half * 4
                src = bank(ada_bank(n))
                if name.startswith("gate"):
                    dve.wait_ge(row_landed[ffn], 16 * (layer + 1))
                    r = row[:, ffn, half * HALF:(half + 1) * HALF]
                    V.scalar_tensor_tensor(r, src, 1.0, r, ALU.add, ALU.mult).then_inc(ada_done, 1)
                elif name.startswith("shift"):
                    V.tensor_tensor(mod[:, layer, 2 * ffn, ks:ks + 4], src[:, 0:4], b_ada_col(layer, kind, ks, 4), ALU.add).then_inc(ada_done, 1)
                else:
                    dve.wait_ge(ada_done, n)
                    link(V.tensor_tensor(modt[:, :], src[:, 0:4], b_ada_col(layer, kind, ks, 4), ALU.add))
                    V.scalar_tensor_tensor(mod[:, layer, 2 * ffn + 1, ks:ks + 4], modt[:, :], 1.0,
                                           col("g_pre_ffn" if ffn else "g_pre_mix", layer, ks, 4), ALU.add, ALU.mult).then_inc(ada_done, 1)

            def mean_square(request, width, i=None):
                n, tiles = (NT, slice(0, NT)) if i is None else (1, slice(i, i + 1))
                dve.wait_ge(ss_ready, NT * request + (i or 0) + n)
                V.tensor_scalar(ms[:, request, tiles], ss[:, request, tiles], 1.0 / width, EPS, ALU.mult, ALU.add).then_inc(ms_ready, n)

            def scaled_tile(request, i):
                dve.wait_ge(rstd_ready, NT * request + i + 1)
                V.tensor_scalar(xn[:, i, :], x_sb[:, i, :], rstd[:, request, i:i + 1], None, ALU.mult).then_inc(xn_ready, 1)

            def input_parts(n, scale_bias, ps_ready, first=0, split=True):
                for b in range(4):
                    if b in ACT_BANKS:
                        dve.wait_ge(ps_ready[0], ps_ready[1] + b + 2)
                        for kc in (2 * b + 2, 2 * b + 3):
                            scale, bias = scale_bias(kc)
                            l = V.tensor_scalar(hT[:, kc, :], bank(first + b + 1)[:, (kc % 2) * T:(kc % 2 + 1) * T], scale, bias, ALU.mult,
                                                *(() if bias is None else (ALU.add,)))
                        l.then_inc(hTf_dve, 1)
                    if not split:
                        continue
                    dve.wait_ge(hT_hi_ready, 4 * n + b + 1)
                    V.tensor_tensor(hT_lo[:, 2 * b:2 * b + 2, :], hT[:, 2 * b:2 * b + 2, :], hT_hi[:, 2 * b:2 * b + 2, :].bitcast(F32),
                                    ALU.subtract).then_inc(hT_lo_ready, 1)

            def modulation(layer, ffn):
                return lambda kc: (mod[:, layer, 2 * ffn + 1, kc:kc + 1], mod[:, layer, 2 * ffn, kc:kc + 1])

            def branch_gain(layer):
                return lambda kc: (col("g_out_attn", layer, kc) if kc < AC else col("g_out_sgu", layer, kc - AC), None)

            def gated(step, B, w):
                dve.wait_ge(sil_ready, step + 1)
                for b in range(B):
                    l = V.tensor_tensor(act_t[:, b, 0:w], sil[:, b, 0:w], bank(2 * b + 1)[:, 0:w], ALU.mult)
                l.then_inc(act_ready, 1)

            def act_lo(step, B, w, tbank, c0=0):
                dve.wait_ge(actT_hi_ready, step + 1)
                for b in range(B):
                    l = V.tensor_tensor(actT_lo[:, 0:w // P, c0 + b * P:c0 + (b + 1) * P], bank(tbank(b))[:, 0:w].rearrange("p (t n) -> p t n", n=P),
                                        actT_hi[:, 0:w // P, c0 + b * P:c0 + (b + 1) * P].bitcast(F32), ALU.subtract)
                l.then_inc(actT_lo_ready, 1)

            def post(request, which, ys, tmp_, n, norm=True):
                dve.wait_ge(ada_done, finished[0])
                for i in range(NT):
                    mean_square(request, D, i)
                    V.tensor_tensor(tmp_[:, i, :], ys[i], row[:, which, :], ALU.mult).then_inc(y_row, 1)
                    if i and norm:
                        mean_square(request + 1, D, 0)
                    dve.wait_ge(rstd_ready, NT * request + i + 1)
                    dve.wait_ge(y_row, NT * n + i + 1)
                    V.scalar_tensor_tensor(x_sb[:, i, :], tmp_[:, i, :], rstd[:, request, i:i + 1], x_sb[:, i, :], ALU.mult, ALU.add).then_inc(x_new, 1)
                if norm:
                    scaled_tile(request + 1, 0)
                    mean_square(request + 1, D, 1)
                    scaled_tile(request + 1, 1)

            for L in range(DEPTH):
                if L == 0:
                    advance(*ada(0, "shift_mix")[0], 1)
                    dve.wait_ge(vecT, 2)
                    V.tensor_copy(vec[:, 0, KC:R0], bank(1)[:, KC:R0])
                    V.tensor_copy(vec[:, 1, 0:NB], bank(1)[:, P:P + NB]).then_inc(vec_ready, 1)
                    advance(*ada(0, "scale_mix")[0], 0)
                if L == 0:
                    for i in range(NT):
                        mean_square(NORM_MIX, D, i)
                        scaled_tile(NORM_MIX, i)
                if L == 0:
                    advance(*ada(0, "scale_mix")[1], 1)
                    advance("in", 0, "q", 0)
                    finish(MIX_DONE)
                dve.wait_ge(ada_done, DENSE_DONE if L else MIX_DONE)
                input_parts(3 * L, modulation(L, 0), (xT_ready, 8 * L))
                advance("in", L, "k", 0)
                for n in range(2):
                    dve.wait_ge(wT_ps, 2 * L + n + 1)
                    V.tensor_copy(wT[:, 4 * n:4 * n + 4, :], bank(6 + n).rearrange("p (a t) -> p a t", t=P)).then_inc(wT_ready, 1)
                advance("in", L, "v", 0)
                mixer_chunks = [ada_order.index(k) for k in mixer_ada[L].values()]
                finish(mixer_chunks[0] + 1)
                dve.wait_ge(f_ps, L + 1)
                dve.wait_ge(small_landed, 16 * (2 + 2 * L))
                link(V.tensor_tensor(fz[:, 0, :].rearrange("p (i h) -> p i h", i=NT), bank(0)[:, 0:NT * H].rearrange("p (i h) -> p i h", i=NT),
                                     b_f[:, :].unsqueeze(1).to_broadcast([P, NT, H]), ALU.add))
                V.tensor_scalar(fz[:, 2, :], fz[:, 0, :], 0.0, None, ALU.min)
                V.scalar_tensor_tensor(fz[:, 1, :], fz[:, 0, :], -1.0, fz[:, 0, :], ALU.mult, ALU.min).then_inc(z_ready, 1)
                finish(mixer_chunks[1] + 1)
                advance("in", L, "v", 1)
                dve.wait_ge(lnz_ready, L + 1)
                V.tensor_tensor(logf[:, :, :].rearrange("p i h -> p (i h)"), fz[:, 2, :], fz[:, 3, :], ALU.subtract).then_inc(logf_ready, 1)
                dve.wait_ge(L_ps, L + 1)
                dve.wait_ge(consts, 1)
                V.tensor_copy(LT[0:H, :], bank(1)[0:H, 0:T])
                V.tensor_copy(Lq[:, :, :].rearrange("p i h -> p (i h)"), bank(1)[:, T:T + NT * H]).then_inc(L_ready, 1)
                products_done(dve, ("in", L, "v", 1))
                for i in range(NT):
                    V.tensor_copy(v_sb[:, i, :], bank(2 + i)).then_inc(v_ready, 1)
                advance("in", L, "u", 0)
                advance("in", L, "u", 1)
                dve.wait_ge(L_ready, L + 1)
                dve.wait_ge(score_ps, 2 * L + 1)
                V.tensor_tensor(S0, bank(4, 2).rearrange("p (h k) -> p h k", h=H), Lq[:, 0, :].unsqueeze(2).to_broadcast([P, H, P]), ALU.add).then_inc(score_sb, 1)
                advance("in", L, "s", 0)
                dve.wait_ge(score_ps, 2 * L + 2)
                V.tensor_tensor(S1, bank(0, 4).rearrange("p (h k) -> p h k", h=H), Lq[:, 1, :].unsqueeze(2).to_broadcast([P, H, T]), ALU.add).then_inc(score_sb, 1)
                for qb, S in enumerate((S0, S1)):
                    if qb == 1:
                        advance("in", L, "s", 1)
                    dve.wait_ge(masked, 2 * L + qb + 1)
                    V.tensor_reduce(nmax[:, qb, :], S, AX_X, ALU.max, negate=True).then_inc(max_ready, 1)
                if L == 0:
                    advance(*out_ada[0], 1)
                finish(mixer_chunks[-1] + 1)
                dve.wait_ge(exp_ready, 2 * L + 2)
                link(V.reciprocal(rsums[:, :, :], psums[:, :, :]))
                for n in range(1, 6, 2):
                    dve.wait_ge(PT_ps, 6 * L + n + 1)
                    b = (0, 1, 2, 3, 6, 7)[n]
                    V.tensor_copy(PT[:, 4 * n:4 * n + 4, :], bank(b).rearrange("p (a t) -> p a t", t=P)).then_inc(PT_dve, 1)
                dve.wait_ge(gelu_ready, 4 * L + 4)
                V.tensor_scalar(nmean[:, :], ssum[:, :], -1.0 / AW, None, ALU.mult).then_inc(mean_ready, 1)
                mean_square(L * NR + SV, AW)
                dve.wait_ge(rstd_ready, NT * (L * NR + SV + 1))
                dve.wait_ge(g_v_landed, 16 * (L + 1))
                for i in range(NT):
                    link(V.tensor_scalar(s_sb[:, i, :], s_sb[:, i, :], nmean[:, i:i + 1], rstd[:, L * NR + SV, i:i + 1], ALU.add, ALU.mult))
                    V.tensor_tensor(s_sb[:, i, :], s_sb[:, i, :], g_v_sb, ALU.mult).then_inc(s_ready, 1)
                for i in range(NT):
                    dve.wait_ge(pv_ps, 2 * L + i + 1)
                    V.tensor_tensor(attn[:, i, :].rearrange("p (h d) -> p h d", h=H), bank(4 + i).rearrange("p (h d) -> p h d", h=H),
                                    rsums[:, i, :].unsqueeze(2).to_broadcast([P, H, DH]), ALU.mult).then_inc(attn_raw, 1)
                dve.wait_ge(mix_ps, L + 1)
                for i in range(NT):
                    link(V.tensor_tensor(sgu[:, i, :].rearrange("p (b g d) -> p b g d", b=2, g=G // 2),
                                         ps[:, 6:8, :].rearrange("p b (g i d) -> p b g i d", g=G // 2, i=NT)[:, :, :, i],
                                         col("b_spatial", L, 0, G).rearrange("p (b g) -> p b g", b=2).unsqueeze(3).to_broadcast([P, 2, G // 2, DH]), ALU.add))
                    V.tensor_tensor(sgu[:, i, :], sgu[:, i, :], u_sb[:, i, :], ALU.mult).then_inc(sgu_raw, 1)
                    if i == 0:
                        mean_square(L * NR + ATTN, AW)
                dve.wait_ge(rstd_ready, NT * (L * NR + ATTN + 1))
                for i in range(NT):
                    V.tensor_scalar(attn[:, i, :], attn[:, i, :], rstd[:, L * NR + ATTN, i:i + 1], None, ALU.mult).then_inc(attn_ready, 1)
                mean_square(L * NR + SGU, AW)
                dve.wait_ge(rstd_ready, NT * (L * NR + SGU + 1))
                for i in range(NT):
                    V.tensor_scalar(sgu[:, i, :], sgu[:, i, :], rstd[:, L * NR + SGU, i:i + 1], None, ALU.mult).then_inc(sgu_ready, 1)
                advance("out", L, 0, 0)
                input_parts(3 * L + 1, branch_gain(L), (mT_ps, 4 * L))
                advance("out", L, 1, 1)
                if L == 0:
                    finish(FFN_DONE)
                    advance("ffn", "gate", 0, 1)
                post(L * NR + POST_MIX, 0, [bank(4 + 2 * i, 2) for i in range(NT)], tmp, 2 * L)
                if L == 1:
                    dve.wait_ge(ada_done, len(ada_order))
                input_parts(3 * L + 2, modulation(L, 1), (xT_ready, 8 * L + 4), 4, split=L == 0)
                if L == 0:
                    order = ffn_order(SD, lambda s: dense_tiles(s) // 2)
                    for j, (kind, s, h) in enumerate(order):
                        advance("ffn", kind, s, h)
                        for kind, s, h in ((order[j - STAGED + 1],) if j >= STAGED - 1 else ()) if j < len(order) - 1 else order[j - STAGED + 1:]:
                            w = P * dense_tiles(s)
                            if kind == "up" and h == 1:
                                gated(s, NT, w)
                                if s == 0:
                                    act_lo(s, NT, w, lambda b: 2 * b + 1)
                            if kind == "down" and h == 0 and s < SD - 2:
                                finish(FFN_DONE + 2 * (s + 2))
                            if kind == "down" and h == dense_tiles(s) // 2 - 1 and s < SD - 1:
                                act_lo(s + 1, NT, P * dense_tiles(s + 1), lambda b: 2 * b + 1)
                    finish(DENSE_DONE)
                    advance("in", 1, "q", 1)
                    post(POST_FFN, 1, [bank(4 + 2 * i, 2) for i in range(NT)], tmp, 1)

            write_lo(dve, ("exp", 0) + expert_order[0])
            dve.wait_ge(logit_ps, 1)
            link(V.tensor_copy(lg[:, :, :].rearrange("p i e -> p (i e)"), bank(4)[:, 0:NT * E]))
            V.tensor_reduce(lmax[:, :], lg[:, :, :], AX_X, ALU.max, negate=True).then_inc(lmax_ready, 1)
            other = lg[:, :, :].unsqueeze(2).to_broadcast([P, NT, E, E])
            own = lg[:, :, :].unsqueeze(3).to_broadcast([P, NT, E, E])
            V.tensor_tensor(cmp1, other, own, ALU.is_gt)
            link(V.tensor_tensor(cmp2, other, own, ALU.is_equal))
            dve.wait_ge(moe_consts, 1)
            for i in range(NT):
                l = V.tensor_tensor(cmp2[:, i], cmp2[:, i], before, ALU.mult)
            link(l)
            link(V.tensor_tensor(cmp1, cmp1, cmp2, ALU.add))
            link(V.tensor_reduce(rank[:, :, :], cmp1, AX_X, ALU.add))
            V.tensor_scalar(sel[:, :, :], rank[:, :, :], 2.0, None, ALU.is_lt).then_inc(sel_ready, 1)
            dve.wait_ge(htok_ps, 2)
            V.tensor_copy(htok[:, 1, :], bank(2, 2)).then_inc(htok_dve, 1)
            dve.wait_ge(sel_ready, 1)
            dve.wait_ge(gexp_ready, 1)
            link(V.tensor_tensor(gate[:, :, 0:E], gate[:, :, 0:E], sel[:, :, :], ALU.mult))
            link(V.tensor_reduce(gden[:, :], gate[:, :, 0:E], AX_X, ALU.add))
            link(V.reciprocal(gden[:, :], gden[:, :]))
            for i in range(NT):
                V.tensor_scalar(gate[:, i, 0:E], gate[:, i, 0:E], gden[:, i:i + 1], None, ALU.mult)
            dve.wait_ge(pos_ps, 1)
            V.memset(posm[:, :, E:E + 1], -1.0)
            V.memset(gate[:, :, E:E + 1], 0.0)
            link(V.scalar_tensor_tensor(posm[:, :, 0:E], bank(4)[:, 0:NT * E].rearrange("p (i e) -> p i e", i=NT), 1.0, sel[:, :, :], ALU.add, ALU.mult))
            V.tensor_scalar(posm[:, :, 0:E], posm[:, :, 0:E], -1.0, None, ALU.add)
            V.tensor_scalar(wide[:, :], bank(4)[0:1, NT * E:NT * E + E], float(P), None, ALU.is_gt).then_inc(route_ready, 1)

            def pick_slots(dst, e, gated_, ready):
                for i in range(NT):
                    if gated_:
                        l = V.tensor_scalar(dst[:, i, :], iota, posm[:, i, bass.ds(e, 1)], gate[:, i, bass.ds(e, 1)], ALU.is_equal, ALU.mult)
                    else:
                        l = V.tensor_scalar(dst[:, i, :], iota, posm[:, i, bass.ds(e, 1)], None, ALU.is_equal)
                l.then_inc(ready, 1)

            def gathered_lo(e, first):
                for b in range(2):
                    dve.wait_ge(hT_hi_ready, GATHERED + 2 * e + b + 1)
                    V.tensor_tensor(slots(hT_lo, b, 0), bank(first + b).rearrange("p (k t) -> p k t", t=P),
                                    slots(hT_hi, b, 0).bitcast(F32), ALU.subtract).then_inc(hT_lo_ready, 1)

            def expert(e, B, last):
                order, step0 = expert_order, SD + e * SE
                if B == 2:
                    dve.wait_ge(second_hi, e + 1)
                    for b in range(2):
                        l = V.tensor_tensor(slots(hT_lo, b, 1), bank(2 + b).rearrange("p (k t) -> p k t", t=P),
                                            slots(hT_hi, b, 1).bitcast(F32), ALU.subtract)
                    l.then_inc(second_lo, 1)
                else:
                    V.nop().then_inc(second_lo, 1)
                for j, (kind, s, h) in enumerate(order):
                    if j >= AHEAD:
                        write_lo(dve, ("exp", e, kind, s, h))
                    if j == 3:
                        pick_slots(pickg, e, True, pickg_ready)
                    if j == 6:
                        dve.wait_ge(pickgT_ps, e + 1)
                        V.tensor_copy(pickgT, bank(7).rearrange("p (b t) -> p b t", b=NT)).then_inc(pickgT_ready, 1)
                        pick_slots(pick, e + 1, False, pick_ready)
                    for kind, s, h in ((order[j - STAGED + 1],) if j >= STAGED - 1 else ()) if j < PE_ - 1 else order[j - STAGED + 1:]:
                        if kind == "up" and h == 1:
                            gated(step0 + s, B, HALF)
                            if s == 0 and B == 2:
                                act_lo(step0 + s, B, HALF, lambda b: 2 * b + 1)
                            if s == SE - 1 and B == 1:
                                gathered_lo(e + 1, 6)
                        if B == 1 and kind == "gate" and s == 1 and h == 1:
                            act_lo(step0, B, HALF, lambda b: 2)
                        if kind == "down" and s < SE - 1 and h == B - 1:
                            act_lo(step0 + s + 1, B, HALF, (lambda b: 2) if B == 1 else (lambda b: 2 * b + 1), act_column(B, s + 1))
                if not last:
                    write_lo(dve, ("exp", e + 1) + order[0])
                products_done(dve, ("exp", e, "down", SE - 1, 1))
                for b in range(B):
                    l = V.tensor_copy(ye[:, b, HALF:D], bank(5 + 2 * b))
                l.then_inc(ye_dve, 1)
                if B == 2:
                    gathered_lo(e + 1, 0)
                if not last:
                    for key in order[1:AHEAD]:
                        write_lo(dve, ("exp", e + 1) + key)
                for i in range(NT):
                    dve.wait_ge(scat_ps, e * NT + i + 1)
                    dve.wait_ge(yacc_done, e * NT + i + 1)
                    V.tensor_tensor(yacc[:, i, :], yacc[:, i, :], bank((6, 4)[i], 2), ALU.add).then_inc(yacc_done, 1)

            def routed(e, last):
                size = dve.value_load(wide[0:1, bass.ds(e, 1)], min_val=0, max_val=1)
                with dve.If(size == 0):
                    expert(e, 1, last)
                with dve.Else():
                    expert(e, 2, last)

            dve.wait_ge(route_ready, 1)
            pick_slots(pick, 0, False, pick_ready)
            for key in expert_order[1:AHEAD]:
                write_lo(dve, ("exp", 0) + key)
            gathered_lo(0, 6)
            for i in range(NT):
                V.memset(yacc[:, i, :], 0.0).then_inc(yacc_done, 1)
            with dve.Fori(0, E - 1) as e:
                routed(e, False)
            routed(E - 1, True)
            dve.wait_ge(yacc_done, NT * (E + 1))
            post(NR + POST_FFN, 1, [yacc[:, i, :] for i in range(NT)], tmp_e, 3, norm=False)

        @block.tensor
        def _(pe):
            mm = nc.tensor.matmul

            pe.wait_ge(consts, 1)
            pe.wait_ge(c_landed, 16)
            nc.tensor.transpose(bank(0)[:, 0:KC], vec_raw[0:KC, 0, :], ident[0:KC, 0:KC]).then_inc(vecT, 1)
            pe.wait_ge(vec_landed, 16 * len(rows0))
            for a, n in enumerate((R0, NB)):
                l = nc.tensor.transpose(bank(1)[:, a * P:a * P + n], vec_raw[0:n, a, :], ident[0:n, 0:n])
            l.then_inc(vecT, 1)
            nada = [0]

            def ada_reduce():
                n = nada[0]
                nada[0] += 1
                pe.wait_ge(raw_used, raw_at[ada_order[n] + (1,)] + 1)
                if n >= 2:
                    pe.wait_ge(ada_done, n - 1)
                acc = ada_acc[:, n % 2, :]
                dst = bank(ada_bank(n))
                if ada_order[n] in gate_order:
                    mm(dst, ones[:, :], acc, start=True, stop=True).then_inc(ada_out, 1)
                else:
                    for j in range(4):
                        l = mm(dst[:, j:j + 1], acc[:, j * P:(j + 1) * P], ones[:, 0:1], start=True, stop=True)
                    l.then_inc(ada_out, 1)

            def input_transposed(n, first):
                for i in range(NT):
                    pe.wait_ge(xn_ready, NT * n + i + 1)
                    for kc in range(KC):
                        l = nc.tensor.transpose(bank(first + kc // 2)[:, (kc % 2) * T + i * P:(kc % 2) * T + (i + 1) * P],
                                                xn[:, i, kc * P:(kc + 1) * P], ident[:, :])
                        if i == NT - 1 and kc % 2:
                            l.then_inc(xT_ready, 1)

            def input_ready(n, b=3):
                pe.wait_ge(hT_lo_ready, 4 * n + b + 1)

            def product(dst, stationary, moving, first, last, start=None):
                s_hi, s_lo = stationary
                m_hi, m_lo = moving
                start = first if start is None else start
                mm(dst, s_hi, m_hi, start=start, stop=False, skip_group_check=True)
                mm(dst, s_hi, m_lo, start=False, stop=False, skip_group_check=True)
                return mm(dst, s_lo, m_hi, start=False, stop=last, skip_group_check=True)

            def tokens(k, i):
                return hT_hi[:, k, i * P:(i + 1) * P], hT_lo[:, k, i * P:(i + 1) * P]

            def moving_weights(key, dst_of, B, ready=None):
                h = key[-1]
                hi, lo = staged(pe, key)
                last = key[0] == "out" and key[2:] == (1, 1)
                order = [(k, b) for k in range(KC // 2) for b in range(B)]
                for k, b in sorted(order, key=lambda kb: kb[1]) if last else order:
                    kc = h * KC // 2 + k
                    if ready is not None and k % 2 == 0 and b == 0:
                        pe.wait_ge(hT_lo_ready, ready(kc))
                    l = product(dst_of(b), tokens(kc, b), (hi[:, k, :], lo[:, k, :]), kc == 0, kc == KC - 1)
                    if last and (k, b) == (KC // 2 - 1, 0):
                        l.then_inc(y_ps, 1)
                l.then_inc(used, 1)

            def ffn_piece(key, B, s_first, s_last, ready=None, w=HALF):
                kind, s, h = key[-3:]
                if kind == "down":
                    hi, lo = staged(pe, key)
                    c0 = act_column(B, s)
                    for b in range(B):
                        for t in range(2):
                            tt = 2 * h + t
                            for half in range(2):
                                cols = slice(half * HALF, (half + 1) * HALF)
                                l = product(bank(4 + 2 * b + half), (actT_hi[:, tt, c0 + b * P:c0 + (b + 1) * P], actT_lo[:, tt, c0 + b * P:c0 + (b + 1) * P]),
                                            (hi[:, t, cols], lo[:, t, cols]), s_first and tt == 0, s_last(tt))
                        if key[:3] == ("ffn", "down", SD - 1) and b == 0:
                            l.then_inc(y_ps, 1)
                    l.then_inc(used, 1)
                else:
                    u = int(kind == "up")
                    moving_weights(key, lambda b: bank(2 * b + u)[:, 0:w], B, ready)

            def act_transposed(step, B, tiles, tbank):
                pe.wait_ge(act_ready, step + 1)
                for b in range(B):
                    for t in range(tiles):
                        l = nc.tensor.transpose(bank(tbank(b))[:, t * P:(t + 1) * P], act_t[:, b, t * P:(t + 1) * P], ident[:, :])
                l.then_inc(T_ps, 1)

            for L in range(DEPTH):
                if L:
                    pe.wait_ge(x_new, NT * 2)
                    pe.wait_ge(ada_done, nada[0])
                if L == 0:
                    for _ in range(2):
                        ada_reduce()
                    pe.wait_ge(vec_ready, 2)
                input_transposed(2 * L, 0)
                if L == 0:
                    for _ in range(2):
                        ada_reduce()
                for j, name in enumerate("qk"):
                    for h in range(2):
                        hi, lo = staged(pe, ("in", L, name, h))
                        for k in range(KC // 2):
                            kc = h * KC // 2 + k
                            if j == 0 and k % 2 == 0:
                                input_ready(3 * L, kc // 2)
                            if j == 1 and kc == 0:
                                pe.wait_ge(wT_ready, 2 * L + 2)
                                pe.wait_ge(small_landed, 16 * (2 + 2 * L))
                            if j == 1:
                                for i in range(NT):
                                    l = mm(bank(0)[:, i * H:(i + 1) * H], hT[:, kc, i * P:(i + 1) * P], w_f[:, kc, :],
                                           start=(kc == 0 and i == 0), stop=(kc == KC - 1), skip_group_check=True)
                                if kc == KC - 1:
                                    l.then_inc(f_ps, 1)
                            for m in range(AC):
                                cols = slice(m * P, (m + 1) * P)
                                l = product(bank(4 + 2 * j + m // 2)[:, (m % 2) * T:(m % 2 + 1) * T], (hi[:, k, cols], lo[:, k, cols]),
                                            (hT_hi[:, kc, :], hT_lo[:, kc, :]), kc == 0, kc == KC - 1, start=(kc == 0 and m % 2 == 0))
                        l.then_inc(used, 1)
                        if j == 0 and h == 0:
                            pe.wait_ge(wsp_masked, L + 1)
                            for g in range(G):
                                l = nc.tensor.transpose(bank(6 + g // 4)[:, (g % 4) * P:(g % 4 + 1) * P], wsp_raw[:, g, :], ident[:, :])
                                if g % 4 == 3:
                                    l.then_inc(wT_ps, 1)
                        if j == 1:
                            ada_reduce()

                def project(name, first, *halves):
                    for h in halves or range(2):
                        moving_weights(("in", L, name, h), lambda b: bank(first + b), NT)

                pe.wait_ge(ada_done, nada[0] - 1)
                project("v", 2)
                pe.wait_ge(logf_ready, L + 1)
                pe.wait_ge(ada_done, nada[0])
                dst = bank(1)[0:H, 0:P]
                mm(dst, logf[:, 0, :], tri[:, :], start=True, stop=True)
                dst = bank(1)[0:H, P:T]
                mm(dst, logf[:, 0, :], ones[:, :], start=True, stop=False)
                mm(dst, logf[:, 1, :], tri[:, :], start=False, stop=True)
                mm(bank(1)[:, T:T + H], tri[:, :], logf[:, 0, :], start=True, stop=True)
                mm(bank(1)[:, T + H:T + 2 * H], ones[:, :], logf[:, 0, :], start=True, stop=False)
                mm(bank(1)[:, T + H:T + 2 * H], tri[:, :], logf[:, 1, :], start=False, stop=True).then_inc(L_ps, 1)
                pe.wait_ge(qk_ready, L + 1)
                pe.wait_ge(k_ready, L + 1)
                pe.wait_ge(L_ready, L + 1)
                for qb in range(NT):
                    nk = (qb + 1) * P
                    if qb:
                        pe.wait_ge(v_ready, 2 * (L + 1))
                    for h in range(H):
                        dst = bank(4, 2)[:, h * P:(h + 1) * P] if qb == 0 else bank(0, 4)[:, h * T:(h + 1) * T]
                        mm(dst, qz[:, h, qb * P:(qb + 1) * P], kT[:, h // 2, 0:nk], start=True, stop=False)
                        l = mm(dst, neg_pick[:, h, :], LT[:, 0:nk], start=False, stop=True)
                    l.then_inc(score_ps, 1)
                project("u", 6)
                pe.wait_ge(score_sb, 2 * L + 1)
                project("s", 4, 0)
                pe.wait_ge(score_sb, 2 * L + 2)
                for _ in range(2):
                    ada_reduce()
                project("s", 4, 1)
                pe.wait_ge(ada_done, nada[0])
                pe.wait_ge(exp_ready, 2 * L + 2)
                for b in range(24):
                    n = b // 4
                    if b == 16:
                        pe.wait_ge(gelu_ready, 4 * L + 2)
                    src = S1[:, b // 2, (b % 2) * P:(b % 2 + 1) * P] if b < 16 else S0[:, b - 16, :]
                    l = nc.tensor.transpose(bank((0, 1, 2, 3, 6, 7)[n])[:, (b % 4) * P:(b % 4 + 1) * P], src, ident[:, :])
                    if b % 4 == 3:
                        l.then_inc(PT_ps, 1)
                pe.wait_ge(gelu_ready, 4 * L + 4)
                pe.wait_ge(PT_act, 3 * (L + 1))
                pe.wait_ge(PT_dve, 3 * (L + 1))
                for qb in range(NT):
                    for h in range(H):
                        dst = bank(4 + qb)[:, h * DH:(h + 1) * DH]
                        for kb in range(qb + 1):
                            l = mm(dst, PT[:, 2 * h + kb if qb else 16 + h, :], v_sb[:, kb, h * DH:(h + 1) * DH], start=(kb == 0), stop=(kb == qb))
                    l.then_inc(pv_ps, 1)
                pe.wait_ge(s_ready, 2 * L + NT)
                for g in range(G):
                    dst = bank(6 + 2 * g // G)[:, (g % (G // 2)) * NT * DH:(g % (G // 2) + 1) * NT * DH]
                    l = mm(dst.rearrange("p (i d) -> p i d", i=NT), wT[:, g, :], s_sb[:, :, g * DH:(g + 1) * DH], start=True, stop=True)
                l.then_inc(mix_ps, 1)
                for branch, (src, ready) in enumerate(((attn, attn_ready), (sgu, sgu_ready))):
                    pe.wait_ge(ready, 2 * (L + 1))
                    for kc in range(AC):
                        for i in range(NT):
                            l = nc.tensor.transpose(bank(2 * branch + kc // 2)[:, (kc % 2) * T + i * P:(kc % 2) * T + (i + 1) * P],
                                                    src[:, i, kc * P:(kc + 1) * P], ident[:, :])
                        if kc % 2:
                            l.then_inc(mT_ps, 1)
                for half in range(2):
                    for h in range(2):
                        moving_weights(("out", L, half, h), lambda b: bank(4 + 2 * b + half), NT, (lambda kc: 4 * (3 * L + 1) + kc // 2 + 1) if half == 0 else None)
                        if L == 0 and half != h:
                            ada_reduce()
                if L == 0:
                    pe.wait_ge(ada_done, nada[0])
                input_transposed(2 * L + 1, 4)
                if L == 0:
                    pe.wait_ge(x_new, NT)
                    for kind, s, h in ffn_order(SD, lambda s: dense_tiles(s) // 2):
                        tiles = dense_tiles(s)
                        if kind == "down" and h == 0:
                            pe.wait_ge(actT_lo_ready, s + 1)
                            if s == 0:
                                pe.wait_ge(ada_done, nada[0])
                        if s and kind == "gate" and h == 0:
                            pe.wait_ge(sil_ready, s)
                            pe.wait_ge(ada_done, nada[0])
                        if s and kind == "up" and h == 0:
                            pe.wait_ge(actT_lo_ready, s)
                            pe.wait_ge(ada_done, nada[0])
                        ffn_piece(("ffn", kind, s, h), NT, s == 0, lambda tt: s == SD - 1 and tt == tiles - 1,
                                  ready=(lambda kc: 4 * 2 + kc // 2 + 1) if (kind, s) == ("gate", 0) else None, w=tiles * P)
                        if s == 0 and kind == "up":
                            if h == 1:
                                act_transposed(0, NT, tiles, lambda b: 2 * b + 1)
                            ada_reduce()
                        if kind == "down" and h == tiles // 2 - 1 and s < SD - 1:
                            act_transposed(s + 1, NT, dense_tiles(s + 1), lambda b: 2 * b + 1)
                        if kind == "down" and h == 0 and s < SD - 2:
                            pe.wait_ge(sil_ready, s + 2)
                            for _ in range(2):
                                ada_reduce()

            pe.wait_ge(hTf_act, 12)
            pe.wait_ge(hTf_dve, 12)
            pe.wait_ge(router_landed, 16)
            for i in range(NT):
                for k in range(KC):
                    l = mm(bank(4)[:, i * E:(i + 1) * E], hT[:, k, i * P:(i + 1) * P], w_r[:, k, :], start=(k == 0), stop=(k == KC - 1))
            l.then_inc(logit_ps, 1)
            for i in range(NT):
                for k in range(KC):
                    l = nc.tensor.transpose(bank(2 * i, 2)[:, k * P:(k + 1) * P], hT[:, k, i * P:(i + 1) * P], ident[:, :])
                l.then_inc(htok_ps, 1)
            pe.wait_ge(sel_ready, 1)
            pe.wait_ge(moe_consts, 1)
            mm(bank(4)[:, 0:E], tri_strict, sel[:, 0, :], start=True, stop=True)
            mm(bank(4)[:, E:2 * E], ones[:, :], sel[:, 0, :], start=True, stop=False)
            mm(bank(4)[:, E:2 * E], tri_strict, sel[:, 1, :], start=False, stop=True)
            mm(bank(4)[:, 2 * E:3 * E], ones[:, :], sel[:, 0, :], start=True, stop=False)
            mm(bank(4)[:, 2 * E:3 * E], ones[:, :], sel[:, 1, :], start=False, stop=True).then_inc(pos_ps, 1)
            pe.wait_ge(route_ready, 1)
            pe.wait_ge(htok_act, 1)
            pe.wait_ge(htok_dve, 1)

            def gather(block, first):
                for k in range(KC):
                    for i in range(NT):
                        l = mm(bank(first + k // 4)[:, (k % 4) * P:(k % 4 + 1) * P], htok[:, i, k * P:(k + 1) * P],
                               pick[:, i, block * P:(block + 1) * P], start=(i == 0), stop=(i == NT - 1))
                return l

            def expert(e, B):
                step0 = SD + e * SE
                tbank = (lambda b: 2) if B == 1 else (lambda b: 2 * b + 1)
                if B == 2:
                    pe.wait_ge(actT_lo_ready, step0)
                    gather(1, 2).then_inc(second_ps, 1)
                    pe.wait_ge(second_lo, e + 1)
                else:
                    nc.tensor.nop().then_inc(second_ps, 1)
                for kind, s, h in expert_order:
                    if kind == "down" and h == 0:
                        pe.wait_ge(actT_lo_ready, step0 + s + 1)
                        if s == 0:
                            pe.wait_ge(pickgT_ready, e + 1)
                    if kind == "gate" and s and h == 0:
                        pe.wait_ge(sil_ready, step0 + s)
                    if kind == "up" and s and h == 0:
                        pe.wait_ge(act_ready, step0 + s)
                        if B == 2:
                            pe.wait_ge(actT_lo_ready, step0 + s)
                    ffn_piece(("exp", e, kind, s, h), B, s == 0, lambda tt: s == SE - 1 and tt == TPC - 1,
                              ready=(lambda kc: GATHERED + 2 * e + kc // 4 + 1) if kind == "gate" and s == 0 else None)
                    if B == 1 and s == SE - 1 and kind == "up" and h == 1:
                        pe.wait_ge(pick_ready, e + 2)
                        gather(0, 6).then_inc(gath_ps, 1)
                    if s == 0 and h == 1 and kind == ("gate" if B == 2 else "up"):
                        pe.wait_ge(pickg_ready, e + 1)
                        pe.wait_ge(yacc_done, (e + 1) * NT)
                        for b in range(NT):
                            for i in range(NT):
                                l = nc.tensor.transpose(bank(7)[:, b * T + i * P:b * T + (i + 1) * P], pickg[:, i, b * P:(b + 1) * P], ident[:, :])
                        l.then_inc(pickgT_ps, 1)
                    if (B == 2 and s == 0 and kind == "up" and h == 1) or (B == 1 and s == 1 and kind == "gate" and h == 1):
                        act_transposed(step0, B, TPC, tbank)
                    if kind == "down" and s < SE - 1 and h == B - 1:
                        act_transposed(step0 + s + 1, B, TPC, tbank)
                if B == 2:
                    pe.wait_ge(pick_ready, e + 2)
                    gather(0, 0).then_inc(gath_ps, 1)
                pe.wait_ge(ye_act, e + 1)
                pe.wait_ge(ye_dve, e + 1)
                pe.wait_ge(pickgT_ready, e + 1)
                for i in range(NT):
                    for half in range(2):
                        for b in range(B):
                            l = mm(bank((6, 4)[i] + half), pickgT[:, b, i * P:(i + 1) * P], ye[:, b, half * HALF:(half + 1) * HALF],
                                   start=(b == 0), stop=(b == B - 1))
                    l.then_inc(scat_ps, 1)

            pe.wait_ge(pick_ready, 1)
            gather(0, 6).then_inc(gath_ps, 1)
            with pe.Fori(0, E) as e:
                size = pe.value_load(wide[0:1, bass.ds(e, 1)], min_val=0, max_val=1)
                with pe.If(size == 0):
                    expert(e, 1)
                with pe.Else():
                    expert(e, 2)


_INS = ["x", "c", "w_ada", "b_ada", "g_pre_mix", "g_post_mix", "g_pre_ffn", "g_post_ffn", "w_in", "b_forget", "g_v",
        "w_spatial", "b_spatial", "g_out_attn", "g_out_sgu", "w_out", "w_gate_up_dense", "w_down_dense", "w_router",
        "w_gate_up_exp", "w_down_exp"]


def kernel(**inputs):
    import numpy as _np
    import concourse.bacc as _bacc
    from concourse import mybir as _mybir
    from concourse.bass_utils import run_bass_kernel_spmd as _run

    nc = _bacc.Bacc("TRN2", target_bir_lowering=False, num_devices=1)
    arrays, args = {}, []
    for name in _INS:
        a = _np.ascontiguousarray(inputs[name])
        arrays[f"in_{name}_dram"] = a
        args.append(nc.dram_tensor(f"in_{name}_dram", a.shape, _mybir.dt.from_np(a.dtype), kind="ExternalInput").ap())
    o = nc.dram_tensor("out_0_dram", inputs["x"].shape, _mybir.dt.float32, kind="ExternalOutput").ap()
    hybrid_fox_sgu_moe(nc, *args, o)
    r = _run(nc, [arrays], core_ids=[0])
    return r.results[0]["out_0_dram"]
```
